# Optimizing a Trainium2 kernel written in Bass

```python
import jax, jax.numpy as jnp
from jax import lax
import numpy as np
import math

D_MODEL = 1024
BATCH = 1
SEQ = 256
DEPTH = 2

CHUNK = 64
MEM_LEN = 256
HEAD_GROUP = 64
A_WIDTH = 384
B_WIDTH = 320
C_WIDTH = 320
MIX_WIDTH = A_WIDTH + B_WIDTH + C_WIDTH
N_MIX_GROUPS = MIX_WIDTH // HEAD_GROUP
C_GROUPS = C_WIDTH // HEAD_GROUP
A_KERNEL = 31
B_KERNEL = 3
GMLP_BLOCK = 128
PROJ_WIDTH = 2 * A_WIDTH + 3 * B_WIDTH + 2 * C_WIDTH
X_HEADS = 4
X_HEAD_DIM = D_MODEL // X_HEADS
D_FF = 2816
N_EXPERTS = 8
TOP_K = 2
D_EXPERT = 3584
N_DENSE = (DEPTH + 1) // 2
N_MOE = DEPTH // 2
EPS = 1e-6


def rmsnorm(x, g):
    xf = x.astype(jnp.float32)
    y = xf * lax.rsqrt(jnp.mean(xf * xf, axis=-1, keepdims=True) + EPS)
    return (y * g.astype(jnp.float32)).astype(x.dtype)

def layernorm(x, g, b):
    xf = x.astype(jnp.float32)
    mu = jnp.mean(xf, axis=-1, keepdims=True)
    xc = xf - mu
    var = jnp.mean(xc * xc, axis=-1, keepdims=True)
    y = xc * lax.rsqrt(var + EPS) * g.astype(jnp.float32) + b.astype(jnp.float32)
    return y.astype(x.dtype)

def causal_depthwise_conv(x, w):
    k, c = w.shape
    return lax.conv_general_dilated(
        x, w[:, None, :], window_strides=(1,), padding=[(k - 1, 0)],
        dimension_numbers=("NWC", "WIO", "NWC"), feature_group_count=c)

def chunk_spatial_gate(u, v, ws, bias):
    bsz, s, c = v.shape
    n_blocks = s // GMLP_BLOCK
    chunk_id = jnp.arange(GMLP_BLOCK) // CHUNK
    mask = chunk_id[:, None] >= chunk_id[None, :]
    ws = jnp.where(mask[None], ws, jnp.zeros((), ws.dtype))
    vb = v.reshape(bsz, n_blocks, GMLP_BLOCK, C_GROUPS, HEAD_GROUP)
    mixed = jnp.einsum("gij,bnjgc->bnigc", ws, vb) + bias.T[None, None, :, :, None]
    return u * mixed.reshape(bsz, s, c)

def hybrid_mixer(xn, w_in, conv_a_w, conv_a_b, ln_a_g, ln_a_b, conv_b_w,
                 ln_c_g, ln_c_b, gmlp_ws, gmlp_b, mix_out_g, w_mix_out):
    z = xn @ w_in
    splits = [A_WIDTH, 2 * A_WIDTH, 2 * A_WIDTH + B_WIDTH,
              2 * A_WIDTH + 2 * B_WIDTH, 2 * A_WIDTH + 3 * B_WIDTH]
    a_val, a_gate, b_gate, c_gate, b_in, c_z = jnp.split(z, splits, axis=-1)
    ya = a_val * jax.nn.sigmoid(a_gate)
    ya = causal_depthwise_conv(ya, conv_a_w) + conv_a_b
    ya = jax.nn.silu(layernorm(ya, ln_a_g, ln_a_b))
    yb = b_gate * causal_depthwise_conv(c_gate * b_in, conv_b_w)
    c_z = jax.nn.gelu(c_z)
    c_u, c_v = jnp.split(c_z, 2, axis=-1)
    c_v = layernorm(c_v, ln_c_g, ln_c_b)
    yc = chunk_spatial_gate(c_u, c_v, gmlp_ws, gmlp_b)
    y = jnp.concatenate([ya, yb, yc], axis=-1)
    bsz, s, _ = y.shape
    y = rmsnorm(y.reshape(bsz, s, N_MIX_GROUPS, HEAD_GROUP),
                mix_out_g.reshape(N_MIX_GROUPS, HEAD_GROUP)).reshape(bsz, s, MIX_WIDTH)
    return y @ w_mix_out

def memory_cross_attention(xn, memn, w_xq, w_xkv, w_xo):
    bsz, s, _ = xn.shape
    m = memn.shape[1]
    q = (xn @ w_xq).reshape(bsz, s, X_HEADS, X_HEAD_DIM)
    k, v = jnp.split(memn @ w_xkv, 2, axis=-1)
    k = k.reshape(bsz, m, X_HEADS, X_HEAD_DIM)
    v = v.reshape(bsz, m, X_HEADS, X_HEAD_DIM)
    scores = jnp.einsum("bshd,bmhd->bhsm", q, k).astype(jnp.float32) * (X_HEAD_DIM ** -0.5)
    p = jax.nn.softmax(scores, axis=-1).astype(v.dtype)
    o = jnp.einsum("bhsm,bmhd->bshd", p, v).reshape(bsz, s, D_MODEL)
    return o @ w_xo

def swiglu(x, w_gate, w_up, w_down):
    return (jax.nn.silu(x @ w_gate) * (x @ w_up)) @ w_down

def moe_swiglu(xn, w_router, w_gate, w_up, w_down):
    bsz, s, d = xn.shape
    xt = xn.reshape(-1, d)
    logits = (xt @ w_router).astype(jnp.float32)
    top_vals, top_idx = lax.top_k(logits, TOP_K)
    top_w = jax.nn.softmax(top_vals, axis=-1)
    combine = jnp.sum(jax.nn.one_hot(top_idx, N_EXPERTS, dtype=jnp.float32) * top_w[..., None], axis=1)
    combine = combine.astype(xn.dtype)
    y = jnp.zeros_like(xt)
    for e in range(N_EXPERTS):
        y = y + combine[:, e:e + 1] * swiglu(xt, w_gate[e], w_up[e], w_down[e])
    return y.reshape(bsz, s, d)

def first_inputs(seed: int = 0) -> dict:
    key = jax.random.key(seed)
    ks = jax.random.split(key, 32)
    f32 = jnp.float32

    def nrm(k, shape, scale):
        return jax.random.normal(k, shape, f32) * scale

    def gain(k, shape):
        return 1.0 + 0.02 * jax.random.normal(k, shape, f32)

    return {
        "x": nrm(ks[0], (BATCH, SEQ, D_MODEL), 1.0),
        "mem": nrm(ks[1], (BATCH, MEM_LEN, D_MODEL), 1.0),
        "norm_mix_g": gain(ks[2], (DEPTH, D_MODEL)),
        "w_in": nrm(ks[3], (DEPTH, D_MODEL, PROJ_WIDTH), D_MODEL ** -0.5),
        "conv_a_w": nrm(ks[4], (DEPTH, A_KERNEL, A_WIDTH), A_KERNEL ** -0.5),
        "conv_a_b": nrm(ks[5], (DEPTH, A_WIDTH), 0.02),
        "ln_a_g": gain(ks[6], (DEPTH, A_WIDTH)),
        "ln_a_b": nrm(ks[7], (DEPTH, A_WIDTH), 0.02),
        "conv_b_w": nrm(ks[8], (DEPTH, B_KERNEL, B_WIDTH), B_KERNEL ** -0.5),
        "ln_c_g": gain(ks[9], (DEPTH, C_WIDTH)),
        "ln_c_b": nrm(ks[10], (DEPTH, C_WIDTH), 0.02),
        "gmlp_ws": nrm(ks[11], (DEPTH, C_GROUPS, GMLP_BLOCK, GMLP_BLOCK), GMLP_BLOCK ** -0.5),
        "gmlp_b": 1.0 + nrm(ks[12], (DEPTH, C_GROUPS, GMLP_BLOCK), 0.1),
        "mix_out_g": gain(ks[13], (DEPTH, MIX_WIDTH)),
        "w_mix_out": nrm(ks[14], (DEPTH, MIX_WIDTH, D_MODEL), MIX_WIDTH ** -0.5),
        "norm_x_g": gain(ks[15], (DEPTH, D_MODEL)),
        "norm_mem_g": gain(ks[16], (DEPTH, D_MODEL)),
        "w_xq": nrm(ks[17], (DEPTH, D_MODEL, D_MODEL), D_MODEL ** -0.5),
        "w_xkv": nrm(ks[18], (DEPTH, D_MODEL, 2 * D_MODEL), D_MODEL ** -0.5),
        "w_xo": nrm(ks[19], (DEPTH, D_MODEL, D_MODEL), D_MODEL ** -0.5),
        "norm_ffn_g": gain(ks[20], (DEPTH, D_MODEL)),
        "ffn_w_gate": nrm(ks[21], (N_DENSE, D_MODEL, D_FF), D_MODEL ** -0.5),
        "ffn_w_up": nrm(ks[22], (N_DENSE, D_MODEL, D_FF), D_MODEL ** -0.5),
        "ffn_w_down": nrm(ks[23], (N_DENSE, D_FF, D_MODEL), D_FF ** -0.5),
        "moe_router": nrm(ks[24], (N_MOE, D_MODEL, N_EXPERTS), D_MODEL ** -0.5),
        "moe_w_gate": nrm(ks[25], (N_MOE, N_EXPERTS, D_MODEL, D_EXPERT), D_MODEL ** -0.5),
        "moe_w_up": nrm(ks[26], (N_MOE, N_EXPERTS, D_MODEL, D_EXPERT), D_MODEL ** -0.5),
        "moe_w_down": nrm(ks[27], (N_MOE, N_EXPERTS, D_EXPERT, D_MODEL), D_EXPERT ** -0.5),
        "norm_final_g": gain(ks[28], (D_MODEL,)),
    }

def first_block(x, mem, norm_mix_g, w_in, conv_a_w, conv_a_b, ln_a_g, ln_a_b, conv_b_w,
              ln_c_g, ln_c_b, gmlp_ws, gmlp_b, mix_out_g, w_mix_out, norm_x_g, norm_mem_g,
              w_xq, w_xkv, w_xo, norm_ffn_g, ffn_w_gate, ffn_w_up, ffn_w_down,
              moe_router, moe_w_gate, moe_w_up, moe_w_down, norm_final_g):
    h = x
    for layer in range(DEPTH):
        h = h + hybrid_mixer(rmsnorm(h, norm_mix_g[layer]), w_in[layer], conv_a_w[layer],
                             conv_a_b[layer], ln_a_g[layer], ln_a_b[layer], conv_b_w[layer],
                             ln_c_g[layer], ln_c_b[layer], gmlp_ws[layer], gmlp_b[layer],
                             mix_out_g[layer], w_mix_out[layer])
        h = h + memory_cross_attention(rmsnorm(h, norm_x_g[layer]), rmsnorm(mem, norm_mem_g[layer]),
                                       w_xq[layer], w_xkv[layer], w_xo[layer])
        hn = rmsnorm(h, norm_ffn_g[layer])
        i = layer // 2
        if layer % 2 == 0:
            h = h + swiglu(hn, ffn_w_gate[i], ffn_w_up[i], ffn_w_down[i])
        else:
            h = h + moe_swiglu(hn, moe_router[i], moe_w_gate[i], moe_w_up[i], moe_w_down[i])
    return rmsnorm(h, norm_final_g)


HEAD_DIM = 64
N_HEADS_A = 8
N_HEADS_B = 8
N_KV_HEADS_B = 2
DILATED_BRANCHES = ((128, 1), (512, 4), (2048, 16))
WINDOW_B = 128
REL_BUCKETS = 32
REL_MAX_DIST = 1024
N_REL_HEADS = N_HEADS_A + N_HEADS_B
D_ATTN_IN = (3 * N_HEADS_A + N_HEADS_B + 2 * N_KV_HEADS_B) * HEAD_DIM
D_ATTN_OUT = (N_HEADS_A + N_HEADS_B) * HEAD_DIM
RWKV_HEAD = 64
RWKV_HEADS = D_MODEL // RWKV_HEAD
DECAY_LORA = 64
AAA_LORA = 64
GATE_LORA = 128
D_FF_2 = 4 * D_MODEL
N_ATTN_LAYERS = (DEPTH + 1) // 2
N_RWKV_LAYERS = DEPTH // 2
NORM_EPS = 1e-6
GN_EPS = 64e-5
NEG_INF = -1e30


F32 = jnp.float32

def rms_norm(x, g):
    x32 = x.astype(F32)
    y = x32 * lax.rsqrt(jnp.mean(x32 * x32, axis=-1, keepdims=True) + NORM_EPS)
    return (y * g.astype(F32)).astype(x.dtype)

def t5_bucket(rel):
    nb = REL_BUCKETS // 2
    max_exact = nb // 2
    bucket = jnp.where(rel > 0, nb, 0)
    n = jnp.abs(rel)
    nf = jnp.maximum(n, 1).astype(F32)
    large = max_exact + (jnp.log(nf / max_exact) / math.log(REL_MAX_DIST / max_exact)
                         * (nb - max_exact)).astype(jnp.int32)
    large = jnp.minimum(large, nb - 1)
    return bucket + jnp.where(n < max_exact, n, large)

def band_rel_bias(table_h, block, dilation):
    i = jnp.arange(block)[:, None]
    j = jnp.arange(3 * block)[None, :]
    bucket = t5_bucket((j - block - i) * dilation)
    return jnp.transpose(table_h[bucket], (2, 0, 1))

def banded_attention(q, k, v, bias, radius, block, sink=None):
    nB, H, G, L, hd = q.shape
    nb = -(-L // block)
    pad = nb * block - L
    qb = jnp.pad(q, [(0, 0)] * 3 + [(0, pad), (0, 0)]).reshape(nB, H, G, nb, block, hd)

    def windows(t):
        tb = jnp.pad(t, [(0, 0)] * 3 + [(block, block + pad), (0, 0)]).reshape(nB, H, G, nb + 2, block, hd)
        return jnp.concatenate([tb[:, :, :, :-2], tb[:, :, :, 1:-1], tb[:, :, :, 2:]], axis=-2)

    kb, vb = windows(k), windows(v)
    valid = jnp.pad(jnp.ones((L,), bool), (block, block + pad)).reshape(nb + 2, block)
    valid = jnp.concatenate([valid[:-2], valid[1:-1], valid[2:]], axis=-1)
    rel = jnp.arange(3 * block)[None, :] - block - jnp.arange(block)[:, None]
    mask = (jnp.abs(rel) <= radius)[None] & valid[:, None, :]
    s = jnp.einsum('bhgnqd,bhgnkd->bhgnqk', qb, kb).astype(F32) * (hd ** -0.5)
    s = s + bias.astype(F32)[None, :, None, None]
    s = jnp.where(mask, s, NEG_INF)
    m = jnp.max(s, axis=-1)
    if sink is not None:
        sink_b = sink.astype(F32)[None, :, None, None, None]
        m = jnp.maximum(m, sink_b)
    p = jnp.exp(s - m[..., None])
    denom = jnp.sum(p, axis=-1)
    if sink is not None:
        denom = denom + jnp.exp(sink_b - m)
    o = jnp.einsum('bhgnqk,bhgnkd->bhgnqd', p, vb.astype(F32)) / denom[..., None]
    lse = m + jnp.log(denom)
    o = o.reshape(nB, H, G, nb * block, hd)[..., :L, :]
    lse = lse.reshape(nB, H, G, nb * block)[..., :L]
    return o, lse

def dilated_attention(q, k, v, table_a):
    nB, H, S, hd = q.shape
    outs, lses = [], []
    for window, dil in DILATED_BRANCHES:
        radius = window // 2 // dil

        def split(t):
            return t.reshape(nB, H, S // dil, dil, hd).transpose(0, 1, 3, 2, 4)

        bias = band_rel_bias(table_a, radius, dil)
        o, lse = banded_attention(split(q), split(k), split(v), bias, radius, radius)
        outs.append(o.transpose(0, 1, 3, 2, 4).reshape(nB, H, S, hd))
        lses.append(lse.transpose(0, 1, 3, 2).reshape(nB, H, S))
    wts = jax.nn.softmax(jnp.stack(lses), axis=0)
    return jnp.einsum('rbhs,rbhsd->bhsd', wts, jnp.stack(outs))

def window_gqa(q, k, v, sink, table_b):
    rep = N_HEADS_B // N_KV_HEADS_B
    k = jnp.repeat(k, rep, axis=1)
    v = jnp.repeat(v, rep, axis=1)
    bias = band_rel_bias(table_b, WINDOW_B, 1)
    o, _ = banded_attention(q[:, :, None], k[:, :, None], v[:, :, None], bias, WINDOW_B, WINDOW_B, sink)
    return o[:, :, 0]

def attention_mixer(h, w_in, sink, w_out, rel_table):
    nB, S, _ = h.shape
    proj = h @ w_in
    sizes = [N_HEADS_A * HEAD_DIM] * 3 + [N_HEADS_B * HEAD_DIM, N_KV_HEADS_B * HEAD_DIM, N_KV_HEADS_B * HEAD_DIM]
    cuts = [int(c) for c in np.cumsum(sizes)[:-1]]
    qa, ka, va, qb, kb, vb = jnp.split(proj, cuts, axis=-1)

    def heads(t):
        return t.reshape(nB, S, -1, HEAD_DIM).transpose(0, 2, 1, 3)

    oa = dilated_attention(heads(qa), heads(ka), heads(va), rel_table[:, :N_HEADS_A])
    ob = window_gqa(heads(qb), heads(kb), heads(vb), sink, rel_table[:, N_HEADS_A:])
    o = jnp.concatenate([oa, ob], axis=1).astype(h.dtype)
    o = o.transpose(0, 2, 1, 3).reshape(nB, S, D_ATTN_OUT)
    return o @ w_out

def rwkv7_scan(r, w, k, v, kk, a):
    def step(state, inp):
        r_t, w_t, k_t, v_t, kk_t, a_t = inp
        sa = jnp.einsum('bhvk,bhk->bhv', state, -kk_t)
        state = (state * w_t[:, :, None, :] + sa[..., None] * (kk_t * a_t)[:, :, None, :]
                 + v_t[..., None] * k_t[:, :, None, :])
        return state, jnp.einsum('bhvk,bhk->bhv', state, r_t)

    nB, S, H, N = r.shape
    xs = tuple(jnp.moveaxis(t, 1, 0) for t in (r, w, k, v, kk, a))
    _, out = lax.scan(step, jnp.zeros((nB, H, N, N), F32), xs)
    return jnp.moveaxis(out, 0, 1)

def group_norm(o, gn_w, gn_b):
    mu = jnp.mean(o, axis=-1, keepdims=True)
    var = jnp.mean(jnp.square(o - mu), axis=-1, keepdims=True)
    y = (o - mu) * lax.rsqrt(var + GN_EPS)
    nB, S, H, N = o.shape
    return y.reshape(nB, S, H * N) * gn_w.astype(F32) + gn_b.astype(F32)

def rwkv7_mixer(h, mu_prev, mu_next, w_r, w_k, w_v, w_o, k_k, k_a, r_k, gn_w, gn_b,
                w0, w1, w2, a0, a1, a2, g1, g2):
    nB, S, D = h.shape
    H, N = RWKV_HEADS, RWKV_HEAD
    dx_p = jnp.pad(h, ((0, 0), (1, 0), (0, 0)))[:, :-1] - h
    dx_n = jnp.pad(h, ((0, 0), (0, 1), (0, 0)))[:, 1:] - h

    def mix(c):
        return h + dx_p * mu_prev[c] + dx_n * mu_next[c]

    def heads(t):
        return t.astype(F32).reshape(nB, S, H, N)

    xw, xa, xg = mix(1), mix(4), mix(5)
    r = mix(0) @ w_r
    k = mix(2) @ w_k
    v = mix(3) @ w_v
    kk = heads(k * k_k)
    kk = kk / jnp.maximum(jnp.sqrt(jnp.sum(kk * kk, axis=-1, keepdims=True)), 1e-12)
    rh, vh = heads(r), heads(v)
    dir_out = []
    for d in range(2):
        w_log = -jax.nn.softplus(-(w0[d] + jnp.tanh(xw @ w1[d]) @ w2[d])) - 0.5
        decay = jnp.exp(-jnp.exp(w_log.astype(F32)))
        a = jax.nn.sigmoid(a0[d] + (xa @ a1[d]) @ a2[d])
        g = jax.nn.sigmoid(xg @ g1[d]) @ g2[d]
        kd = heads(k * (1 + (a - 1) * k_a))
        ins = [rh, heads(decay), kd, vh, kk, heads(a)]
        if d == 1:
            ins = [jnp.flip(t, axis=1) for t in ins]
        o = rwkv7_scan(*ins)
        if d == 1:
            o = jnp.flip(o, axis=1)
        bonus = jnp.sum(rh * kd * r_k.astype(F32), axis=-1, keepdims=True) * vh
        dir_out.append((group_norm(o, gn_w, gn_b) + bonus.reshape(nB, S, D)) * g.astype(F32))
    y = dir_out[0] + dir_out[1]
    return y.astype(h.dtype) @ w_o

def second_inputs(seed: int = 0) -> dict:
    key = jax.random.key(seed)
    ks = iter(jax.random.split(key, 40))

    def nrm(shape, scale):
        return scale * jax.random.normal(next(ks), shape, F32)

    NA, NR, D = N_ATTN_LAYERS, N_RWKV_LAYERS, D_MODEL
    return {
        'x': nrm((BATCH, SEQ, D), 1.0),
        'rel_table': nrm((REL_BUCKETS, N_REL_HEADS), 0.5),
        'norm_g': 1.0 + nrm((DEPTH, 4, D), 0.05),
        'attn_w_in': nrm((NA, D, D_ATTN_IN), D ** -0.5),
        'attn_sink': nrm((NA, N_HEADS_B), 0.5),
        'attn_w_out': nrm((NA, D_ATTN_OUT, D), D_ATTN_OUT ** -0.5),
        'rk_mu_prev': jax.random.uniform(next(ks), (NR, 6, D), F32, 0.0, 0.5),
        'rk_mu_next': jax.random.uniform(next(ks), (NR, 6, D), F32, 0.0, 0.5),
        'rk_w_r': nrm((NR, D, D), D ** -0.5),
        'rk_w_k': nrm((NR, D, D), D ** -0.5),
        'rk_w_v': nrm((NR, D, D), D ** -0.5),
        'rk_w_o': nrm((NR, D, D), D ** -0.5),
        'rk_k_k': 0.85 + nrm((NR, D), 0.05),
        'rk_k_a': 1.0 + nrm((NR, D), 0.05),
        'rk_r_k': nrm((NR, RWKV_HEADS, RWKV_HEAD), 0.1),
        'rk_gn_w': 1.0 + nrm((NR, D), 0.05),
        'rk_gn_b': nrm((NR, D), 0.02),
        'rk_w0': -2.0 + nrm((NR, 2, D), 1.0),
        'rk_w1': nrm((NR, 2, D, DECAY_LORA), D ** -0.5),
        'rk_w2': nrm((NR, 2, DECAY_LORA, D), 0.1 * DECAY_LORA ** -0.5),
        'rk_a0': nrm((NR, 2, D), 0.5),
        'rk_a1': nrm((NR, 2, D, AAA_LORA), D ** -0.5),
        'rk_a2': nrm((NR, 2, AAA_LORA, D), 0.5 * AAA_LORA ** -0.5),
        'rk_g1': nrm((NR, 2, D, GATE_LORA), D ** -0.5),
        'rk_g2': nrm((NR, 2, GATE_LORA, D), GATE_LORA ** -0.5),
        'mlp_w1': nrm((DEPTH, D, D_FF_2), D ** -0.5),
        'mlp_w2': nrm((DEPTH, D_FF_2, D), D_FF_2 ** -0.5),
    }

def second_block(x, rel_table, norm_g, attn_w_in, attn_sink, attn_w_out,
              rk_mu_prev, rk_mu_next, rk_w_r, rk_w_k, rk_w_v, rk_w_o, rk_k_k, rk_k_a, rk_r_k,
              rk_gn_w, rk_gn_b, rk_w0, rk_w1, rk_w2, rk_a0, rk_a1, rk_a2, rk_g1, rk_g2,
              mlp_w1, mlp_w2):
    h = x
    for layer in range(DEPTH):
        g = norm_g[layer]
        i = layer // 2
        u = rms_norm(h, g[0])
        if layer % 2 == 0:
            u = attention_mixer(u, attn_w_in[i], attn_sink[i], attn_w_out[i], rel_table)
        else:
            u = rwkv7_mixer(u, rk_mu_prev[i], rk_mu_next[i], rk_w_r[i], rk_w_k[i], rk_w_v[i], rk_w_o[i],
                            rk_k_k[i], rk_k_a[i], rk_r_k[i], rk_gn_w[i], rk_gn_b[i],
                            rk_w0[i], rk_w1[i], rk_w2[i], rk_a0[i], rk_a1[i], rk_a2[i], rk_g1[i], rk_g2[i])
        h = h + rms_norm(u, g[1])
        u = rms_norm(h, g[2])
        u = jnp.square(jax.nn.relu(u @ mlp_w1[layer])) @ mlp_w2[layer]
        h = h + rms_norm(u, g[3])
    return h


def setup_inputs(seed=0):
    out = dict(first_inputs(seed))
    for name, value in second_inputs(seed + 1).items():
        if name != "x":
            out[name + "_2"] = value
    return out


def reference(
    x, mem, norm_mix_g, w_in, conv_a_w, conv_a_b, ln_a_g, ln_a_b, conv_b_w, ln_c_g, ln_c_b,
    gmlp_ws, gmlp_b, mix_out_g, w_mix_out, norm_x_g, norm_mem_g, w_xq, w_xkv, w_xo, norm_ffn_g,
    ffn_w_gate, ffn_w_up, ffn_w_down, moe_router, moe_w_gate, moe_w_up, moe_w_down,
    norm_final_g, rel_table_2, norm_g_2, attn_w_in_2, attn_sink_2, attn_w_out_2, rk_mu_prev_2,
    rk_mu_next_2, rk_w_r_2, rk_w_k_2, rk_w_v_2, rk_w_o_2, rk_k_k_2, rk_k_a_2, rk_r_k_2,
    rk_gn_w_2, rk_gn_b_2, rk_w0_2, rk_w1_2, rk_w2_2, rk_a0_2, rk_a1_2, rk_a2_2, rk_g1_2,
    rk_g2_2, mlp_w1_2, mlp_w2_2,
):
    x = first_block(
        x, mem, norm_mix_g, w_in, conv_a_w, conv_a_b, ln_a_g, ln_a_b, conv_b_w, ln_c_g, ln_c_b,
        gmlp_ws, gmlp_b, mix_out_g, w_mix_out, norm_x_g, norm_mem_g, w_xq, w_xkv, w_xo,
        norm_ffn_g, ffn_w_gate, ffn_w_up, ffn_w_down, moe_router, moe_w_gate, moe_w_up,
        moe_w_down, norm_final_g,
    )
    return second_block(
        x, rel_table_2, norm_g_2, attn_w_in_2, attn_sink_2, attn_w_out_2, rk_mu_prev_2,
        rk_mu_next_2, rk_w_r_2, rk_w_k_2, rk_w_v_2, rk_w_o_2, rk_k_k_2, rk_k_a_2, rk_r_k_2,
        rk_gn_w_2, rk_gn_b_2, rk_w0_2, rk_w1_2, rk_w2_2, rk_a0_2, rk_a1_2, rk_a2_2, rk_g1_2,
        rk_g2_2, mlp_w1_2, mlp_w2_2,
    )


_drawn_inputs = setup_inputs


def setup_inputs(seed=0):
    import zlib

    import numpy as np

    out = dict(_drawn_inputs(seed))
    spreads = {}
    factors = {'ln_c_g': 3.19,
     'ln_c_b': 2.718,
     'norm_x_g': 7.948,
     'norm_mem_g': 3.091,
     'attn_sink_2': 8.0,
     'rk_gn_b_2': 5.81,
     'rk_w1_2': 2.864,
     'rk_w2_2': 3.247}
    for name, (base, spread) in spreads.items():
        noise = np.random.default_rng([zlib.crc32(name.encode()), seed]).standard_normal(out[name].shape)
        drawn = base * np.exp(spread * noise) if base else spread * noise
        out[name] = __import__('jax').numpy.asarray(drawn.astype(out[name].dtype))
    for name, factor in factors.items():
        out[name] = (out[name] * factor).astype(out[name].dtype)
    return out
```

```python
from contextlib import ExitStack

import numpy as np

import concourse.bass as bass
from concourse import mybir
from concourse.alu_op_type import AluOpType as ALU

F32 = mybir.dt.float32
I32 = mybir.dt.int32
U32 = mybir.dt.uint32
ACT = mybir.ActivationFunctionType
AX_X = mybir.AxisListType.X

P = 128
SEQ = 256
D = 1024
TT = SEQ // P
KC = D // P
EPS = 1e-6
GN_EPS = 64e-5
HEAD = 64
A_W, B_W, C_W = 384, 320, 320
A_TILES = A_W // P
B_TILES = [(0, 128), (128, 64), (192, 128)]
C_PIECES = [(0, 256), (256, 256), (512, 128)]
A_TAPS, B_TAPS = 31, 3
C_GROUPS = C_W // HEAD
N_EXPERTS = 8
SLOTS = 96
MAX_TILES = -(-SEQ // SLOTS)
VIRTUAL = MAX_TILES * N_EXPERTS
MAX_ITEMS = N_EXPERTS + (2 * SEQ - 1) // (SLOTS + 1)
CHUNK = 256
RING = 8
UNIT = KC * 256
DIST = 2 * SEQ


class Signal:

    def __init__(self, sem):
        self.sem, self.base = sem, 0

    def at(self, n):
        return self.base + n

    def over(self, n):
        self.base += n


class Chain:

    def __init__(self, eng, counter):
        self.eng, self.counter, self.n = eng, counter, 0

    def do(self, ins):
        ins.then_inc(self.counter.sem, 1)
        self.n += 1
        return self.n

    def wait(self, n=None):
        self.eng.wait_ge(self.counter.sem, self.counter.at(self.n if n is None else n))

    def link(self, ins):
        self.do(ins)
        self.wait()


class Weights:

    def __init__(self, ring, loaded, used):
        self.ring, self.loaded, self.used = ring, loaded, used
        self.runs = []
        self.loads = [0] * RING

    def slot(self, n):
        return self.ring[:, n, :]


class Run:
    def __init__(self, weights, first, pieces):
        self.w, self.first, self.pieces = weights, first, pieces
        self.issued = self.taken = 0
        self.value, self.used_at = {}, {}

    def place(self, u):
        src = self.pieces[u]
        _, a, b = src.shape
        return self.w.slot((self.first + u) % RING)[:, 0:a * b].rearrange("p (a b) -> p a b", a=a)

    def load_until(self, sp, n):
        while self.issued < min(n, len(self.pieces)):
            u = self.issued
            s = (self.first + u) % RING
            if u >= RING:
                sp.wait_ge(self.w.used.sem, self.used_at[u - RING])
            self.w.loads[s] += 16
            self.value[u] = self.w.loads[s]
            sp.dma_start(self.place(u), self.pieces[u]).then_inc(self.w.loaded[s], 16)
            self.issued += 1


def by_cols(w, width):
    v = w.rearrange("(c p) n -> p c n", p=P)
    return [v[:, :, i:i + width] for i in range(0, w.shape[1], width)]


class Model:
    def __init__(self, nc, I, out, ctx):
        self.nc, self.I, self.out, self.ctx = nc, I, out, ctx
        self.n_tmp = 0
        self.named = {}
        sb, sem = self.sb, self.sem
        self.h = sb("h", [P, TT, D])
        self.xT = sb("xT", [P, KC, SEQ])
        self.ring = sb("ring", [P, RING, UNIT])
        self.ident = sb("ident", [P, P])
        self.ones = sb("ones", [P, P])
        self.neg_half = sb("neg_half", [P, 64])
        self.cols = sb("cols", [P, 6, P])
        self.ps = ctx.enter_context(nc.psum_tensor("ps", [P, 8, 512], F32))
        self.piece_loaded = [ctx.enter_context(nc.semaphore(f"piece_loaded{i}")) for i in range(RING)]
        self.product_done = sem("product_done")
        self.weights = Weights(self.ring, self.piece_loaded, self.product_done)
        self.side_loaded = sem("side_loaded")
        self.squares_summed = sem("squares_summed")
        self.pool_step = sem("pool_step")
        self.rstd_ready = sem("rstd_ready")
        self.rows_scaled = sem("rows_scaled")
        self.turned = sem("turned")
        self.out_stored = sem("out_stored")
        self.evac_dve = sem("evac_dve")
        self.evac_act = sem("evac_act")
        self.vec_step = sem("vec_step")
        self.act_step = sem("act_step")
        self.pe_step = sem("pe_step")
        self.pool_done = sem("pool_done")
        self.scores_done = sem("scores_done")
        self.max_ready = sem("max_ready")
        self.probs_ready = sem("probs_ready")
        self.probs_turned = sem("probs_turned")
        self.probsT_ready = sem("probsT_ready")
        self.heads_done = sem("heads_done")
        self.head_stored = sem("head_stored")
        self.mlp = self.mlp_signals("ffn_")
        self.moe = self.mlp_signals("moe_")
        self.pick_ready = sem("moe_pick_ready")
        self.gathered = sem("moe_gathered")
        self.xg_ready = sem("moe_xg_ready")
        self.pick_turned = sem("moe_pick_turned")
        self.pickT_ready = sem("moe_pickT_ready")
        self.y_done = sem("moe_y_done")
        self.y_copied = sem("moe_y_copied")
        self.combined = sem("moe_combined")
        self.added = sem("moe_added")

    def sb(self, name, shape, dt=F32, ctx=None):
        return (ctx or self.ctx).enter_context(self.nc.sbuf_tensor(name, shape, dt))

    def tmp(self, ctx, name, shape, dt=F32):
        self.n_tmp += 1
        return self.sb(f"{name}_{self.n_tmp}", shape, dt, ctx)

    def sem(self, name):
        return Signal(self.ctx.enter_context(self.nc.semaphore(name)))

    def mlp_signals(self, pre):
        sem = self.sem
        s = {n: sem(pre + n) for n in ("gate_done", "up_done", "down_done", "act_done", "hidden_ready")}
        s["loaded"] = [[sem(f"{pre}{kind}{p}_loaded") for p in range(2)] for kind in ("gate", "up", "down")]
        return s

    def block(self):
        return self.nc.Block(no_gpsimd_drain=True)

    def col(self, name, c=0):
        t, r = self.col_at[name]
        return self.cols[:, t, r + c:r + c + 1]

    def constants(self):
        nc, I = self.nc, self.I
        tables, self.col_at = [[] for _ in range(6)], {}
        fill = [0] * 6

        def put(t, name, src, wide=P):
            n = src.shape[0]
            self.col_at[name] = (t, fill[t])
            tables[t].append((fill[t], n, wide, src))
            fill[t] += n

        def put_vec(t, name, src):
            put(t, name, src.rearrange("(c p) -> c p", p=P))

        for l in range(2):
            for n in ("norm_mix_g", "mix_out_g", "norm_x_g", "norm_mem_g", "norm_ffn_g"):
                put_vec(0, f"{n}{l}", I[n][l])
            for j in (0, 2):
                put_vec(0, f"norm2_{l}{j}", I["norm_g_2"][l, j])
        for m in range(6):
            put_vec(1, f"mu_prev{m}", I["rk_mu_prev_2"][0, m])
            put_vec(1, f"mu_next{m}", I["rk_mu_next_2"][0, m])
        put_vec(1, "k_k", I["rk_k_k_2"][0])
        put_vec(1, "k_a", I["rk_k_a_2"][0])
        put(1, "r_k", I["rk_r_k_2"][0].rearrange("(c a) b -> c (a b)", a=2))
        for d in range(2):
            put_vec(2, f"w0{d}", I["rk_w0_2"][0, d])
            put_vec(2, f"a0{d}", I["rk_a0_2"][0, d])
        for l in range(2):
            put(2, f"conv_a_b{l}", I["conv_a_b"][l].rearrange("(c p) -> c p", p=P))
            put(2, f"gmlp_b{l}", I["gmlp_b"][l])
            for i, (o, n) in enumerate(B_TILES):
                put(2, f"conv_b{l}{i}", I["conv_b_w"][l, :, o:o + n], n)
            for i in range(A_TILES):
                put(3 + l, f"conv_a{l}{i}", I["conv_a_w"][l, :, i * P:(i + 1) * P])
        with ExitStack() as ctx:
            raw = self.tmp(ctx, "raw", [P, 6, P])
            loads = sum(len(t) for t in tables)
            with self.block() as block:
                @block.sync
                def _(sp):
                    sp.dma_start(self.h[:], I["x"].rearrange("a (t p) d -> p (a t) d", p=P)).then_inc(self.side_loaded.sem, 16)
                    sp.wait_ge(self.pool_done.sem, self.pool_done.at(1))
                    for t, rows in enumerate(tables):
                        for r, n, wide, src in rows:
                            sp.dma_start(raw[r:r + n, t, 0:wide], src).then_inc(self.side_loaded.sem, 16)
                    self.run.load_until(sp, RING)

                @block.gpsimd
                def _(pool):
                    pool.memset(raw[:], 0.0).then_inc(self.pool_done.sem, 1)
                    pool.memset(self.ones[:], 1.0).then_inc(self.pool_done.sem, 1)
                    pool.memset(self.neg_half[:], -0.5)
                    pool.wait_ge(self.pool_done.sem, self.pool_done.at(2))
                    pool.affine_select(out=self.ident[:], in_=self.ones[:], compare_op=ALU.is_equal, fill=0.0, base=0,
                                       pattern=[[-1, P]], channel_multiplier=1).then_inc(self.pool_done.sem, 1)

                @block.tensor
                def _(pe):
                    pe.wait_ge(self.pool_done.sem, self.pool_done.at(3))
                    pe.wait_ge(self.side_loaded.sem, self.side_loaded.at(16 * (loads + 1)))
                    for t in range(5):
                        last = pe.transpose(self.ps[:, t // 4, (t % 4) * P:(t % 4 + 1) * P], raw[:, t, :], self.ident[:])
                    last.then_inc(self.turned.sem, 1)

                @block.vector
                def _(dve):
                    dve.wait_ge(self.turned.sem, self.turned.at(1))
                    dve.tensor_copy(self.cols[:, 0:4, :], self.ps[:, 0, :].rearrange("p (a b) -> p a b", a=4))
                    dve.tensor_copy(self.cols[:, 4, :], self.ps[:, 1, 0:P])
            self.side_loaded.over(16 * (loads + 1))
            self.pool_done.over(3)
            self.turned.over(1)

    def norm_turn(self, src, gain, dst, keep_rows=None, norm=True):
        with ExitStack() as ctx:
            junk = self.tmp(ctx, "junk", [P, D])
            rows = keep_rows if keep_rows is not None else self.tmp(ctx, "rows", [P, TT, D])
            if not norm:
                rows = src
            stat = self.tmp(ctx, "stat", [P, 3, TT])
            with self.block() as block:
                @block.sync
                def _(sp):
                    self.run.load_until(sp, self.run.taken + RING)

                if norm:
                    @block.gpsimd
                    def _(pool):
                        pool.wait_ge(self.squares_summed.sem, self.squares_summed.at(TT))
                        pool.tensor_scalar(stat[:, 1, :], stat[:, 0, :], 1.0 / D, EPS, ALU.mult, ALU.add).then_inc(self.pool_step.sem, 1)
                        pool.wait_ge(self.pool_step.sem, self.pool_step.at(1))
                        pool.tensor_tensor(stat[:, 2, :], stat[:, 1, :], self.neg_half[:, 0:TT], ALU.pow).then_inc(self.rstd_ready.sem, 1)

                @block.tensor
                def _(pe):
                    for t in range(TT):
                        if norm:
                            pe.wait_ge(self.rows_scaled.sem, self.rows_scaled.at(t + 1))
                        for c in range(KC):
                            last = pe.transpose(self.ps[:, c // 2, (c % 2) * SEQ + t * P:(c % 2) * SEQ + (t + 1) * P],
                                                rows[:, t, c * P:(c + 1) * P], self.ident[:])
                            if t == TT - 1:
                                last.then_inc(self.turned.sem, 1)

                def turned_cols(c):
                    return self.ps[:, c // 2, (c % 2) * SEQ:(c % 2 + 1) * SEQ]

                @block.scalar
                def _(act):
                    if norm:
                        for t in range(TT):
                            if t:
                                act.wait_ge(self.squares_summed.sem, self.squares_summed.at(t))
                            act.activation(junk[:], src[:, t, :], ACT.Square, accum_out=stat[:, 0, t:t + 1]).then_inc(self.squares_summed.sem, 1)
                    for c in (2, 3, 6, 7):
                        act.wait_ge(self.turned.sem, self.turned.at((c | 1) + 1))
                        act.activation(dst[:, c, :], turned_cols(c), ACT.Copy, scale=self.col(gain, c))

                @block.vector
                def _(dve):
                    if norm:
                        dve.wait_ge(self.rstd_ready.sem, self.rstd_ready.at(1))
                        for t in range(TT):
                            dve.tensor_scalar(rows[:, t, :], src[:, t, :], stat[:, 2, t:t + 1], None, ALU.mult).then_inc(self.rows_scaled.sem, 1)
                    for c in (0, 1, 4, 5):
                        dve.wait_ge(self.turned.sem, self.turned.at((c | 1) + 1))
                        dve.tensor_scalar(dst[:, c, :], turned_cols(c), self.col(gain, c), None, ALU.mult)
            if norm:
                self.squares_summed.over(TT)
                self.pool_step.over(1)
                self.rstd_ready.over(1)
                self.rows_scaled.over(TT)
            self.turned.over(KC)

    def products(self, jobs, extra=None):
        run = self.run
        first = run.taken
        pieces = sorted({j[0] for j in jobs})
        assert pieces == list(range(len(pieces)))
        last_job = {p: max(n for n, j in enumerate(jobs) if j[0] == p) for p in pieces}
        banks = 8
        for p in pieces:
            run.used_at[first + p] = self.product_done.at(last_job[p] + 1)

        def bank(n, dst):
            m, w = dst.shape[0], dst.shape[1]
            return self.ps[0:m, n % banks, 0:w]

        chain = Chain(self.nc.vector, self.vec_step)
        with self.block() as block:
            @block.sync
            def _(sp):
                run.load_until(sp, first + len(pieces) + RING)

            @block.tensor
            def _(pe):
                seen = set()
                for n, (p, pairs, dst, add) in enumerate(jobs):
                    u = first + p
                    if p not in seen:
                        pe.wait_ge(self.piece_loaded[(run.first + u) % RING], run.value[u])
                        seen.add(p)
                    if n >= banks:
                        who = self.evac_dve if n % 2 == 0 else self.evac_act
                        pe.wait_ge(who.sem, who.at((n - banks) // 2 + 1))
                    here = run.place(u)
                    for i, (left, right) in enumerate(pairs):
                        mm = pe.matmul(bank(n, dst), left(here), right(here), start=(i == 0), stop=(i == len(pairs) - 1))
                    mm.then_inc(self.product_done.sem, 1)

            @block.vector
            def _(dve):
                if extra is not None:
                    extra(dve, chain)
                for n, (p, pairs, dst, add) in enumerate(jobs):
                    if n % 2 and not add:
                        continue
                    dve.wait_ge(self.product_done.sem, self.product_done.at(n + 1))
                    who = self.evac_dve if n % 2 == 0 else self.evac_act
                    if add:
                        dve.tensor_tensor(dst, dst, bank(n, dst), ALU.add).then_inc(who.sem, 1)
                    else:
                        dve.tensor_copy(dst, bank(n, dst)).then_inc(who.sem, 1)

            @block.scalar
            def _(act):
                for n, (p, pairs, dst, add) in enumerate(jobs):
                    if n % 2 == 0 or add:
                        continue
                    act.wait_ge(self.product_done.sem, self.product_done.at(n + 1))
                    act.activation(dst, bank(n, dst), ACT.Copy).then_inc(self.evac_act.sem, 1)
        run.taken += len(pieces)
        self.vec_step.over(chain.n)
        self.product_done.over(len(jobs))
        self.evac_dve.over((len(jobs) + 1) // 2)
        self.evac_act.over(len(jobs) // 2)

    def sig(self, name):
        if name not in self.named:
            self.named[name] = self.sem(name)
        return self.named[name]

    def mixer_products(self, a_cols, b_cols, c_rows):
        jobs = []
        x = self.xT

        def turned_job(p, o, m, dst):
            jobs.append((p, [(lambda w, c=c: w[:, c, o:o + m], lambda w, c=c: x[:, c, :]) for c in range(KC)], dst, False))

        for p in range(3):
            for i in range(2):
                turned_job(p, i * P, P, a_cols[:, 2 * p + i, :])
        for p in range(3):
            for i, (o, m) in enumerate(B_TILES):
                turned_job(3 + 2 * p + i // 2, o if i < 2 else 0, m, b_cols[0:m, 3 * p + i, :])
        for p, (o, m) in enumerate(C_PIECES):
            for t in range(TT):
                jobs.append((9 + p, [(lambda w, c=c, t=t: x[:, c, t * P:(t + 1) * P], lambda w, c=c: w[:, c, :])
                                     for c in range(KC)], c_rows[:, t, o:o + m], False))
        self.products(jobs)

    def add_rows(self, x, width, dst, add=True, extra=None):
        jobs = []
        for p in range(D // width):
            for t in range(TT):
                jobs.append((p, [(lambda w, c=c, t=t: x[:, c, t * P:(t + 1) * P], lambda w, c=c: w[:, c, :])
                                 for c in range(KC)], dst[:, t, p * width:(p + 1) * width], add))
        self.products(jobs, extra)

    def cols_jobs(self, x, p, n, dst, first):
        return [(p, [(lambda w, c=c, i=i: w[:, c, i * P:(i + 1) * P], lambda w, c=c: x[:, c, :]) for c in range(KC)],
                 dst[:, first + i, :], False) for i in range(n)]

    def hybrid_mixer(self, l):
        I = self.I
        self.norm_turn(self.h, f"norm_mix_g{l}", self.xT)
        with ExitStack() as ctx:
            y = self.tmp(ctx, "y", [P, TT, D])
            c_rows = self.tmp(ctx, "c_rows", [P, TT, 2 * C_W])
            with ExitStack() as inner:
                a_cols = self.tmp(inner, "a_cols", [P, 2 * A_TILES, SEQ])
                b_cols = self.tmp(inner, "b_cols", [P, 9, SEQ])
                self.mixer_products(a_cols, b_cols, c_rows)
                self.mixer_middle(l, a_cols, b_cols, c_rows, y, inner)
            self.group_norm_rows(y)
            self.norm_turn(y, f"mix_out_g{l}", self.xT, norm=False)
        self.add_rows(self.xT, 256, self.h)

    def mixer_middle(self, l, a_cols, b_cols, c_rows, y, ctx):
        I = self.I
        pad_a, pad_b = A_TAPS - 1, B_TAPS - 1
        gated = self.tmp(ctx, "gated", [P, A_TILES, pad_a + SEQ])
        conv = self.tmp(ctx, "conv", [P, A_TILES, SEQ])
        cb = self.tmp(ctx, "cb", [P, 3, pad_b + SEQ])
        conv_b = self.tmp(ctx, "conv_b", [P, 3, SEQ])
        ws = self.tmp(ctx, "ws", [P, C_GROUPS, P])
        wsT = self.tmp(ctx, "wsT", [P, C_GROUPS, P])
        gains = self.tmp(ctx, "gains", [P, 2 * A_W + 2 * C_W])
        ga, ba = gains[:, 0:A_W], gains[:, A_W:2 * A_W]
        gc, bc = gains[:, 2 * A_W:2 * A_W + C_W], gains[:, 2 * A_W + C_W:]
        stats = self.tmp(ctx, "stats", [P, 4, 6])
        mv = self.tmp(ctx, "mv", [P, 4, 2])
        rstd = self.tmp(ctx, "rstd", [P, 4])
        var = self.tmp(ctx, "var", [P, 4])
        vnorm = self.tmp(ctx, "vnorm", [P, TT, C_W])
        side, sigm, conv_ready, turned = self.side_loaded, self.sig("gate_sigmoid"), self.sig("conv_ready"), self.turned
        gelu_ready, wsT_ready, v_ready, var_ready = self.sig("gelu_ready"), self.sig("wsT_ready"), self.sig("v_ready"), self.sig("var_ready")
        mixed, affine_ready, silu_done = self.sig("gate_mixed"), self.sig("affine_ready"), self.sig("silu_done")
        ps = self.ps
        rows_a = [ps[:, t, 0:A_W] for t in range(TT)]
        rows_b = [ps[:, 2 + t, 0:B_W] for t in range(TT)]
        mix_c = [ps[:, 4 + t, 0:C_W] for t in range(TT)]
        wsT_ps = ps[:, 6:8, :]
        chain = Chain(self.nc.vector, self.vec_step)
        with self.block() as block:
            @block.sync
            def _(sp):
                sp.dma_start(ws[:], I["gmlp_ws"][l].rearrange("g i j -> i g j")).then_inc(side.sem, 16)
                for dst, name, n in ((ga, "ln_a_g", A_W), (ba, "ln_a_b", A_W), (gc, "ln_c_g", C_W), (bc, "ln_c_b", C_W)):
                    sp.dma_start(dst, I[name][l:l + 1, :].broadcast_to([P, n])).then_inc(side.sem, 16)
                self.run.load_until(sp, self.run.taken + RING)

            @block.scalar
            def _(act):
                act.activation(a_cols[:, A_TILES:, :], a_cols[:, A_TILES:, :], ACT.Sigmoid).then_inc(sigm.sem, 1)
                act.activation(c_rows[:], c_rows[:], ACT.Gelu_apprx_tanh).then_inc(gelu_ready.sem, 1)
                for t in range(TT):
                    act.wait_ge(affine_ready.sem, affine_ready.at(t + 1))
                    act.activation(y[:, t, 0:A_W], y[:, t, 0:A_W], ACT.Silu).then_inc(silu_done.sem, 1)

            @block.gpsimd
            def _(pool):
                for i in range(4):
                    pool.wait_ge(v_ready.sem, v_ready.at(i + 1))
                    pool.tensor_scalar(var[:, i:i + 1], mv[:, i, 1:2], EPS, 1.0, ALU.add, ALU.mult).then_inc(self.pool_step.sem, 1)
                    pool.wait_ge(self.pool_step.sem, self.pool_step.at(i + 1))
                    pool.tensor_tensor(rstd[:, i:i + 1], var[:, i:i + 1], self.neg_half[:, 0:1], ALU.pow).then_inc(var_ready.sem, 1)

            @block.tensor
            def _(pe):
                pe.wait_ge(side.sem, side.at(16 * 5))
                for g in range(C_GROUPS):
                    last = pe.transpose(wsT_ps[:, g // 4, (g % 4) * P:(g % 4 + 1) * P], ws[:, g, :], self.ident[:])
                last.then_inc(turned.sem, 1)
                pe.wait_ge(conv_ready.sem, conv_ready.at(1))
                for t in range(TT):
                    for i, (o, m) in enumerate(B_TILES):
                        last = pe.transpose(rows_b[t][:, o:o + m], conv_b[0:m, i, t * P:(t + 1) * P], self.ident[0:m, 0:m])
                last.then_inc(turned.sem, 1)
                pe.wait_ge(wsT_ready.sem, wsT_ready.at(1))
                for t in range(TT):
                    pe.wait_ge(self.sig("vnorm_ready").sem, self.sig("vnorm_ready").at(t + 1))
                    for g in range(C_GROUPS):
                        last = pe.matmul(mix_c[t][:, g * HEAD:(g + 1) * HEAD], wsT[:, g, :], vnorm[:, t, g * HEAD:(g + 1) * HEAD], start=True, stop=True)
                    last.then_inc(mixed.sem, 1)
                pe.wait_ge(conv_ready.sem, conv_ready.at(2))
                for t in range(TT):
                    for i in range(A_TILES):
                        last = pe.transpose(rows_a[t][:, i * P:(i + 1) * P], conv[:, i, t * P:(t + 1) * P], self.ident[:])
                last.then_inc(turned.sem, 1)

            @block.vector
            def _(dve):
                dve.memset(gated[:, :, 0:pad_a], 0.0)
                dve.memset(cb[:, :, 0:pad_b], 0.0)
                for i, (_, m) in enumerate(B_TILES):
                    chain.do(dve.tensor_tensor(cb[0:m, i, pad_b:], b_cols[0:m, 3 + i, :], b_cols[0:m, 6 + i, :], ALU.mult))
                chain.wait()
                for k in range(B_TAPS):
                    for i, (_, m) in enumerate(B_TILES):
                        w = self.col(f"conv_b{l}{i}", k)[0:m]
                        if k == 0:
                            chain.do(dve.tensor_scalar(conv_b[0:m, i, :], cb[0:m, i, 0:SEQ], w, None, ALU.mult))
                        else:
                            chain.wait(chain.n - 2)
                            chain.do(dve.scalar_tensor_tensor(conv_b[0:m, i, :], cb[0:m, i, k:k + SEQ], w, conv_b[0:m, i, :], ALU.mult, ALU.add))
                chain.wait()
                for i, (_, m) in enumerate(B_TILES):
                    last = dve.tensor_tensor(conv_b[0:m, i, :], conv_b[0:m, i, :], b_cols[0:m, i, :], ALU.mult)
                last.then_inc(conv_ready.sem, 1)
                dve.wait_ge(turned.sem, turned.at(1))
                chain.do(dve.tensor_copy(wsT[:], wsT_ps.rearrange("p a b -> p (a b)")[:, 0:C_GROUPS * P].rearrange("p (g i) -> p g i", g=C_GROUPS)))
                chain.wait()
                dve.memset(wsT[HEAD:P, :, 0:HEAD], 0.0).then_inc(wsT_ready.sem, 1)
                dve.wait_ge(side.sem, side.at(16 * 5))

                def layer_norm(i, src, dst, g, b):
                    chain.link(dve.bn_stats(stats[:, i, :], src))
                    dve.bn_aggr(mv[:, i, :], stats[:, i, :]).then_inc(v_ready.sem, 1)
                    dve.wait_ge(var_ready.sem, var_ready.at(i + 1))
                    chain.link(dve.tensor_scalar(dst, src, mv[:, i, 0:1], rstd[:, i:i + 1], ALU.subtract, ALU.mult))
                    chain.link(dve.tensor_tensor(dst, dst, g, ALU.mult))
                    return dve.tensor_tensor(dst, dst, b, ALU.add)

                dve.wait_ge(gelu_ready.sem, gelu_ready.at(1))
                for t in range(TT):
                    layer_norm(t, c_rows[:, t, C_W:], vnorm[:, t, :], gc, bc).then_inc(self.sig("vnorm_ready").sem, 1)
                dve.wait_ge(sigm.sem, sigm.at(1))
                chain.do(dve.tensor_tensor(gated[:, :, pad_a:], a_cols[:, 0:A_TILES, :], a_cols[:, A_TILES:, :], ALU.mult))
                chain.wait()
                for k in range(A_TAPS):
                    for i in range(A_TILES):
                        w = self.col(f"conv_a{l}{i}", k)
                        if k == 0:
                            chain.do(dve.tensor_scalar(conv[:, i, :], gated[:, i, 0:SEQ], w, self.col(f"conv_a_b{l}", i), ALU.mult, ALU.add))
                        else:
                            chain.wait(chain.n - A_TILES + 1)
                            ins = dve.scalar_tensor_tensor(conv[:, i, :], gated[:, i, k:k + SEQ], w, conv[:, i, :], ALU.mult, ALU.add)
                            if (k, i) == (A_TAPS - 1, A_TILES - 1):
                                ins.then_inc(conv_ready.sem, 1)
                            else:
                                chain.do(ins)
                dve.wait_ge(turned.sem, turned.at(2))
                for t in range(TT):
                    dve.tensor_copy(y[:, t, A_W:A_W + B_W], rows_b[t])
                for t in range(TT):
                    dve.wait_ge(mixed.sem, mixed.at(t + 1))
                    for g in range(C_GROUPS):
                        o = A_W + B_W + g * HEAD
                        dve.scalar_tensor_tensor(y[:, t, o:o + HEAD], mix_c[t][:, g * HEAD:(g + 1) * HEAD], self.col(f"gmlp_b{l}", g),
                                                 c_rows[:, t, g * HEAD:(g + 1) * HEAD], ALU.add, ALU.mult)
                dve.wait_ge(turned.sem, turned.at(3))
                for t in range(TT):
                    layer_norm(2 + t, rows_a[t], y[:, t, 0:A_W], ga, ba).then_inc(affine_ready.sem, 1)
        side.over(16 * 5)
        self.vec_step.over(chain.n)
        for s, n in ((sigm, 1), (gelu_ready, 1), (affine_ready, TT), (silu_done, TT), (v_ready, 4), (self.pool_step, 4), (var_ready, 4),
                     (turned, 3), (conv_ready, 2), (wsT_ready, 1), (self.sig("vnorm_ready"), TT), (mixed, TT)):
            s.over(n)

    def group_norm_rows(self, y):
        G = D // HEAD
        squared, rstd_ready = self.sig("groups_squared"), self.sig("groups_rstd")
        with ExitStack() as ctx:
            sq = self.tmp(ctx, "sq", [P, TT, D])
            s = self.tmp(ctx, "s", [P, 3, TT * G])
            with self.block() as block:
                @block.scalar
                def _(act):
                    for t in range(TT):
                        act.activation(sq[:, t, :], y[:, t, :], ACT.Square).then_inc(squared.sem, 1)

                @block.gpsimd
                def _(pool):
                    pool.wait_ge(self.vec_step.sem, self.vec_step.at(TT))
                    pool.tensor_scalar(s[:, 1, :], s[:, 0, :], 1.0 / HEAD, EPS, ALU.mult, ALU.add).then_inc(self.pool_step.sem, 1)
                    pool.wait_ge(self.pool_step.sem, self.pool_step.at(1))
                    pool.tensor_tensor(s[:, 2, :], s[:, 1, :], self.neg_half[:, 0:TT * G], ALU.pow).then_inc(rstd_ready.sem, 1)

                @block.vector
                def _(dve):
                    for t in range(TT):
                        dve.wait_ge(squared.sem, squared.at(t + 1))
                        dve.tensor_reduce(s[:, 0, t * G:(t + 1) * G], sq[:, t, :].rearrange("p (g e) -> p g e", g=G), AX_X, ALU.add).then_inc(self.vec_step.sem, 1)
                    dve.wait_ge(rstd_ready.sem, rstd_ready.at(1))
                    for t in range(TT):
                        v = y[:, t, :].rearrange("p (g e) -> p g e", g=G)
                        dve.tensor_tensor(v, v, s[:, 2, t * G:(t + 1) * G].unsqueeze(2).to_broadcast([P, G, HEAD]), ALU.mult)
        squared.over(TT)
        self.pool_step.over(1)
        rstd_ready.over(1)
        self.vec_step.over(TT)

    def attend(self, heads, o_rows, scale, qT, kT, v, bias=None, sink=None):
        with ExitStack() as ctx:
            s_sb = self.tmp(ctx, "scores", [P, 2, TT, SEQ])
            p_sb = self.tmp(ctx, "probs", [P, 2, TT, SEQ])
            pT = self.tmp(ctx, "probsT", [P, 2, TT, SEQ])
            mx = self.tmp(ctx, "mx", [P, heads, TT])
            nm = self.tmp(ctx, "nm", [P, heads, TT])
            den = self.tmp(ctx, "den", [P, heads, TT])
            rden = self.tmp(ctx, "rden", [P, heads, TT])
            es = self.tmp(ctx, "es", [P, heads, TT])
            ps = self.ps
            sc = [ps[:, b, :].rearrange("p (t m) -> p t m", t=TT) for b in range(2)]
            tp = [ps[:, 2 + b, :].rearrange("p (t m) -> p t m", t=TT) for b in range(2)]
            dh = v(0, 0).shape[1]
            op = [[ps[:, 4 + 2 * b + t, 0:dh] for t in range(TT)] for b in range(2)]
            scores, mxr, probs, turned, pT_ready, o_done, o_stored = (
                self.scores_done, self.max_ready, self.probs_ready, self.probs_turned, self.probsT_ready, self.heads_done, self.head_stored)
            chain = Chain(self.nc.vector, self.vec_step)
            per_tile = TT
            bias_used = self.sig("bias_used")
            with self.block() as block:
                @block.sync
                def _(sp):
                    if bias is not None:
                        bias.load(sp, bias_used)
                    self.run.load_until(sp, self.run.taken + RING)

                @block.tensor
                def _(pe):
                    def score(h):
                        if h >= 2:
                            if bias is None:
                                pe.wait_ge(probs.sem, probs.at(per_tile * (h - 1)))
                            else:
                                pe.wait_ge(bias_used.sem, bias_used.at(h - 1))
                        for t in range(TT):
                            pairs = list(zip(qT(h, t), kT(h)))
                            for i, (q, k) in enumerate(pairs):
                                mm = pe.matmul(sc[h % 2][:, t, :], q, k, start=(i == 0), stop=(i == len(pairs) - 1))
                        mm.then_inc(scores.sem, 1)

                    score(0)
                    for h in range(heads):
                        if h + 1 < heads:
                            score(h + 1)
                        pe.wait_ge(probs.sem, probs.at(per_tile * (h + 1)))
                        if h >= 2:
                            pe.wait_ge(pT_ready.sem, pT_ready.at(h - 1))
                        for m in range(TT):
                            for t in range(TT):
                                mm = pe.transpose(tp[h % 2][:, m, t * P:(t + 1) * P], p_sb[:, h % 2, t, m * P:(m + 1) * P], self.ident[:])
                        mm.then_inc(turned.sem, 1)
                        pe.wait_ge(pT_ready.sem, pT_ready.at(h + 1))
                        if h >= 2:
                            pe.wait_ge(o_stored.sem, o_stored.at(h - 1))
                        for t in range(TT):
                            for m in range(TT):
                                mm = pe.matmul(op[h % 2][t], pT[:, h % 2, m, t * P:(t + 1) * P], v(h, m), start=(m == 0), stop=(m == TT - 1))
                        mm.then_inc(o_done.sem, 1)

                @block.scalar
                def _(act):
                    for h in range(heads):
                        src = sc[h % 2] if bias is None else s_sb[:, h % 2]
                        act.wait_ge(mxr.sem, mxr.at(h + 1))
                        if h >= 2:
                            act.wait_ge(turned.sem, turned.at(h - 1))
                        for t in range(TT):
                            act.activation(p_sb[:, h % 2, t, :], src[:, t, :], ACT.Exp, bias=nm[:, h, t:t + 1], scale=scale if bias is None else 1.0,
                                           accum_out=den[:, h, t:t + 1]).then_inc(probs.sem, 1)
                        if sink is not None:
                            for t in range(TT):
                                act.activation(es[:, h, t:t + 1], sink(h), ACT.Exp, bias=nm[:, h, t:t + 1]).then_inc(self.sig("sink_exp").sem, 1) if sink(h) is not None else None
                        act.wait_ge(turned.sem, turned.at(h + 1))
                        if h >= 2:
                            act.wait_ge(o_done.sem, o_done.at(h - 1))
                        act.activation(pT[:, h % 2], tp[h % 2], ACT.Copy).then_inc(pT_ready.sem, 1)

                sinks = [h for h in range(heads) if sink is not None and sink(h) is not None]

                @block.vector
                def _(dve):
                    def maximum(h):
                        dve.wait_ge(scores.sem, scores.at(h + 1))
                        src = sc[h % 2]
                        if bias is not None:
                            bias.wait(dve, h)
                            if h >= 2:
                                dve.wait_ge(probs.sem, probs.at(per_tile * (h - 1)))
                            src = s_sb[:, h % 2]
                            dve.scalar_tensor_tensor(src, sc[h % 2], scale, bias.tile(h), ALU.mult, ALU.add).then_inc(bias_used.sem, 1)
                            dve.wait_ge(bias_used.sem, bias_used.at(h + 1))
                        chain.link(dve.tensor_reduce(mx[:, h, :], src, AX_X, ALU.max))
                        if h in sinks:
                            chain.link(dve.tensor_scalar(mx[:, h, :], mx[:, h, :], sink(h), None, ALU.max))
                        dve.tensor_scalar(nm[:, h, :], mx[:, h, :], -scale if bias is None else -1.0, None, ALU.mult).then_inc(mxr.sem, 1)

                    maximum(0)
                    for h in range(heads):
                        if h + 1 < heads:
                            maximum(h + 1)
                        dve.wait_ge(probs.sem, probs.at(per_tile * (h + 1)))
                        if h in sinks:
                            dve.wait_ge(self.sig("sink_exp").sem, self.sig("sink_exp").at(TT * (sinks.index(h) + 1)))
                            chain.link(dve.tensor_tensor(den[:, h, :], den[:, h, :], es[:, h, :], ALU.add))
                        chain.link(dve.reciprocal(rden[:, h, :], den[:, h, :]))
                        dve.wait_ge(o_done.sem, o_done.at(h + 1))
                        for t in range(TT):
                            last = dve.tensor_scalar(o_rows[:, t, h * dh:(h + 1) * dh], op[h % 2][t], rden[:, h, t:t + 1], None, ALU.mult)
                        last.then_inc(o_stored.sem, 1)
            if bias is not None:
                bias_used.over(heads)
            self.vec_step.over(chain.n)
            for s, n in ((scores, heads), (mxr, heads), (probs, per_tile * heads), (turned, heads), (pT_ready, heads), (o_done, heads), (o_stored, heads)):
                s.over(n)
            if sinks:
                self.sig("sink_exp").over(TT * len(sinks))

    def turn_only(self, rows, dst):
        with self.block() as block:
            @block.sync
            def _(sp):
                self.run.load_until(sp, self.run.taken + RING)

            @block.tensor
            def _(pe):
                for c in range(KC):
                    for t in range(TT):
                        last = pe.transpose(self.ps[:, c // 2, (c % 2) * SEQ + t * P:(c % 2) * SEQ + (t + 1) * P],
                                            rows[:, t, c * P:(c + 1) * P], self.ident[:])
                    last.then_inc(self.turned.sem, 1)

            @block.vector
            def _(dve):
                for b in range(0, KC // 2, 2):
                    dve.wait_ge(self.turned.sem, self.turned.at(2 * b + 2))
                    dve.tensor_copy(dst[:, 2 * b:2 * b + 2, :], self.ps[:, b, :].rearrange("p (a s) -> p a s", a=2))

            @block.scalar
            def _(act):
                for b in range(1, KC // 2, 2):
                    act.wait_ge(self.turned.sem, self.turned.at(2 * b + 2))
                    act.activation(dst[:, 2 * b:2 * b + 2, :], self.ps[:, b, :].rearrange("p (a s) -> p a s", a=2), ACT.Copy)
        self.turned.over(KC)

    def cross_attention(self, l):
        XH, XD = 4, D // 4
        with ExitStack() as ctx:
            kT = self.tmp(ctx, "kT", [P, KC, SEQ])
            v = self.tmp(ctx, "v", [P, TT, D])
            qT = self.tmp(ctx, "qT", [P, KC, SEQ])
            with ExitStack() as inner:
                mem = self.tmp(inner, "mem", [P, TT, D])
                with self.block() as block:
                    @block.sync
                    def _(sp):
                        sp.dma_start(mem[:], self.I["mem"].rearrange("a (t p) d -> p (a t) d", p=P)).then_inc(self.side_loaded.sem, 16)
                        sp.wait_ge(self.side_loaded.sem, self.side_loaded.at(16))
                self.side_loaded.over(16)
                self.norm_turn(mem, f"norm_mem_g{l}", self.xT)
                jobs = []
                for p in range(4):
                    jobs += self.cols_jobs(self.xT, p, 2, kT, 2 * p)
                self.products(jobs)
                self.add_rows(self.xT, 256, v, add=False)
            self.norm_turn(self.h, f"norm_x_g{l}", self.xT)
            jobs = []
            for p in range(4):
                jobs += self.cols_jobs(self.xT, p, 2, qT, 2 * p)
            self.products(jobs)
            o = self.tmp(ctx, "o", [P, TT, D])
            self.attend(XH, o, XD ** -0.5,
                        lambda h, t: [qT[:, 2 * h + c, t * P:(t + 1) * P] for c in range(2)],
                        lambda h: [kT[:, 2 * h + c, :] for c in range(2)],
                        lambda h, m: v[:, m, h * XD:(h + 1) * XD])
            self.turn_only(o, self.xT)
        self.add_rows(self.xT, 256, self.h)

    def ffn(self, chunks, gate, up, down, next_run, dst, add):
        s = self.mlp
        n = chunks
        pairs = (n - 2) // 2
        slots = [[self.ring[:, 2 * k + p, 0:KC * CHUNK] for p in range(2)] for k in range(3)]
        gate_w = [x.rearrange("p (c f) -> p c f", c=KC) for x in slots[0]]
        up_w = [x.rearrange("p (c f) -> p c f", c=KC) for x in slots[1]]
        down_w = [x.rearrange("p (c f) -> p c f", c=2) for x in slots[2]]
        ps = self.ps
        gb = [ps[:, p, :] for p in range(2)]
        ub = [ps[:, 2 + p, :] for p in range(2)] if up else gb
        kinds = [(0, gate, gate_w, s["gate_done"])] + ([(1, up, up_w, s["up_done"])] if up else []) + [(2, down, down_w, s["down_done"])]
        with ExitStack() as ctx:
            acted = self.tmp(ctx, "acted", [P, 2, 2 * SEQ])
            hidden = self.tmp(ctx, "hidden", [P, 2, 2, SEQ])
            with self.block() as block:
                @block.sync
                def _(sp):
                    for j in range(2):
                        for k, src, w, _ in kinds:
                            sp.dma_start(w[j], src(j)).then_inc(s["loaded"][k][j].sem, 16)

                    def load(j, p):
                        for k, src, w, done in kinds:
                            sp.wait_ge(done.sem, done.at(j - 1))
                            sp.dma_start(w[p], src(j)).then_inc(s["loaded"][k][p].sem, 16)

                    with sp.Fori(0, pairs) as i:
                        load(2 * i + 2, 0)
                        load(2 * i + 3, 1)
                    if n % 2:
                        load(n - 1, 0)
                    if next_run is not None:
                        next_run.load_until(sp, 2)
                        sp.wait_ge(s["down_done"].sem, s["down_done"].at(n))
                        next_run.load_until(sp, RING)

                @block.tensor
                def _(pe):
                    def in_part(j, p, i=0):
                        arrived = (j - p) // 2 if isinstance(j, int) else i + 1
                        if not (isinstance(j, int) and j < 2):
                            pe.wait_ge(s["hidden_ready"].sem, s["hidden_ready"].at(j - 1))
                        for k, src, w, done in kinds[:-1]:
                            pe.wait_ge(s["loaded"][k][p].sem, s["loaded"][k][p].at(16 * (arrived + 1)))
                            bank = (gb, ub)[k][p]
                            for m in range(2):
                                for c in range(KC):
                                    mm = pe.matmul(bank[:, m * SEQ:(m + 1) * SEQ], w[p][:, c, m * P:(m + 1) * P], self.xT[:, c, :],
                                                   start=(c == 0), stop=(c == KC - 1))
                            mm.then_inc(done.sem, 1)

                    def out_part(j, p, i=0, first=False, last=False):
                        arrived = (j - p) // 2 if isinstance(j, int) else (i + p if p else i + 1)
                        arrived = (j - p) // 2 if isinstance(j, int) else (i if p else i + 1)
                        pe.wait_ge(s["loaded"][2][p].sem, s["loaded"][2][p].at(16 * (arrived + 1)))
                        pe.wait_ge(s["hidden_ready"].sem, s["hidden_ready"].at(j + 1))
                        for f in range(2):
                            for t in range(TT):
                                for half in range(2):
                                    mm = pe.matmul(ps[:, 4 + 2 * t + half, :], hidden[:, p, f, t * P:(t + 1) * P],
                                                   down_w[p][:, f, half * 512:(half + 1) * 512], start=first and f == 0, stop=last and f == 1,
                                                   skip_group_check=True)
                        mm.then_inc(s["down_done"].sem, 1)

                    in_part(0, 0)
                    in_part(1, 1)
                    out_part(0, 0, first=True)
                    with pe.Fori(0, pairs) as i:
                        in_part(2 * i + 2, 0, i)
                        out_part(2 * i + 1, 1, i)
                        in_part(2 * i + 3, 1, i)
                        out_part(2 * i + 2, 0, i)
                    if n % 2:
                        in_part(n - 1, 0)
                        out_part(n - 2, 1)
                    out_part(n - 1, (n - 1) % 2, last=True)

                @block.scalar
                def _(act):
                    def activate(j, p):
                        act.wait_ge(s["gate_done"].sem, s["gate_done"].at(j + 1))
                        if not (isinstance(j, int) and j < 2):
                            act.wait_ge(s["hidden_ready"].sem, s["hidden_ready"].at(j - 1))
                        act.activation(acted[:, p, :], gb[p], ACT.Silu if up else ACT.Relu).then_inc(s["act_done"].sem, 1)

                    activate(0, 0)
                    activate(1, 1)
                    with act.Fori(0, pairs) as i:
                        activate(2 * i + 2, 0)
                        activate(2 * i + 3, 1)
                    if n % 2:
                        activate(n - 1, 0)

                @block.vector
                def _(dve):
                    def multiply(j, p):
                        dve.wait_ge(s["act_done"].sem, s["act_done"].at(j + 1))
                        if up:
                            dve.wait_ge(s["up_done"].sem, s["up_done"].at(j + 1))
                        if not (isinstance(j, int) and j < 2):
                            dve.wait_ge(s["down_done"].sem, s["down_done"].at(j - 1))
                        dve.tensor_tensor(hidden[:, p].rearrange("p f s -> p (f s)"), acted[:, p, :], ub[p], ALU.mult).then_inc(s["hidden_ready"].sem, 1)

                    multiply(0, 0)
                    multiply(1, 1)
                    with dve.Fori(0, pairs) as i:
                        multiply(2 * i + 2, 0)
                        multiply(2 * i + 3, 1)
                    if n % 2:
                        multiply(n - 1, 0)
                    dve.wait_ge(s["down_done"].sem, s["down_done"].at(n))
                    for t in range(TT):
                        for half in range(2):
                            d = dst[:, t, half * 512:(half + 1) * 512]
                            if add:
                                dve.tensor_tensor(d, d, ps[:, 4 + 2 * t + half, :], ALU.add)
                            else:
                                dve.tensor_copy(d, ps[:, 4 + 2 * t + half, :])
        for k in range(3):
            if k == 1 and not up:
                continue
            s["loaded"][k][0].over(16 * ((n + 1) // 2))
            s["loaded"][k][1].over(16 * (n // 2))
        for name in ("gate_done", "down_done", "act_done", "hidden_ready") + (("up_done",) if up else ()):
            s[name].over(n)
        if next_run is not None:
            self.run = next_run

    def store_rows(self, src):
        with self.block() as block:
            @block.sync
            def _(sp):
                sp.dma_start(self.out.rearrange("a (t p) d -> p (a t) d", p=P), src[:]).then_inc(self.out_stored.sem, 16)
                sp.wait_ge(self.out_stored.sem, self.out_stored.at(16))

    def layer_pieces(self, l):
        I = self.I
        w = I["w_in"][l]
        pieces = by_cols(w[:, 0:2 * A_W], 256)
        for o in range(2 * A_W, 2 * A_W + 3 * B_W, B_W):
            pieces += by_cols(w[:, o:o + 192], 192) + by_cols(w[:, o + 192:o + B_W], 128)
        for o, m in C_PIECES:
            pieces += by_cols(w[:, 2 * A_W + 3 * B_W + o:2 * A_W + 3 * B_W + o + m], m)
        pieces += by_cols(I["w_mix_out"][l], 256) + by_cols(I["w_xkv"][l], 256)
        return pieces + by_cols(I["w_xq"][l], 256) + by_cols(I["w_xo"][l], 256)

    def ffn_sources(self, gate, up, down):
        def cols(w):
            v = w.rearrange("(c p) f -> p c f", p=P)
            return lambda j: v[:, :, bass.ds(j * CHUNK, CHUNK)]
        d = down.rearrange("(c p) n -> p c n", p=P)
        return cols(gate), cols(up) if up is not None else None, lambda j: d[:, bass.ds(j * 2, 2), :]

    def experts(self, next_run):
        I, ps = self.I, self.ps
        V, K, E = VIRTUAL, MAX_ITEMS, N_EXPERTS
        with ExitStack() as ctx:
            rows = self.tmp(ctx, "rows", [P, TT, D])
            self.norm_turn(self.h, "norm_ffn_g1", self.xT, keep_rows=rows)
            table = self.tmp(ctx, "table", [P, TT, V, 2])
            items_e = self.tmp(ctx, "items_e", [1, K], I32)
            items_v = self.tmp(ctx, "items_v", [1, K], I32)
            n_items = self.tmp(ctx, "n_items", [1, 1], I32)
            slot_no = self.tmp(ctx, "slot_no", [P, SLOTS])
            with ExitStack() as inner:
                self.route(inner, table, items_e, items_v, n_items, slot_no)
            self.expert_items(ctx, rows, table, items_e, items_v, n_items, slot_no, next_run)
        self.run = next_run

    def route(self, ctx, table, items_e, items_v, n_items, slot_no):
        I, ps = self.I, self.ps
        V, K, E = VIRTUAL, MAX_ITEMS, N_EXPERTS
        tmp = self.tmp
        router = tmp(ctx, "router", [P, KC, E])
        before = tmp(ctx, "before", [P, P])
        v_no = tmp(ctx, "v_no", [1, V])
        e_no = tmp(ctx, "e_no", [1, V])
        k_no = tmp(ctx, "k_no", [1, K, V])
        logits = tmp(ctx, "logits", [P, TT, E])
        top = tmp(ctx, "top", [P, TT, E])
        top_i = tmp(ctx, "top_i", [P, TT, E], U32)
        top_f = tmp(ctx, "top_f", [P, TT, 2])
        first, second, chosen, wts, rank = (tmp(ctx, n, [P, TT, E]) for n in ("first", "second", "chosen", "wts", "rank"))
        gap, ex, den, w1, w2 = (tmp(ctx, n, [P, TT, 1]) for n in ("gap", "ex", "den", "w1", "w2"))
        count = tmp(ctx, "count", [1, E])
        active, upto, key = (tmp(ctx, n, [1, V]) for n in ("active", "upto", "key"))
        match, pickv = (tmp(ctx, n, [1, K, V]) for n in ("match", "pickv"))
        found = tmp(ctx, "found", [1, 2, K])
        logits_done, gap_ready, exp_ready, chosen_ready, ranks_done = (
            self.sig(n) for n in ("logits_done", "gap_ready", "exp_ready", "chosen_ready", "ranks_done"))
        chain = Chain(self.nc.vector, self.vec_step)
        with self.block() as block:
            @block.sync
            def _(sp):
                sp.dma_start(router[:], I["moe_router"][0].rearrange("(c p) e -> p c e", p=P)).then_inc(self.side_loaded.sem, 16)

            @block.gpsimd
            def _(pool):
                pool.iota(slot_no[:], [[1, SLOTS]], base=0, channel_multiplier=0, allow_small_or_imprecise_dtypes=True)
                pool.iota(v_no[:], [[1, V]], base=0, channel_multiplier=0, allow_small_or_imprecise_dtypes=True)
                pool.iota(e_no[:], [[0, MAX_TILES], [1, E]], base=0, channel_multiplier=0, allow_small_or_imprecise_dtypes=True)
                pool.iota(k_no[:], [[1, K], [0, V]], base=0, channel_multiplier=0, allow_small_or_imprecise_dtypes=True)
                pool.affine_select(out=before[:], in_=self.ones[:], compare_op=ALU.is_gt, fill=0.0, base=0,
                                   pattern=[[1, P]], channel_multiplier=-1).then_inc(self.pool_done.sem, 1)

            @block.tensor
            def _(pe):
                pe.wait_ge(self.side_loaded.sem, self.side_loaded.at(16))
                for t in range(TT):
                    for c in range(KC):
                        mm = pe.matmul(ps[:, t, 0:E], self.xT[:, c, t * P:(t + 1) * P], router[:, c, :], start=(c == 0), stop=(c == KC - 1))
                mm.then_inc(logits_done.sem, 1)
                pe.wait_ge(chosen_ready.sem, chosen_ready.at(1))
                pe.wait_ge(self.pool_done.sem, self.pool_done.at(1))
                pe.matmul(ps[:, 2, 0:E], before[:], chosen[:, 0, :], start=True, stop=True)
                pe.matmul(ps[:, 3, 0:E], before[:], chosen[:, 1, :], start=True, stop=False)
                pe.matmul(ps[:, 3, 0:E], self.ones[:], chosen[:, 0, :], start=False, stop=True)
                pe.matmul(ps[0:1, 4, 0:E], self.ones[:, 0:1], chosen[:, 0, :], start=True, stop=False)
                pe.matmul(ps[0:1, 4, 0:E], self.ones[:, 0:1], chosen[:, 1, :], start=False, stop=True).then_inc(ranks_done.sem, 1)

            @block.scalar
            def _(act):
                act.wait_ge(gap_ready.sem, gap_ready.at(1))
                act.activation(ex[:], gap[:], ACT.Exp).then_inc(exp_ready.sem, 1)

            @block.vector
            def _(dve):
                tt, ts, stt, link = dve.tensor_tensor, dve.tensor_scalar, dve.scalar_tensor_tensor, chain.link
                dve.wait_ge(logits_done.sem, logits_done.at(1))
                for t in range(TT):
                    chain.do(dve.tensor_copy(logits[:, t, :], ps[:, t, 0:E]))
                chain.wait()
                for t in range(TT):
                    link(dve.max(top[:, t, :], logits[:, t, :]))
                    link(dve.max_index(top_i[:, t, :], top[:, t, :], logits[:, t, :]))
                link(dve.tensor_copy(top_f[:], top_i[:, :, 0:2]))
                tt(gap[:], top[:, :, 1:2], top[:, :, 0:1], ALU.subtract).then_inc(gap_ready.sem, 1)
                dve.wait_ge(self.pool_done.sem, self.pool_done.at(1))
                for t in range(TT):
                    chain.do(ts(first[:, t, :], slot_no[:, 0:E], top_f[:, t, 0:1], None, ALU.is_equal))
                    chain.do(ts(second[:, t, :], slot_no[:, 0:E], top_f[:, t, 1:2], None, ALU.is_equal))
                chain.wait()
                tt(chosen[:], first[:], second[:], ALU.add).then_inc(chosen_ready.sem, 1)
                dve.wait_ge(exp_ready.sem, exp_ready.at(1))
                link(ts(den[:], ex[:], 1.0, None, ALU.add))
                link(dve.reciprocal(w1[:], den[:]))
                link(tt(w2[:], ex[:], w1[:], ALU.mult))
                for t in range(TT):
                    chain.do(ts(wts[:, t, :], first[:, t, :], w1[:, t], None, ALU.mult))
                chain.wait()
                for t in range(TT):
                    chain.do(stt(wts[:, t, :], second[:, t, :], w2[:, t], wts[:, t, :], ALU.mult, ALU.add))
                dve.wait_ge(ranks_done.sem, ranks_done.at(1))
                for t in range(TT):
                    chain.do(stt(rank[:, t, :], ps[:, 2 + t, 0:E], 1.0, chosen[:, t, :], ALU.add, ALU.mult))
                chain.do(dve.tensor_copy(count[:], ps[0:1, 4, 0:E]))
                chain.wait()
                for k in range(MAX_TILES):
                    chain.do(ts(table[:, :, k * E:(k + 1) * E, 0], rank[:], -1.0 - SLOTS * k, None, ALU.add))
                    chain.do(dve.tensor_copy(table[:, :, k * E:(k + 1) * E, 1], wts[:]))
                    chain.do(ts(active[:, k * E:(k + 1) * E], count[:], float(SLOTS * k) if k else -1.0, None, ALU.is_gt))
                chain.wait()
                link(dve.tensor_tensor_scan(upto[:], self.ones[0:1, 0:V], active[:], 0.0, ALU.mult, ALU.add))
                link(tt(key[:], upto[:], active[:], ALU.mult))
                link(ts(key[:], key[:], -1.0, None, ALU.add))
                link(tt(match[:], key[:].unsqueeze(1).to_broadcast([1, K, V]), k_no[:], ALU.is_equal))
                for n, no in enumerate((e_no, v_no)):
                    link(tt(pickv[:], match[:], no[:].unsqueeze(1).to_broadcast([1, K, V]), ALU.mult))
                    link(dve.tensor_reduce(found[:, n, :], pickv[:], AX_X, ALU.add))
                chain.do(dve.tensor_copy(items_e[:], found[:, 0, :]))
                chain.do(dve.tensor_copy(items_v[:], found[:, 1, :]))
                chain.do(dve.tensor_copy(n_items[:], upto[:, V - 1:V]))
        self.side_loaded.over(16)
        self.pool_done.over(1)
        self.vec_step.over(chain.n)
        for s in (logits_done, gap_ready, exp_ready, chosen_ready, ranks_done):
            s.over(1)

    def expert_items(self, ctx, rows, table, items_e, items_v, n_items, slot_no, next_run):
        I, ps, s = self.I, self.ps, self.moe
        K, V, E = MAX_ITEMS, VIRTUAL, N_EXPERTS
        n = I["moe_w_gate"].shape[3] // CHUNK
        assert n % 2 == 0
        per, pairs = n // 2, (n - 2) // 2
        tmp = self.tmp
        cur = tmp(ctx, "cur", [P, TT, 1, 2])
        pick = tmp(ctx, "pick", [P, TT, SLOTS])
        pick_w = tmp(ctx, "pick_w", [P, TT, SLOTS])
        pickT = tmp(ctx, "pickT", [SLOTS, TT, P])
        xg = tmp(ctx, "xg", [P, KC, SLOTS])
        acted = tmp(ctx, "acted", [P, 2, 2 * SLOTS])
        hidden = tmp(ctx, "hidden", [P, 2, 2, SLOTS])
        y = tmp(ctx, "y", [SLOTS, D])
        slots = [[self.ring[:, 2 * k + p, 0:KC * CHUNK] for p in range(2)] for k in range(3)]
        w_in = [[x.rearrange("p (c f) -> p c f", c=KC) for x in slots[k]] for k in range(2)]
        w_out = [x.rearrange("p (c f) -> p c f", c=2) for x in slots[2]]
        gate_v = I["moe_w_gate"][0].rearrange("e (c p) f -> e p c f", p=P)
        up_v = I["moe_w_up"][0].rearrange("e (c p) f -> e p c f", p=P)
        down_v = I["moe_w_down"][0].rearrange("e (c p) n -> e p c n", p=P)
        gb = [ps[:, p, 0:2 * SLOTS] for p in range(2)]
        ub = [ps[:, 2 + p, 0:2 * SLOTS] for p in range(2)]
        yb = [ps[0:SLOTS, 4 + half, :] for half in range(2)]
        xb = [ps[:, 4 + b, 0:4 * SLOTS].rearrange("p (c s) -> p c s", c=4) for b in range(2)]
        tb = ps[0:SLOTS, 6, 0:TT * P].rearrange("p (t s) -> p t s", t=TT)
        gate_done, up_done, down_done, act_done, hidden_ready = (s[k] for k in ("gate_done", "up_done", "down_done", "act_done", "hidden_ready"))
        loaded = s["loaded"]
        FREE, ADDS = 2, 2 * TT
        chain = Chain(self.nc.vector, self.sig("moe_vec_step"))
        DVE_STEPS = 1

        def items(eng):
            return eng.value_load(n_items[0:1, 0:1], min_val=1, max_val=K)

        with self.block() as block:
            @block.sync
            def _(sp):
                with sp.Fori(0, items(sp)) as i:
                    e = sp.value_load(items_e[0:1, bass.ds(i, 1)], min_val=0, max_val=E - 1)
                    with sp.Fori(0, per) as q:
                        for p in range(2):
                            j = i * n + q * 2 + p
                            f = bass.ds(q * (2 * CHUNK) + p * CHUNK, CHUNK)
                            sp.wait_ge(gate_done.sem, j + 1)
                            sp.dma_start(w_in[0][p], gate_v[bass.ds(e, 1), :, :, f].rearrange("a p c f -> p (a c) f")).then_inc(loaded[0][p].sem, 16)
                            sp.wait_ge(up_done.sem, j + 1)
                            sp.dma_start(w_in[1][p], up_v[bass.ds(e, 1), :, :, f].rearrange("a p c f -> p (a c) f")).then_inc(loaded[1][p].sem, 16)
                            sp.wait_ge(down_done.sem, j + 1)
                            sp.dma_start(w_out[p], down_v[bass.ds(e, 1), :, bass.ds(q * 4 + p * 2, 2), :].rearrange("a p c f -> p (a c) f")).then_inc(loaded[2][p].sem, 16)

            @block.tensor
            def _(pe):
                for sg in (gate_done, up_done, down_done):
                    pe.sem_inc(sg.sem, FREE)
                with pe.Fori(0, items(pe)) as i:
                    pe.wait_ge(self.pick_ready.sem, i + 1)
                    for b in range(2):
                        for c in range(4):
                            for t in range(TT):
                                mm = pe.matmul(xb[b][:, c, :], rows[:, t, (4 * b + c) * P:(4 * b + c + 1) * P], pick[:, t, :],
                                               start=(t == 0), stop=(t == TT - 1))
                        mm.then_inc(self.gathered.sem, 1)
                    for t in range(TT):
                        mm = pe.transpose(tb[:, t, :], pick_w[:, t, :], self.ident[:])
                    mm.then_inc(self.pick_turned.sem, 1)
                    pe.wait_ge(self.xg_ready.sem, i * 2 + 2)
                    pe.wait_ge(self.added.sem, i * ADDS + ADDS)

                    def in_part(j, p, pair):
                        pe.wait_ge(hidden_ready.sem, j + (FREE - 1))
                        for k, bank, done in ((0, gb, gate_done), (1, ub, up_done)):
                            pe.wait_ge(loaded[k][p].sem, pair * 16 + 16)
                            for m in range(2):
                                for c in range(KC):
                                    mm = pe.matmul(bank[p][:, m * SLOTS:(m + 1) * SLOTS], w_in[k][p][:, c, m * P:(m + 1) * P], xg[:, c, :],
                                                   start=(c == 0), stop=(c == KC - 1))
                            mm.then_inc(done.sem, 1)

                    def out_part(j, p, pair, first=False, last=False):
                        pe.wait_ge(loaded[2][p].sem, pair * 16 + 16)
                        pe.wait_ge(hidden_ready.sem, j + (1 + FREE))
                        for f in range(2):
                            for half in range(2):
                                mm = pe.matmul(yb[half], hidden[:, p, f, :], w_out[p][:, f, half * 512:(half + 1) * 512],
                                               start=first and f == 0, stop=last and f == 1, skip_group_check=True)
                        mm.then_inc(down_done.sem, 1)

                    J, Q = i * n, i * per
                    in_part(J, 0, Q)
                    in_part(J + 1, 1, Q)
                    out_part(J, 0, Q, first=True)
                    with pe.Fori(0, pairs) as r:
                        j, q = i * n + r * 2, i * per + r
                        in_part(j + 2, 0, q + 1)
                        out_part(j + 1, 1, q)
                        in_part(j + 3, 1, q + 1)
                        out_part(j + 2, 0, q + 1)
                    out_part(J + (n - 1), 1, Q + (per - 1), last=True)
                    pe.wait_ge(self.y_copied.sem, i * 2 + 2)
                    pe.wait_ge(self.pickT_ready.sem, i + 1)
                    for t in range(TT):
                        for half in range(2):
                            pe.matmul(ps[:, 2 * t + half, :], pickT[:, t, :], y[:, half * 512:(half + 1) * 512],
                                      start=True, stop=True).then_inc(self.combined.sem, 1)

            @block.scalar
            def _(act):
                with act.Fori(0, items(act)) as i:
                    act.wait_ge(self.gathered.sem, i * 2 + 2)
                    for c in range(4):
                        mm = act.activation(xg[:, 4 + c, :], xb[1][:, c, :], ACT.Copy, scale=self.col("norm_ffn_g1", 4 + c))
                    mm.then_inc(self.xg_ready.sem, 1)
                    with act.Fori(0, per) as r:
                        for p in range(2):
                            j = i * n + r * 2 + p
                            act.wait_ge(gate_done.sem, j + (1 + FREE))
                            act.wait_ge(hidden_ready.sem, j + (FREE - 1))
                            act.activation(acted[:, p, :], gb[p], ACT.Silu).then_inc(act_done.sem, 1)
                    act.wait_ge(down_done.sem, i * n + (n + FREE))
                    act.activation(y[:, 512:D], yb[1], ACT.Copy).then_inc(self.y_copied.sem, 1)

            @block.vector
            def _(dve):
                dve.sem_inc(hidden_ready.sem, FREE)
                dve.sem_inc(self.added.sem, ADDS)
                step = self.sig("moe_vec_step").sem
                with dve.Fori(0, items(dve)) as i:
                    v = dve.value_load(items_v[0:1, bass.ds(i, 1)], min_val=0, max_val=V - 1)
                    dve.tensor_copy(cur[:], table[:, :, bass.ds(v, 1), :]).then_inc(step, DVE_STEPS)
                    dve.wait_ge(step, i * DVE_STEPS + DVE_STEPS)
                    for t in range(TT):
                        dve.tensor_scalar(pick[:, t, :], slot_no[:], cur[:, t, 0, 0:1], None, ALU.is_equal)
                        mm = dve.tensor_scalar(pick_w[:, t, :], slot_no[:], cur[:, t, 0, 0:1], cur[:, t, 0, 1:2], ALU.is_equal, ALU.mult)
                    mm.then_inc(self.pick_ready.sem, 1)
                    dve.wait_ge(self.gathered.sem, i * 2 + 1)
                    for c in range(4):
                        mm = dve.tensor_scalar(xg[:, c, :], xb[0][:, c, :], self.col("norm_ffn_g1", c), None, ALU.mult)
                    mm.then_inc(self.xg_ready.sem, 1)
                    dve.wait_ge(self.pick_turned.sem, i + 1)
                    dve.tensor_copy(pickT[:], tb).then_inc(self.pickT_ready.sem, 1)
                    with dve.Fori(0, per) as r:
                        for p in range(2):
                            j = i * n + r * 2 + p
                            dve.wait_ge(act_done.sem, j + 1)
                            dve.wait_ge(up_done.sem, j + (1 + FREE))
                            dve.wait_ge(down_done.sem, j + (FREE - 1))
                            dve.tensor_tensor(hidden[:, p].rearrange("p f s -> p (f s)"), acted[:, p, :], ub[p], ALU.mult).then_inc(hidden_ready.sem, 1)
                    dve.wait_ge(down_done.sem, i * n + (n + FREE))
                    dve.tensor_copy(y[:, 0:512], yb[0]).then_inc(self.y_copied.sem, 1)
                    for t in range(TT):
                        for half in range(2):
                            dve.wait_ge(self.combined.sem, i * ADDS + (2 * t + half + 1))
                            d = self.h[:, t, half * 512:(half + 1) * 512]
                            dve.tensor_tensor(d, d, ps[:, 2 * t + half, :], ALU.add).then_inc(self.added.sem, 1)
        if next_run is not None:
            self.run = next_run
            with self.block() as block:
                @block.sync
                def _(sp):
                    next_run.load_until(sp, RING)

    def rms_rows(self, src, gain, dst, add):
        with ExitStack() as ctx:
            junk = self.tmp(ctx, "junk", [P, D])
            g = self.tmp(ctx, "g", [P, D])
            normed = self.tmp(ctx, "normed", [P, TT, D])
            stat = self.tmp(ctx, "stat", [P, 3, TT])
            with self.block() as block:
                @block.sync
                def _(sp):
                    sp.dma_start(g[:], gain.broadcast_to([P, D])).then_inc(self.side_loaded.sem, 16)
                    self.run.load_until(sp, self.run.taken + RING)

                @block.scalar
                def _(act):
                    for t in range(TT):
                        if t:
                            act.wait_ge(self.squares_summed.sem, self.squares_summed.at(t))
                        act.activation(junk[:], src[:, t, :], ACT.Square, accum_out=stat[:, 0, t:t + 1]).then_inc(self.squares_summed.sem, 1)

                @block.gpsimd
                def _(pool):
                    pool.wait_ge(self.squares_summed.sem, self.squares_summed.at(TT))
                    pool.tensor_scalar(stat[:, 1, :], stat[:, 0, :], 1.0 / D, EPS, ALU.mult, ALU.add).then_inc(self.pool_step.sem, 1)
                    pool.wait_ge(self.pool_step.sem, self.pool_step.at(1))
                    pool.tensor_tensor(stat[:, 2, :], stat[:, 1, :], self.neg_half[:, 0:TT], ALU.pow).then_inc(self.rstd_ready.sem, 1)

                @block.vector
                def _(dve):
                    dve.wait_ge(self.side_loaded.sem, self.side_loaded.at(16))
                    dve.wait_ge(self.rstd_ready.sem, self.rstd_ready.at(1))
                    for t in range(TT):
                        d = normed[:, t, :] if add else dst[:, t, :]
                        dve.scalar_tensor_tensor(d, src[:, t, :], stat[:, 2, t:t + 1], g[:], ALU.mult, ALU.mult).then_inc(self.vec_step.sem, 1)
                    if add:
                        for t in range(TT):
                            dve.wait_ge(self.vec_step.sem, self.vec_step.at(t + 1))
                            dve.tensor_tensor(dst[:, t, :], dst[:, t, :], normed[:, t, :], ALU.add)
        self.side_loaded.over(16)
        self.squares_summed.over(TT)
        self.pool_step.over(1)
        self.rstd_ready.over(1)
        self.vec_step.over(TT)

    def bias_rows(self):
        I, ps = self.I, self.ps
        H = 16
        self.bias_line = self.nc.dram_tensor("bias_line", [H, DIST], F32)
        self.bias_many = self.nc.dram_tensor("bias_many", [H, P, DIST], F32)
        done, written = self.sig("bias_made"), self.sig("bias_written")
        with ExitStack() as ctx:
            table = self.tmp(ctx, "table", [32, H])
            of_bucket = self.tmp(ctx, "of_bucket", [32, DIST])
            mask = self.tmp(ctx, "mask", [H, DIST])
            line = self.tmp(ctx, "line", [H, DIST])
            with self.block() as block:
                @block.sync
                def _(sp):
                    sp.dma_start(table[:], I["rel_table_2"]).then_inc(self.side_loaded.sem, 16)
                    sp.dma_start(of_bucket[:], I["bucket_of_distance"]).then_inc(self.side_loaded.sem, 16)
                    sp.dma_start(mask[:], I["distance_mask"]).then_inc(self.side_loaded.sem, 16)
                    sp.wait_ge(done.sem, done.at(2))
                    sp.dma_start(self.bias_line.ap(), line[:]).then_inc(written.sem, 16)
                    sp.wait_ge(written.sem, written.at(16))
                    sp.dma_start(self.bias_many.ap(), self.bias_line.ap().unsqueeze(1).to_broadcast([H, P, DIST])).then_inc(written.sem, 16)

                @block.tensor
                def _(pe):
                    pe.wait_ge(self.side_loaded.sem, self.side_loaded.at(48))
                    pe.matmul(ps[0:H, 0, :], table[:], of_bucket[:], start=True, stop=True).then_inc(done.sem, 1)

                @block.vector
                def _(dve):
                    dve.wait_ge(done.sem, done.at(1))
                    dve.tensor_tensor(line[:], ps[0:H, 0, :], mask[:], ALU.add).then_inc(done.sem, 1)
        self.side_loaded.over(48)
        done.over(2)
        written.over(32)

    def attention_mixer(self, u):
        I = self.I
        HA, HB = 8, 8
        with ExitStack() as ctx:
            qa, ka, qb = (self.tmp(ctx, n, [P, 4, SEQ]) for n in ("qa", "ka", "qb"))
            kb = self.tmp(ctx, "kb", [P, 2, SEQ])
            va = self.tmp(ctx, "va", [P, TT, HA * HEAD])
            vb = self.tmp(ctx, "vb", [P, TT, 2 * HEAD])
            sinks = self.tmp(ctx, "sinks", [P, HB])
            with ExitStack() as inner:
                swapped = self.tmp(inner, "swapped", [P, KC, 2 * HEAD])
                w_kb = I["attn_w_in_2"][0].rearrange("(c p) n -> p c n", p=P)
                with self.block() as block:
                    @block.sync
                    def _(sp):
                        k0 = 2048
                        sp.dma_start(swapped[:, :, 0:HEAD], w_kb[:, :, k0 + HEAD:k0 + 2 * HEAD]).then_inc(self.side_loaded.sem, 16)
                        sp.dma_start(swapped[:, :, HEAD:], w_kb[:, :, k0:k0 + HEAD]).then_inc(self.side_loaded.sem, 16)
                        sp.dma_start(sinks[:], I["attn_sink_2"].broadcast_to([P, HB])).then_inc(self.side_loaded.sem, 16)
                        sp.wait_ge(self.side_loaded.sem, self.side_loaded.at(48))
                        sp.wait_ge(self.sig("bias_written").sem, self.sig("bias_written").at(0))
                self.side_loaded.over(48)
                self.norm_turn(self.h, "norm2_00", self.xT)
                x = self.xT
                jobs = []
                for dst, p0 in ((qa, 0), (ka, 2)):
                    for p in range(2):
                        jobs += self.cols_jobs(x, p0 + p, 2, dst, 2 * p)
                for p in range(2):
                    for t in range(TT):
                        jobs.append((4 + p, [(lambda w, c=c, t=t: x[:, c, t * P:(t + 1) * P], lambda w, c=c: w[:, c, :]) for c in range(KC)],
                                     va[:, t, p * 256:(p + 1) * 256], False))
                for p in range(2):
                    jobs += self.cols_jobs(x, 6 + p, 2, qb, 2 * p)
                jobs += self.cols_jobs(x, 8, 1, kb, 0)
                jobs.append((8, [(lambda w, c=c: swapped[:, c, :], lambda w, c=c: x[:, c, :]) for c in range(KC)], kb[:, 1, :], False))
                for t in range(TT):
                    jobs.append((8, [(lambda w, c=c, t=t: x[:, c, t * P:(t + 1) * P], lambda w, c=c: w[:, c, 2 * HEAD:4 * HEAD]) for c in range(KC)],
                                 vb[:, t, :], False))
                self.products(jobs)

            def half(h):
                return slice((h % 2) * HEAD, (h % 2 + 1) * HEAD)

            def q_of(h, t):
                src, n = (qa, h) if h < HA else (qb, h - HA)
                return [src[half(n), n // 2, t * P:(t + 1) * P]]

            def k_of(h):
                if h < HA:
                    return [ka[half(h), h // 2, :]]
                n = h - HA
                return [kb[half(n), 0 if n % 2 == n // 4 else 1, :]]

            def v_of(h, m):
                if h < HA:
                    return va[:, m, h * HEAD:(h + 1) * HEAD]
                g = (h - HA) // 4
                return vb[:, m, g * HEAD:(g + 1) * HEAD]

            o = self.tmp(ctx, "o", [P, TT, D])
            bias = Bias(self, self.tmp(ctx, "bias", [P, 4, TT, SEQ]), HA + HB)
            self.attend(HA + HB, o, HEAD ** -0.5, q_of, k_of, v_of, bias=bias,
                        sink=lambda h: None if h < HA else sinks[:, h - HA:h - HA + 1])
            bias.over()
            self.turn_only(o, self.xT)
        self.add_rows(self.xT, 256, u, add=False)

    def second_mlp(self, l, next_run, u):
        I = self.I
        self.norm_turn(self.h, f"norm2_{l}2", self.xT)
        g, _, d = self.ffn_sources(I["mlp_w1_2"][l], None, I["mlp_w2_2"][l])
        self.ffn(I["mlp_w1_2"].shape[2] // CHUNK, g, None, d, next_run, u, False)
        self.rms_rows(u, I["norm_g_2"][l, 3:4, :], self.h, True)


class Bias:

    def __init__(self, model, ring, heads):
        self.m, self.ring, self.heads = model, ring, heads
        self.loaded = [model.sig(f"bias_loaded{i}") for i in range(4)]

    def load(self, sp, used):
        for h in range(self.heads):
            if h >= 4:
                sp.wait_ge(used.sem, used.at(h - 3))
            for t in range(TT):
                src = bass.AP(self.m.bias_many.ap().tensor, h * P * DIST + (SEQ - 1) - t * P, [[DIST - 1, P], [1, SEQ]])
                sp.dma_start(self.ring[:, h % 4, t, :], src).then_inc(self.loaded[h % 4].sem, 16)

    def wait(self, eng, h):
        s = self.loaded[h % 4]
        eng.wait_ge(s.sem, s.at(16 * TT * (h // 4 + 1)))

    def tile(self, h):
        return self.ring[:, h % 4]

    def over(self):
        for s in self.loaded:
            s.over(16 * TT * self.heads // 4)


def t5_constants():
    dist = np.arange(DIST) - (SEQ - 1)
    half, exact = 16, 8
    n = np.abs(dist)
    large = exact + (np.log(np.maximum(n, 1).astype(np.float32) / np.float32(exact)) / np.float32(np.log(1024 / exact)) * (half - exact)).astype(np.int32)
    bucket = np.where(dist > 0, half, 0) + np.where(n < exact, n, np.minimum(large, half - 1))
    one_hot = (np.arange(32)[:, None] == bucket[None, :]).astype(np.float32)
    branches = (n <= 64).astype(int) + (dist % 4 == 0) + (dist % 16 == 0)
    a = np.where(branches > 0, np.log(np.maximum(branches, 1)), -1e30)
    b = np.where(n <= 128, 0.0, -1e30)
    return one_hot, np.concatenate([np.tile(a, (8, 1)), np.tile(b, (8, 1))]).astype(np.float32)


KAPPA = float(np.exp(-0.5))
LEVELS = 7


def rwkv_constants():
    r, c = np.arange(P)[:, None], np.arange(P)[None, :]
    keep = []
    for strict, incl in ((c > r, c >= r), (c < r, c <= r)):
        keep.append(np.concatenate([-1.0 * strict, 1.0 * incl, 1.0 * strict, 1.0 * incl], axis=1))
    level = []
    for k in range(LEVELS):
        b = 1 << k
        level.append((r // (2 * b) == c // (2 * b)) & (r // b == c // b + 1))
    level += [m.T for m in level]
    pair = (r // HEAD == c // HEAD)
    return (np.stack(keep).astype(np.float32), np.stack(level).astype(np.int32),
            pair.astype(np.float32))


class Rwkv:

    def __init__(self, model):
        self.m = model

    def run(self, u):
        m = self.m
        I, nc = m.I, m.nc
        with ExitStack() as ctx:
            tmp = m.tmp
            r, k = tmp(ctx, "r", [P, KC, SEQ]), tmp(ctx, "k", [P, KC, SEQ])
            v, y = tmp(ctx, "v", [P, TT, D]), u
            g_low = tmp(ctx, "g_low", [P, 2, SEQ])
            m.norm_turn(m.h, "norm2_10", m.xT)
            with ExitStack() as inner:
                dp, dn = tmp(inner, "dp", [P, KC, SEQ]), tmp(inner, "dn", [P, KC, SEQ])
                mixed = [tmp(inner, f"mixed{i}", [P, KC, SEQ]) for i in range(2)]
                w1, a1 = tmp(inner, "w1", [P, KC, 2, HEAD]), tmp(inner, "a1", [P, KC, 2, HEAD])
                g1 = tmp(inner, "g1", [P, KC, 2, P])
                w2, a2 = tmp(inner, "w2", [P, D]), tmp(inner, "a2", [P, D])
                w_low, a_low = tmp(inner, "w_low", [P, SEQ]), tmp(inner, "a_low", [P, SEQ])
                side = m.side_loaded
                x = m.xT
                with m.block() as block:
                    @block.sync
                    def _(sp):
                        for d in range(2):
                            for dst, name in ((w1, "rk_w1_2"), (a1, "rk_a1_2"), (g1, "rk_g1_2")):
                                sp.dma_start(dst[:, :, d, :], I[name][0, d].rearrange("(c p) l -> p c l", p=P)).then_inc(side.sem, 16)
                        for dst, name in ((w2, "rk_w2_2"), (a2, "rk_a2_2")):
                            sp.dma_start(dst[:], I[name][0].rearrange("d l n -> (d l) n")).then_inc(side.sem, 16)
                        sp.wait_ge(side.sem, side.at(16 * 8))

                    @block.vector
                    def _(dve):
                        dve.tensor_tensor(dp[:, :, 1:SEQ], x[:, :, 0:SEQ - 1], x[:, :, 1:SEQ], ALU.subtract)
                        dve.tensor_tensor(dn[:, :, 0:SEQ - 1], x[:, :, 1:SEQ], x[:, :, 0:SEQ - 1], ALU.subtract)
                        dve.tensor_scalar(dp[:, :, 0:1], x[:, :, 0:1], -1.0, None, ALU.mult)
                        dve.tensor_scalar(dn[:, :, SEQ - 1:SEQ], x[:, :, SEQ - 1:SEQ], -1.0, None, ALU.mult)
                side.over(16 * 8)

                def mixing(n, dst):
                    def steps(dve, chain):
                        for c in range(KC):
                            chain.do(dve.scalar_tensor_tensor(dst[:, c, :], dp[:, c, :], m.col(f"mu_prev{n}", c), x[:, c, :], ALU.mult, ALU.add))
                        for c in range(KC):
                            chain.wait(chain.n - KC + 1)
                            chain.do(dve.scalar_tensor_tensor(dst[:, c, :], dn[:, c, :], m.col(f"mu_next{n}", c), dst[:, c, :], ALU.mult, ALU.add))
                    return steps

                chain = Chain(nc.vector, m.vec_step)
                with m.block() as block:
                    @block.vector
                    def _(dve):
                        mixing(0, mixed[0])(dve, chain)
                m.vec_step.over(chain.n)

                def cols_products(src, dst, extra):
                    jobs = []
                    for p in range(4):
                        jobs += m.cols_jobs(src, p, 2, dst, 2 * p)
                    m.products(jobs, extra)

                cols_products(mixed[0], r, mixing(2, mixed[1]))
                cols_products(mixed[1], k, mixing(3, mixed[0]))
                m.add_rows(mixed[0], 256, v, add=False, extra=mixing(1, mixed[1]))
                self.sig_w = [m.ring[:, s, :].rearrange("p (c s) -> p c s", c=KC) for s in (6, 7)]
                self.rate = [m.ring[:, s, :].rearrange("p (c s) -> p c s", c=KC) for s in (0, 1)]
                self.low_rank(mixed[1], w1, w_low, ACT.Tanh, w2, "w0", self.sig_w, mixing(4, mixed[0]))
                self.low_rank(mixed[0], a1, a_low, ACT.Copy, a2, "a0", self.rate, mixing(5, mixed[1]))
                self.gate_low(mixed[1], g1, g_low)
            kk = m.xT
            self.normed_keys(k, kk)
            with ExitStack() as inner:
                self.chunks(inner, r, k, kk, v, g_low, y)
            m.turn_only(y, m.xT)
        m.add_rows(m.xT, 256, u, add=False)

    def low_rank(self, x, w1, low, func, w2, bias, dst, extra):
        m = self.m
        ps = m.ps
        low_done, low_ready, done, taken = (m.sig(n) for n in ("low_done", "low_ready", "rank_done", "rank_taken"))
        chain = Chain(m.nc.vector, m.vec_step)
        with m.block() as block:
            @block.tensor
            def _(pe):
                for c in range(KC):
                    mm = pe.matmul(ps[:, 0, 0:SEQ], w1[:, c].rearrange("p d l -> p (d l)"), x[:, c, :], start=(c == 0), stop=(c == KC - 1))
                mm.then_inc(low_done.sem, 1)
                pe.wait_ge(low_ready.sem, low_ready.at(1))
                for n in range(2 * KC):
                    d, c = n // KC, n % KC
                    if n >= 6:
                        pe.wait_ge(taken.sem, taken.at(n - 5))
                    h = slice(d * HEAD, (d + 1) * HEAD)
                    pe.matmul(ps[:, 2 + n % 6, 0:SEQ], w2[h, c * P:(c + 1) * P], low[h, :], start=True, stop=True).then_inc(done.sem, 1)

            @block.scalar
            def _(act):
                act.wait_ge(low_done.sem, low_done.at(1))
                act.activation(low[:], ps[:, 0, 0:SEQ], func).then_inc(low_ready.sem, 1)
                for n in range(2 * KC):
                    d, c = n // KC, n % KC
                    act.wait_ge(done.sem, done.at(n + 1))
                    act.activation(dst[d][:, c, :], ps[:, 2 + n % 6, 0:SEQ], ACT.Sigmoid, bias=m.col(f"{bias}{d}", c)).then_inc(taken.sem, 1)

            @block.vector
            def _(dve):
                extra(dve, chain)
        m.vec_step.over(chain.n)
        low_done.over(1)
        low_ready.over(1)
        done.over(2 * KC)
        taken.over(2 * KC)

    def gate_low(self, x, g1, low):
        m = self.m
        done = m.sig("gate_low_done")
        with m.block() as block:
            @block.tensor
            def _(pe):
                for d in range(2):
                    for c in range(KC):
                        mm = pe.matmul(m.ps[:, d, 0:SEQ], g1[:, c, d, :], x[:, c, :], start=(c == 0), stop=(c == KC - 1))
                    mm.then_inc(done.sem, 1)

            @block.scalar
            def _(act):
                for d in range(2):
                    act.wait_ge(done.sem, done.at(d + 1))
                    act.activation(low[:, d, :], m.ps[:, d, 0:SEQ], ACT.Sigmoid)
        done.over(2)

    def normed_keys(self, k, kk):
        m = self.m
        ps = m.ps
        raw, squared, summed, rooted = (m.sig(n) for n in ("keys_raw", "keys_squared", "keys_summed", "keys_rooted"))
        chain = Chain(m.nc.vector, m.vec_step)
        with ExitStack() as ctx:
            sq = m.tmp(ctx, "sq", [P, KC, SEQ])
            root = m.tmp(ctx, "root", [P, KC, SEQ])
            pair = m.tmp(ctx, "pair", [P, P])
            with m.block() as block:
                @block.sync
                def _(sp):
                    sp.dma_start(pair[:], m.I["same_head"]).then_inc(m.side_loaded.sem, 16)

                @block.tensor
                def _(pe):
                    pe.wait_ge(m.side_loaded.sem, m.side_loaded.at(16))
                    for c in range(KC):
                        pe.wait_ge(squared.sem, squared.at(c + 1))
                        pe.matmul(ps[:, c, 0:SEQ], pair[:], sq[:, c, :], start=True, stop=True).then_inc(summed.sem, 1)

                @block.scalar
                def _(act):
                    for c in range(KC):
                        act.wait_ge(raw.sem, raw.at(c + 1))
                        act.activation(sq[:, c, :], kk[:, c, :], ACT.Square).then_inc(squared.sem, 1)
                    for c in range(KC):
                        act.wait_ge(summed.sem, summed.at(c + 1))
                        act.activation(root[:, c, :], ps[:, c, 0:SEQ], ACT.Sqrt).then_inc(rooted.sem, 1)

                @block.vector
                def _(dve):
                    for c in range(KC):
                        dve.tensor_scalar(kk[:, c, :], k[:, c, :], m.col("k_k", c), None, ALU.mult).then_inc(raw.sem, 1)
                    dve.wait_ge(rooted.sem, rooted.at(KC))
                    dve.wait_ge(squared.sem, squared.at(KC))
                    chain.link(dve.tensor_scalar(root[:], root[:], 1e-12, None, ALU.max))
                    chain.link(dve.reciprocal(root[:], root[:]))
                    dve.tensor_tensor(kk[:], kk[:], root[:], ALU.mult)
        m.side_loaded.over(16)
        m.vec_step.over(chain.n)
        for s in (raw, squared, summed, rooted):
            s.over(KC)

    def chunks(self, ctx, r, k, kk, v, g_low, y):
        m = self.m
        I, nc, ps = m.I, m.nc, m.ps
        tmp, sig = m.tmp, m.sig
        keep = tmp(ctx, "keep", [P, 2, 4 * P])
        level = tmp(ctx, "level", [P, 2 * LEVELS, P], I32)
        same = tmp(ctx, "same", [P, P])
        head_of = same[:].rearrange("p (h e) -> p h e", h=2)[:, :, 0]
        gn = tmp(ctx, "gn", [P, 2, P])
        g2 = tmp(ctx, "g2", [P, 2, P])
        cc = tmp(ctx, "cc", [P, 2])
        vc = tmp(ctx, "vc", [P, TT, P])
        S, X, Y = (tmp(ctx, n, [P, TT, P]) for n in "SXY")
        MT = tmp(ctx, "MT", [P, 4])
        eK, eR, eB = (tmp(ctx, n, [P, TT, P]) for n in ("eK", "eR", "eB"))
        kd, bb, fa = (tmp(ctx, n, [P, TT, P]) for n in ("kd", "bb", "fa"))
        KR = [tmp(ctx, "KR", [P, TT, 2, P]) for _ in range(2)]
        Bs = [tmp(ctx, "Bs", [P, TT, P]) for _ in range(2)]
        Ks = [tmp(ctx, "Ks", [P, TT, P]) for _ in range(2)]
        rkd = [tmp(ctx, "rkd", [P, TT, P]) for _ in range(2)]
        ends = [tmp(ctx, "ends", [P, 4]) for _ in range(2)]
        GM = [tmp(ctx, "GM", [P, 4, 4, P]) for _ in range(2)]
        M1 = [tmp(ctx, "M1", [P, 4, P]) for _ in range(2)]
        Xi = [tmp(ctx, "Xi", [P, 4, P]) for _ in range(2)]
        XT = [tmp(ctx, "XT", [P, 4, P]) for _ in range(2)]
        Pb = M1
        rowsBK = [tmp(ctx, "rowsBK", [P, 2, P]) for _ in range(2)]
        rhs = [tmp(ctx, "rhs", [P, 2, HEAD]) for _ in range(2)]
        sa = [tmp(ctx, "sa", [P, TT, 2, HEAD]) for _ in range(2)]
        S0 = [tmp(ctx, "S0", [P, 2, HEAD]) for _ in range(2)]
        o = tmp(ctx, "o", [P, TT, 2, HEAD])
        gb = tmp(ctx, "gb", [P, TT * P + 4])
        st = tmp(ctx, "st", [P, 4, 6])
        mv = tmp(ctx, "mv", [P, 4, 2])
        rs = tmp(ctx, "rs", [P, 2, 4])
        gn_eps = tmp(ctx, "gn_eps", [P, 4])

        names = ("shift_ready exps_ready prep_ready vc_ready products_done m1_done rows_done kept_ready x_ready rows_ready "
                 "half_done half_ready step_done rhs_done rhs_ready sa_done sa_ready state_done s0_ready out_done gates_done "
                 "var_ready gn_rstd pair_over slice_loaded").split()
        q = {n: sig("rwkv_" + n) for n in names}
        vec, pool_sig, step_begun = sig("rwkv_vec_step"), sig("rwkv_pool_step"), sig("rwkv_step_begun")
        N = {"shift_ready": 2, "exps_ready": 2, "prep_ready": 2, "vc_ready": 1, "products_done": 8, "m1_done": 2, "rows_done": 2,
             "kept_ready": 2, "x_ready": 2 * LEVELS, "rows_ready": 2, "half_done": 2 * (LEVELS - 1), "half_ready": 2 * (LEVELS - 1),
             "step_done": 2 * (LEVELS - 1), "rhs_done": 4, "rhs_ready": 4, "sa_done": 4, "sa_ready": 4, "state_done": 2, "s0_ready": 2,
             "out_done": 2, "gates_done": 2, "var_ready": 2, "gn_rstd": 2, "pair_over": 1, "slice_loaded": 64}
        pairs = D // P
        with m.block() as block:
            @block.sync
            def _(sp):
                sp.dma_start(keep[:], I["kept_places"].rearrange("d p n -> p d n")).then_inc(m.side_loaded.sem, 16)
                sp.dma_start(level[:], I["level_places"].rearrange("d p n -> p d n")).then_inc(m.side_loaded.sem, 16)
                sp.dma_start(same[:], I["same_head"]).then_inc(m.side_loaded.sem, 16)
                sp.wait_ge(m.side_loaded.sem, m.side_loaded.at(48))
        m.side_loaded.over(48)
        with m.block() as block:
            @block.vector
            def _(dve):
                for d in range(2):
                    dve.memset(S0[d][:], 0.0)
                dve.memset(gn_eps[:], GN_EPS)

        def at(n, i, k):
            return i * N[n] + k

        with m.block() as block:
            @block.sync
            def _(sp):
                m.run.load_until(sp, m.run.taken + 4)
                gn_src = (I["rk_gn_w_2"], I["rk_gn_b_2"])
                g2_src = I["rk_g2_2"][0].rearrange("d l n -> l d n")
                sp.sem_inc(q["pair_over"].sem, 1)
                with sp.Fori(0, pairs) as i:
                    sp.wait_ge(q["pair_over"].sem, i + 1)
                    cols = bass.ds(i * P, P)
                    for n in range(2):
                        sp.dma_start(gn[:, n, :], gn_src[n][0:1, cols].broadcast_to([P, P])).then_inc(q["slice_loaded"].sem, 16)
                    for d in range(2):
                        sp.dma_start(g2[:, d, :], g2_src[:, d, cols]).then_inc(q["slice_loaded"].sem, 16)

            @block.gpsimd
            def _(pool):
                with pool.Fori(0, pairs) as i:
                    pool.wait_ge(q["pair_over"].sem, i + 1)
                    pool.tensor_copy(vc[:], v[:, :, bass.ds(i * P, P)]).then_inc(q["vc_ready"].sem, 1)
                    for d in range(2):
                        pool.wait_ge(q["var_ready"].sem, at("var_ready", i, d + 1))
                        pool.tensor_tensor(rs[:, 0, :], mv[:, :, 1], gn_eps[:], ALU.add).then_inc(pool_sig.sem, 1)
                        pool.wait_ge(pool_sig.sem, i * 2 + (d + 1))
                        pool.tensor_tensor(rs[:, 1, :], rs[:, 0, :], m.neg_half[:, 0:4], ALU.pow).then_inc(q["gn_rstd"].sem, 1)

            @block.scalar
            def _(act):
                with act.Fori(0, pairs) as i:
                    for d in range(2):
                        act.wait_ge(q["shift_ready"].sem, at("shift_ready", i, d + 1))
                        if d:
                            act.wait_ge(q["prep_ready"].sem, at("prep_ready", i, 1))
                        act.activation(eK[:], (X if d else Y)[:], ACT.Exp, scale=KAPPA if d else -KAPPA)
                        act.activation(eR[:], (Y if d else X)[:], ACT.Exp, scale=KAPPA if d else -KAPPA)
                        act.activation(eB[:], (Y if d else X)[:], ACT.Exp, scale=-KAPPA if d else KAPPA)
                        act.activation(ends[d][:], MT[:], ACT.Exp, scale=-KAPPA).then_inc(q["exps_ready"].sem, 1)
                    for d in range(2):
                        act.wait_ge(q["rows_done"].sem, at("rows_done", i, d + 1))
                        act.activation(rowsBK[d][:], ps[:, 4 * d + 3, 0:2 * P].rearrange("p (a b) -> p a b", a=2), ACT.Copy).then_inc(q["rows_ready"].sem, 1)
                    for n in range(N["half_done"]):
                        d = n % 2
                        act.wait_ge(q["half_done"].sem, at("half_done", i, n + 1))
                        act.activation(Pb[d][:].rearrange("p a b -> p (a b)"), ps[:, 4 * d, :], ACT.Copy).then_inc(q["half_ready"].sem, 1)
                    for step in range(2):
                        for d in range(2):
                            n = 2 * step + d
                            act.wait_ge(q["rhs_done"].sem, at("rhs_done", i, n + 1))
                            act.activation(rhs[d][:].rearrange("p a b -> p (a b)"), ps[:, 4 * d, 0:P], ACT.Copy, scale=-1.0).then_inc(q["rhs_ready"].sem, 1)
                        for d in range(2):
                            n = 2 * step + d
                            t = d if step == 0 else 1 - d
                            act.wait_ge(q["sa_done"].sem, at("sa_done", i, n + 1))
                            act.activation(sa[d][:, t].rearrange("p a b -> p (a b)"), ps[:, 4 * d + 1, 0:P], ACT.Copy).then_inc(q["sa_ready"].sem, 1)

            @block.tensor
            def _(pe):
                with pe.Fori(0, pairs) as i:
                    def half(hh):
                        return slice(hh * HEAD, (hh + 1) * HEAD)

                    for d in range(2):
                        pe.wait_ge(q["prep_ready"].sem, at("prep_ready", i, d + 1))
                        for t in range(TT):
                            for hh in range(2):
                                both = KR[d][half(hh), t].rearrange("p a b -> p (a b)")
                                b = ps[:, 4 * d + 2 * t + hh, :]
                                pe.matmul(b[:, 0:2 * P], Bs[d][half(hh), t, :], both, start=True, stop=True)
                                pe.matmul(b[:, 2 * P:4 * P], Ks[d][half(hh), t, :], both, start=True, stop=True).then_inc(q["products_done"].sem, 1)
                    for d in range(2):
                        pe.wait_ge(q["kept_ready"].sem, at("kept_ready", i, d + 1))
                        for t in range(TT):
                            for hh in range(2):
                                mm = pe.matmul(ps[:, 4 * d + hh, t * P:(t + 1) * P], KR[d][half(hh), t, 0, :], Bs[d][half(hh), t, :], start=True, stop=True)
                        mm.then_inc(q["m1_done"].sem, 1)
                        for n, src in enumerate((Bs, Ks)):
                            mm = pe.transpose(ps[:, 4 * d + 3, n * P:(n + 1) * P], src[d][:, d, :], m.ident[:])
                        mm.then_inc(q["rows_done"].sem, 1)
                    for k in range(1, LEVELS):
                        for d in range(2):
                            pe.wait_ge(q["x_ready"].sem, at("x_ready", i, 2 * (k - 1) + d + 1))
                            for n in range(4):
                                mm = pe.matmul(ps[:, 4 * d, n * P:(n + 1) * P], GM[d][:, n, 0, :], Xi[d][:, n, :], start=True, stop=True)
                            mm.then_inc(q["half_done"].sem, 1)
                        for d in range(2):
                            pe.wait_ge(q["half_ready"].sem, at("half_ready", i, 2 * (k - 1) + d + 1))
                            if k < LEVELS - 1:
                                for n in range(4):
                                    pe.matmul(ps[:, 4 * d + 1, n * P:(n + 1) * P], XT[d][:, n, :], Pb[d][:, n, :], start=True, stop=True)
                            for n in range(4):
                                mm = pe.matmul(ps[:, 4 * d + 2, n * P:(n + 1) * P], Pb[d][:, n, :], XT[d][:, n, :], start=True, stop=True)
                            mm.then_inc(q["step_done"].sem, 1)
                    pe.wait_ge(q["vc_ready"].sem, at("vc_ready", i, 1))
                    for step in range(2):
                        for d in range(2):
                            t = d if step == 0 else 1 - d
                            if step == 0:
                                pe.wait_ge(q["x_ready"].sem, at("x_ready", i, 2 * (LEVELS - 1) + d + 1))
                            else:
                                pe.wait_ge(q["s0_ready"].sem, at("s0_ready", i, d + 1))
                            if step:
                                pe.matmul(ps[:, 4 * d, 0:P], KR[d][:, t, 0, :], S0[d][:].rearrange("p a b -> p (a b)"), start=True, stop=False)
                            for hh in range(2):
                                mm = pe.matmul(ps[:, 4 * d, hh * HEAD:(hh + 1) * HEAD], GM[d][:, 2 * t + hh, 2, :], vc[:, t, half(hh)],
                                               start=(step == 0), stop=(step == 0 or hh == 1))
                            mm.then_inc(q["rhs_done"].sem, 1)
                        for d in range(2):
                            t = d if step == 0 else 1 - d
                            pe.wait_ge(q["rhs_ready"].sem, at("rhs_ready", i, 2 * step + d + 1))
                            for hh in range(2):
                                mm = pe.matmul(ps[:, 4 * d + 1, hh * HEAD:(hh + 1) * HEAD], XT[d][:, 2 * t + hh, :], rhs[d][:, hh, :], start=True, stop=True)
                            mm.then_inc(q["sa_done"].sem, 1)
                        for d in range(2):
                            t = d if step == 0 else 1 - d
                            pe.wait_ge(q["sa_ready"].sem, at("sa_ready", i, 2 * step + d + 1))
                            if step == 0:
                                pe.wait_ge(q["rows_ready"].sem, at("rows_ready", i, d + 1))
                                for hh in range(2):
                                    dst = ps[:, 4 * d + 3, 256 + hh * HEAD:256 + (hh + 1) * HEAD]
                                    pe.matmul(dst, rowsBK[d][:, 0, :], sa[d][:, t, hh, :], start=True, stop=False)
                                    mm = pe.matmul(dst, rowsBK[d][:, 1, :], vc[:, t, half(hh)], start=False, stop=True)
                                mm.then_inc(q["state_done"].sem, 1)
                            if step:
                                pe.matmul(ps[:, 4 * d + 2, t * P:(t + 1) * P], KR[d][:, t, 1, :], S0[d][:].rearrange("p a b -> p (a b)"), start=True, stop=False)
                            for hh in range(2):
                                dst = ps[:, 4 * d + 2, (2 * t + hh) * HEAD:(2 * t + hh + 1) * HEAD]
                                pe.matmul(dst, GM[d][:, 2 * t + hh, 1, :], sa[d][:, t, hh, :], start=(step == 0), stop=False)
                                mm = pe.matmul(dst, GM[d][:, 2 * t + hh, 3, :], vc[:, t, half(hh)], start=False, stop=(step == 0 or hh == 1))
                            if step:
                                mm.then_inc(q["out_done"].sem, 1)
                    pe.wait_ge(q["slice_loaded"].sem, at("slice_loaded", i, 64))
                    for d in range(2):
                        for t in range(TT):
                            pe.matmul(ps[:, 4 * d + 3, t * P:(t + 1) * P], g_low[:, d, t * P:(t + 1) * P], g2[:, d, :], start=True, stop=True)
                            mm = pe.matmul(ps[:, 4 * d + 3, 2 * P + 2 * t:2 * P + 2 * t + 2], rkd[d][:, t, :], head_of, start=True, stop=True)
                        mm.then_inc(q["gates_done"].sem, 1)

            @block.vector
            def _(dve):
                tt, ts, stt = dve.tensor_tensor, dve.tensor_scalar, dve.scalar_tensor_tensor
                steps = {"n": 0}
                LINKS = 2 + 2 * 8 + 2 * 4 + 2 * 7

                with dve.Fori(0, pairs) as i:
                    steps["n"] = 0

                    def do(ins):
                        steps["n"] += 1
                        ins.then_inc(vec.sem, 1)

                    def link(ins=None):
                        if ins is not None:
                            do(ins)
                        dve.wait_ge(vec.sem, i * LINKS + steps["n"])

                    def begin_step():
                        dve.sem_inc(step_begun.sem, 1)

                    one = bass.ds(i, 1)
                    do(dve.tensor_copy(cc[:, 0:1], m.cols[:, m.col_at["k_a"][0], bass.ds(i + m.col_at["k_a"][1], 1)]))
                    link(dve.tensor_copy(cc[:, 1:2], m.cols[:, m.col_at["r_k"][0], bass.ds(i + m.col_at["r_k"][1], 1)]))
                    for d in range(2):
                        sg = self.sig_w[d][:, one, :].rearrange("p a (t s) -> p (a t) s", t=TT)
                        rate = self.rate[d][:, one, :].rearrange("p a (t s) -> p (a t) s", t=TT)
                        kc, kkc, rc = (z[:, one, :].rearrange("p a (t s) -> p (a t) s", t=TT) for z in (k, kk, r))
                        if d:
                            dve.wait_ge(q["exps_ready"].sem, at("exps_ready", i, 1))
                        for t in range(TT):
                            do(dve.tensor_tensor_scan(S[:, t, :], m.ones[:], self.sig_w[d][:, one, t * P:(t + 1) * P].rearrange("p a s -> p (a s)"), 0.0, ALU.mult, ALU.add))
                        link()
                        mid = S[:, :, P // 2 - 1:P // 2]
                        do(dve.tensor_copy(MT[:, 0:2], mid.rearrange("p t a -> p (t a)")))
                        do(tt(MT[:, 2:4].unsqueeze(2), S[:, :, P - 1:P], mid, ALU.subtract))
                        do(tt(X[:], S[:], mid.to_broadcast([P, TT, P]), ALU.subtract))
                        link()
                        tt(Y[:], X[:], sg, ALU.subtract).then_inc(q["shift_ready"].sem, 1)
                        link(ts(fa[:], rate, -1.0, cc[:, 0:1], ALU.add, ALU.mult))
                        do(stt(kd[:], fa[:], 1.0, kc, ALU.add, ALU.mult))
                        link(tt(bb[:], kkc, rate, ALU.mult))
                        stt(rkd[d][:], rc, cc[:, 1:2], kd[:], ALU.mult, ALU.mult)
                        dve.wait_ge(q["exps_ready"].sem, at("exps_ready", i, d + 1))
                        tt(KR[d][:, :, 0, :], kkc, eK[:], ALU.mult)
                        tt(KR[d][:, :, 1, :], rc, eR[:], ALU.mult)
                        tt(Bs[d][:], bb[:], eB[:], ALU.mult)
                        tt(Ks[d][:], kd[:], eB[:], ALU.mult).then_inc(q["prep_ready"].sem, 1)
                        if d == 0:
                            dve.wait_ge(q["prep_ready"].sem, at("prep_ready", i, 1))
                    for d in range(2):
                        for n in range(4):
                            dve.wait_ge(q["products_done"].sem, at("products_done", i, 4 * d + n + 1))
                            ins = tt(GM[d][:, n].rearrange("p a b -> p (a b)"), ps[:, 4 * d + n, :], keep[:, d, :], ALU.mult)
                        ins.then_inc(q["kept_ready"].sem, 1)
                    for d in range(2):
                        lower, upper = level[:, LEVELS * d, :], level[:, LEVELS * (1 - d), :]
                        dve.wait_ge(q["m1_done"].sem, at("m1_done", i, d + 1))
                        dve.wait_ge(q["kept_ready"].sem, at("kept_ready", i, d + 1))
                        for hh in range(2):
                            do(tt(M1[d][:].rearrange("p (t h) e -> p h t e", h=2)[:, hh], ps[:, 4 * d + hh, 0:2 * P].rearrange("p (a b) -> p a b", a=2),
                                  keep[:, 1 - d, 0:P].unsqueeze(1).to_broadcast([P, 2, P]), ALU.mult))
                        do(dve.tensor_copy(Xi[d][:], m.ident[:].unsqueeze(1).to_broadcast([P, 4, P])))
                        do(dve.tensor_copy(XT[d][:], m.ident[:].unsqueeze(1).to_broadcast([P, 4, P])))
                        link()
                        begin_step()
                        dve.copy_predicated(Xi[d][:], lower.unsqueeze(1).to_broadcast([P, 4, P]), M1[d][:])
                        dve.copy_predicated(XT[d][:], upper.unsqueeze(1).to_broadcast([P, 4, P]), GM[d][:, :, 0, :]).then_inc(q["x_ready"].sem, 1)
                    for lv in range(1, LEVELS):
                        for d in range(2):
                            lower, upper = level[:, LEVELS * d + lv, :], level[:, LEVELS * (1 - d) + lv, :]
                            dve.wait_ge(q["step_done"].sem, at("step_done", i, 2 * (lv - 1) + d + 1))
                            dve.wait_ge(q["x_ready"].sem, at("x_ready", i, 2 * (lv - 1) + d + 1))
                            begin_step()
                            if lv < LEVELS - 1:
                                dve.copy_predicated(Xi[d][:], lower.unsqueeze(1).to_broadcast([P, 4, P]), ps[:, 4 * d + 1, :].rearrange("p (a b) -> p a b", a=4))
                            dve.copy_predicated(XT[d][:], upper.unsqueeze(1).to_broadcast([P, 4, P]),
                                                ps[:, 4 * d + 2, :].rearrange("p (a b) -> p a b", a=4)).then_inc(q["x_ready"].sem, 1)
                    for d in range(2):
                        dve.wait_ge(q["state_done"].sem, at("state_done", i, d + 1))
                        for hh in range(2):
                            hs = slice(hh * HEAD, (hh + 1) * HEAD)
                            ins = ts(S0[d][hs, hh, :], ps[hs, 4 * d + 3, 256 + hh * HEAD:256 + (hh + 1) * HEAD], ends[d][hs, 2:3], ends[d][hs, 1:2], ALU.mult, ALU.mult)
                        ins.then_inc(q["s0_ready"].sem, 1)
                    for d in range(2):
                        dve.wait_ge(q["out_done"].sem, at("out_done", i, d + 1))
                        bank = ps[:, 4 * d + 2, 0:2 * P].rearrange("p (n e) -> p n e", n=4)
                        ov = o[:].rearrange("p t h e -> p (t h) e")
                        for n in range(4):
                            ins = dve.bn_stats(st[:, n, :], bank[:, n, :])
                        link(ins)
                        dve.wait_ge(q["gates_done"].sem, at("gates_done", i, d + 1))
                        do(dve.tensor_copy(gb[:], ps[:, 4 * d + 3, 0:2 * P + 4]))
                        for n in range(4):
                            ins = dve.bn_aggr(mv[:, n, :], st[:, n, :])
                        ins.then_inc(q["var_ready"].sem, 1)
                        dve.wait_ge(q["gn_rstd"].sem, at("gn_rstd", i, d + 1))
                        for n in range(4):
                            ins = ts(ov[:, n, :], bank[:, n, :], mv[:, n, 0:1], rs[:, 1, n:n + 1], ALU.subtract, ALU.mult)
                        link(ins)
                        o2 = o[:].rearrange("p t h e -> p t (h e)")
                        if d == 0:
                            dve.wait_ge(q["slice_loaded"].sem, at("slice_loaded", i, 64))
                        link(tt(o2, o2, gn[:, 0:1, :].to_broadcast([P, TT, P]), ALU.mult))
                        link(tt(o2, o2, gn[:, 1:2, :].to_broadcast([P, TT, P]), ALU.add))
                        for n in range(4):
                            t, hh = n // 2, n % 2
                            ins = stt(ov[:, n, :], vc[:, t, hh * HEAD:(hh + 1) * HEAD], gb[:, 2 * P + n:2 * P + n + 1], ov[:, n, :], ALU.mult, ALU.add)
                        link(ins)
                        yc = y[:, :, bass.ds(i * P, P)]
                        gates = gb[:, 0:2 * P].rearrange("p (t e) -> p t e", t=TT)
                        if d == 0:
                            link(tt(yc, o2, gates, ALU.mult))
                        else:
                            link(tt(o2, o2, gates, ALU.mult))
                            tt(yc, yc, o2, ALU.add).then_inc(q["pair_over"].sem, 1)
                    assert steps["n"] == LINKS, steps["n"]


def network(nc, I, out):
    with ExitStack() as ctx:
        m = Model(nc, I, out, ctx)
        layers = [Run(m.weights, 6 * l, m.layer_pieces(l)) for l in range(2)]
        attention = Run(m.weights, 6, by_cols(I["attn_w_in_2"][0], 256) + by_cols(I["attn_w_out_2"][0], 256))
        recurrent = Run(m.weights, 6, [p for n in "rkvo" for p in by_cols(I[f"rk_w_{n}_2"][0], 256)])
        m.run = layers[0]
        m.constants()
        m.bias_rows()
        m.hybrid_mixer(0)
        m.cross_attention(0)
        m.norm_turn(m.h, "norm_ffn_g0", m.xT)
        gate, up, down = m.ffn_sources(I["ffn_w_gate"][0], I["ffn_w_up"][0], I["ffn_w_down"][0])
        m.ffn(I["ffn_w_gate"].shape[2] // CHUNK, gate, up, down, layers[1], m.h, True)
        m.hybrid_mixer(1)
        m.cross_attention(1)
        m.experts(attention)
        m.rms_rows(m.h, I["norm_final_g"].unsqueeze(0), m.h, False)
        with ExitStack() as inner:
            u = m.tmp(inner, "u", [P, TT, D])
            m.attention_mixer(u)
            m.rms_rows(u, I["norm_g_2"][0, 1:2, :], m.h, True)
            m.second_mlp(0, recurrent, u)
            Rwkv(m).run(u)
            m.rms_rows(u, I["norm_g_2"][1, 1:2, :], m.h, True)
            m.second_mlp(1, None, u)
        m.store_rows(m.h)


_INS = ["x", "mem", "norm_mix_g", "w_in", "conv_a_w", "conv_a_b", "ln_a_g", "ln_a_b", "conv_b_w", "ln_c_g", "ln_c_b",
        "gmlp_ws", "gmlp_b", "mix_out_g", "w_mix_out", "norm_x_g", "norm_mem_g", "w_xq", "w_xkv", "w_xo", "norm_ffn_g",
        "ffn_w_gate", "ffn_w_up", "ffn_w_down", "moe_router", "moe_w_gate", "moe_w_up", "moe_w_down", "norm_final_g",
        "rel_table_2", "norm_g_2", "attn_w_in_2", "attn_sink_2", "attn_w_out_2", "rk_mu_prev_2", "rk_mu_next_2",
        "rk_w_r_2", "rk_w_k_2", "rk_w_v_2", "rk_w_o_2", "rk_k_k_2", "rk_k_a_2", "rk_r_k_2", "rk_gn_w_2", "rk_gn_b_2",
        "rk_w0_2", "rk_w1_2", "rk_w2_2", "rk_a0_2", "rk_a1_2", "rk_a2_2", "rk_g1_2", "rk_g2_2", "mlp_w1_2", "mlp_w2_2"]


def kernel(**inputs):
    import numpy as _np
    import concourse.bacc as _bacc
    from concourse import mybir as _mybir
    from concourse.bass_utils import run_bass_kernel_spmd as _run

    nc = _bacc.Bacc("TRN2", target_bir_lowering=False, num_devices=1)
    data = {name: _np.ascontiguousarray(inputs[name]) for name in _INS}
    data["bucket_of_distance"], data["distance_mask"] = t5_constants()
    data["kept_places"], data["level_places"], data["same_head"] = rwkv_constants()
    arrays, args = {}, {}
    for name, a in data.items():
        arrays[f"in_{name}_dram"] = a
        args[name] = nc.dram_tensor(f"in_{name}_dram", a.shape, _mybir.dt.from_np(a.dtype), kind="ExternalInput").ap()
    out = nc.dram_tensor("out_0_dram", (1, SEQ, D), _mybir.dt.float32, kind="ExternalOutput").ap()
    network(nc, args, out)
    r = _run(nc, [arrays], core_ids=[0])
    return r.results[0]["out_0_dram"]
```

```python
from contextlib import ExitStack

import numpy as np

import concourse.bass as bass
from concourse import mybir
from concourse.alu_op_type import AluOpType as ALU

F32 = mybir.dt.float32
I32 = mybir.dt.int32
U32 = mybir.dt.uint32
ACT = mybir.ActivationFunctionType
AX_X = mybir.AxisListType.X

P = 128
SEQ = 256
D = 1024
TT = SEQ // P
KC = D // P
EPS = 1e-6
GN_EPS = 64e-5
HEAD = 64
A_W, B_W, C_W = 384, 320, 320
A_TILES = A_W // P
B_TILES = [(0, 128), (128, 64), (192, 128)]
C_PIECES = [(0, 256), (256, 256), (512, 128)]
B_ORDER = (1, 2, 0)
A_TAPS, B_TAPS = 31, 3
C_GROUPS = C_W // HEAD
N_EXPERTS = 8
SLOTS = 96
MAX_TILES = -(-SEQ // SLOTS)
VIRTUAL = MAX_TILES * N_EXPERTS
MAX_ITEMS = N_EXPERTS + (2 * SEQ - 1) // (SLOTS + 1)
CHUNK = 256
RING = 8
UNIT = KC * 256
DIST = 2 * SEQ


class Signal:

    def __init__(self, sem):
        self.sem, self.base = sem, 0

    def at(self, n):
        return self.base + n

    def over(self, n):
        self.base += n


class Chain:

    def __init__(self, eng, counter):
        self.eng, self.counter, self.n = eng, counter, 0

    def do(self, ins):
        ins.then_inc(self.counter.sem, 1)
        self.n += 1
        return self.n

    def wait(self, n=None):
        self.eng.wait_ge(self.counter.sem, self.counter.at(self.n if n is None else n))

    def link(self, ins):
        self.do(ins)
        self.wait()


class Weights:

    def __init__(self, ring, loaded, used):
        self.ring, self.loaded, self.used = ring, loaded, used
        self.loads = [0] * RING

    def slot(self, n):
        return self.ring[:, n, :]


class Run:
    def __init__(self, weights, first, pieces):
        self.w, self.first, self.pieces = weights, first, pieces
        self.issued = self.taken = 0
        self.value, self.used_at = {}, {}

    def place(self, u):
        src = self.pieces[u]
        _, a, b = src.shape
        return self.w.slot((self.first + u) % RING)[:, 0:a * b].rearrange("p (a b) -> p a b", a=a)

    def load_until(self, sp, n):
        while self.issued < min(n, len(self.pieces)):
            u = self.issued
            s = (self.first + u) % RING
            if u >= RING:
                sp.wait_ge(self.w.used.sem, self.used_at[u - RING])
            self.w.loads[s] += 16
            self.value[u] = self.w.loads[s]
            sp.dma_start(self.place(u), self.pieces[u]).then_inc(self.w.loaded[s], 16)
            self.issued += 1


def by_cols(w, width):
    v = w.rearrange("(c p) n -> p c n", p=P)
    return [v[:, :, i:i + width] for i in range(0, w.shape[1], width)]


class Model:
    def __init__(self, nc, I, out, ctx):
        self.nc, self.I, self.out, self.ctx = nc, I, out, ctx
        self.n_tmp = 0
        self.named = {}
        sb, sem = self.sb, self.sem
        self.h = sb("h", [P, TT, D])
        self.xT = sb("xT", [P, KC, SEQ])
        self.ring = sb("ring", [P, RING, UNIT])
        self.ident = sb("ident", [P, P])
        self.ones = sb("ones", [P, P])
        self.neg_half = sb("neg_half", [P, 64])
        self.cols = sb("cols", [P, 5, P])
        self.ps = ctx.enter_context(nc.psum_tensor("ps", [P, 8, 512], F32))
        self.piece_loaded = [ctx.enter_context(nc.semaphore(f"piece_loaded{i}")) for i in range(RING)]
        self.product_done = sem("product_done")
        self.weights = Weights(self.ring, self.piece_loaded, self.product_done)
        self.gain_row = sb("gain_row", [P, D])
        self.next_gain = None
        self.gain_loaded = sem("gain_loaded")
        self.side_loaded = sem("side_loaded")
        self.squares_summed = sem("squares_summed")
        self.pool_step = sem("pool_step")
        self.rstd_ready = sem("rstd_ready")
        self.rows_scaled = sem("rows_scaled")
        self.turned = sem("turned")
        self.out_stored = sem("out_stored")
        self.evac_dve = sem("evac_dve")
        self.evac_act = sem("evac_act")
        self.vec_step = sem("vec_step")
        self.pool_done = sem("pool_done")
        self.scores_done = sem("scores_done")
        self.max_ready = sem("max_ready")
        self.probs_ready = sem("probs_ready")
        self.probs_turned = sem("probs_turned")
        self.probsT_ready = sem("probsT_ready")
        self.heads_done = sem("heads_done")
        self.head_stored = sem("head_stored")
        self.mlp = self.mlp_signals("ffn_")
        self.moe = self.mlp_signals("moe_")
        self.pick_ready = sem("moe_pick_ready")
        self.gathered = sem("moe_gathered")
        self.xg_ready = sem("moe_xg_ready")
        self.pick_turned = sem("moe_pick_turned")
        self.pickT_ready = sem("moe_pickT_ready")
        self.y_copied = sem("moe_y_copied")
        self.combined = sem("moe_combined")
        self.added = sem("moe_added")

    def sb(self, name, shape, dt=F32, ctx=None):
        return (ctx or self.ctx).enter_context(self.nc.sbuf_tensor(name, shape, dt))

    def tmp(self, ctx, name, shape, dt=F32):
        self.n_tmp += 1
        return self.sb(f"{name}_{self.n_tmp}", shape, dt, ctx)

    def sem(self, name):
        return Signal(self.ctx.enter_context(self.nc.semaphore(name)))

    def mlp_signals(self, pre):
        sem = self.sem
        s = {n: sem(pre + n) for n in ("gate_done", "up_done", "down_done", "act_done", "hidden_ready")}
        s["loaded"] = [[sem(f"{pre}{kind}{p}_loaded") for p in range(2)] for kind in ("gate", "up", "down")]
        return s

    def load_gain(self, sp):
        sp.dma_start(self.gain_row[:], self.next_gain.broadcast_to([P, D])).then_inc(self.gain_loaded.sem, 16)

    def block(self):
        return self.nc.Block(no_gpsimd_drain=True)

    def col(self, name, c=0):
        t, r = self.col_at[name]
        return self.cols[:, t, r + c:r + c + 1]

    def constants(self):
        I = self.I
        tables, self.col_at = [[] for _ in range(5)], {}
        fill = [0] * 5

        def put(t, names, src, wide=P):
            n = src.shape[0]
            for i, name in enumerate(names):
                self.col_at[name] = (t, fill[t] + i * (n // len(names)))
            tables[t].append((fill[t], n, wide, src))
            fill[t] += n
            assert fill[t] <= P

        layers = range(2)
        for n in ("norm_mix_g", "mix_out_g", "norm_x_g", "norm_mem_g", "norm_ffn_g"):
            put(0, [f"{n}{l}" for l in layers], I[n].rearrange("l (c p) -> (l c) p", p=P))
        put(0, ["k_k"], I["rk_k_k_2"].rearrange("l (c p) -> (l c) p", p=P))
        put(0, ["k_a"], I["rk_k_a_2"].rearrange("l (c p) -> (l c) p", p=P))
        put(0, ["r_k"], I["rk_r_k_2"][0].rearrange("(c a) b -> c (a b)", a=2))
        put(0, ["w00", "w01"], I["rk_w0_2"][0].rearrange("d (c p) -> (d c) p", p=P))
        put(1, [f"norm2_{l}{j}" for l in layers for j in range(4)], I["norm_g_2"].rearrange("l j (c p) -> (l j c) p", p=P))
        put(1, [f"mu_prev{m}" for m in range(6)], I["rk_mu_prev_2"][0].rearrange("m (c p) -> (m c) p", p=P))
        put(1, [f"gmlp_b{l}" for l in layers], I["gmlp_b"].rearrange("l g p -> (l g) p"))
        put(2, [f"mu_next{m}" for m in range(6)], I["rk_mu_next_2"][0].rearrange("m (c p) -> (m c) p", p=P))
        put(2, ["a00", "a01"], I["rk_a0_2"][0].rearrange("d (c p) -> (d c) p", p=P))
        put(2, [f"conv_a_b{l}" for l in layers], I["conv_a_b"].rearrange("l (c p) -> (l c) p", p=P))
        for i, (o, n) in enumerate(B_TILES):
            put(2, [f"conv_b{l}{i}" for l in layers], I["conv_b_w"][:, :, o:o + n].rearrange("l k p -> (l k) p"), n)
        for i in range(A_TILES):
            put(3 + i // 2, [f"conv_a{l}{i}" for l in layers], I["conv_a_w"][:, :, i * P:(i + 1) * P].rearrange("l k p -> (l k) p"))
        with ExitStack() as ctx:
            raw = self.tmp(ctx, "raw", [P, 5, P])
            loads = sum(len(t) for t in tables)
            with self.block() as block:
                @block.sync
                def _(sp):
                    sp.dma_start(self.h[:], I["x"].rearrange("a (t p) d -> p (a t) d", p=P)).then_inc(self.side_loaded.sem, 16)
                    sp.wait_ge(self.pool_done.sem, self.pool_done.at(1))
                    for t, rows in enumerate(tables):
                        for r, n, wide, src in rows:
                            sp.dma_start(raw[r:r + n, t, 0:wide], src).then_inc(self.side_loaded.sem, 16)
                    self.run.load_until(sp, RING)

                @block.gpsimd
                def _(pool):
                    pool.memset(raw[:], 0.0).then_inc(self.pool_done.sem, 1)
                    pool.memset(self.ones[:], 1.0).then_inc(self.pool_done.sem, 1)
                    pool.memset(self.neg_half[:], -0.5)
                    pool.wait_ge(self.pool_done.sem, self.pool_done.at(2))
                    pool.affine_select(out=self.ident[:], in_=self.ones[:], compare_op=ALU.is_equal, fill=0.0, base=0,
                                       pattern=[[-1, P]], channel_multiplier=1).then_inc(self.pool_done.sem, 1)

                @block.tensor
                def _(pe):
                    pe.wait_ge(self.pool_done.sem, self.pool_done.at(3))
                    pe.wait_ge(self.side_loaded.sem, self.side_loaded.at(16 * (loads + 1)))
                    for t in range(5):
                        last = pe.transpose(self.ps[:, t // 4, (t % 4) * P:(t % 4 + 1) * P], raw[:, t, :], self.ident[:])
                    last.then_inc(self.turned.sem, 1)

                @block.vector
                def _(dve):
                    dve.wait_ge(self.turned.sem, self.turned.at(1))
                    dve.tensor_copy(self.cols[:, 0:4, :], self.ps[:, 0, :].rearrange("p (a b) -> p a b", a=4))
                    dve.tensor_copy(self.cols[:, 4, :], self.ps[:, 1, 0:P])
            self.side_loaded.over(16 * (loads + 1))
            self.pool_done.over(3)
            self.turned.over(1)

    def turned_cols(self, c, bank=0):
        return self.ps[:, bank + c // 2, (c % 2) * SEQ:(c % 2 + 1) * SEQ]

    def turn_scaled(self, pe, rows):
        for t in range(TT):
            pe.wait_ge(self.rows_scaled.sem, self.rows_scaled.at(t + 1))
            for c in range(KC):
                last = pe.transpose(self.turned_cols(c)[:, t * P:(t + 1) * P], rows[:, t, c * P:(c + 1) * P], self.ident[:])
                if t == TT - 1:
                    last.then_inc(self.turned.sem, 1)

    def take_turned_scalar(self, act, gain, dst):
        for c in (2, 3, 6, 7):
            act.wait_ge(self.turned.sem, self.turned.at((c | 1) + 1))
            act.activation(dst[:, c, :], self.turned_cols(c), ACT.Copy, scale=self.col(gain, c))

    def take_turned_vector(self, dve, gain, dst):
        for c in (0, 1, 4, 5):
            dve.wait_ge(self.turned.sem, self.turned.at((c | 1) + 1))
            dve.tensor_scalar(dst[:, c, :], self.turned_cols(c), self.col(gain, c), None, ALU.mult)

    def square_rows(self, act, junk, src, stat, n):
        if n:
            act.wait_ge(self.squares_summed.sem, self.squares_summed.at(n))
        act.activation(junk[:], src, ACT.Square, accum_out=stat[:, 0, n:n + 1]).then_inc(self.squares_summed.sem, 1)

    def rstd_of_rows(self, pool, stat, n):
        pool.wait_ge(self.squares_summed.sem, self.squares_summed.at(n + 1))
        pool.tensor_scalar(stat[:, 1, n:n + 1], stat[:, 0, n:n + 1], 1.0 / D, EPS, ALU.mult, ALU.add).then_inc(self.pool_step.sem, 1)
        pool.wait_ge(self.pool_step.sem, self.pool_step.at(n + 1))
        pool.tensor_tensor(stat[:, 2, n:n + 1], stat[:, 1, n:n + 1], self.neg_half[:, 0:1], ALU.pow).then_inc(self.rstd_ready.sem, 1)

    def norm_turn(self, src, gain, dst, keep_rows=None):
        with ExitStack() as ctx:
            junk = self.tmp(ctx, "junk", [P, D])
            rows = keep_rows if keep_rows is not None else self.tmp(ctx, "rows", [P, TT, D])
            stat = self.tmp(ctx, "stat", [P, 3, TT])
            with self.block() as block:
                @block.sync
                def _(sp):
                    self.run.load_until(sp, self.run.taken + RING)

                @block.gpsimd
                def _(pool):
                    for t in range(TT):
                        self.rstd_of_rows(pool, stat, t)

                @block.tensor
                def _(pe):
                    self.turn_scaled(pe, rows)

                @block.scalar
                def _(act):
                    for t in range(TT):
                        self.square_rows(act, junk, src[:, t, :], stat, t)
                    self.take_turned_scalar(act, gain, dst)

                @block.vector
                def _(dve):
                    for t in range(TT):
                        dve.wait_ge(self.rstd_ready.sem, self.rstd_ready.at(t + 1))
                        dve.tensor_scalar(rows[:, t, :], src[:, t, :], stat[:, 2, t:t + 1], None, ALU.mult).then_inc(self.rows_scaled.sem, 1)
                    self.take_turned_vector(dve, gain, dst)
            self.squares_summed.over(TT)
            self.pool_step.over(TT)
            self.rstd_ready.over(TT)
            self.rows_scaled.over(TT)
            self.turned.over(KC)

    def close_and_norm(self, src, add, gain, dst):
        with ExitStack() as ctx:
            junk = self.tmp(ctx, "junk", [P, D])
            normed = self.tmp(ctx, "normed", [P, TT, D])
            rows = self.tmp(ctx, "rows", [P, TT, D])
            stat = self.tmp(ctx, "stat", [P, 3, 2 * TT])
            h, updated = self.h, self.sig("rows_updated")
            chain = Chain(self.nc.vector, self.vec_step)
            with self.block() as block:
                @block.sync
                def _(sp):
                    self.run.load_until(sp, self.run.taken + RING)

                @block.gpsimd
                def _(pool):
                    for n in range(2 * TT):
                        self.rstd_of_rows(pool, stat, n)

                @block.tensor
                def _(pe):
                    self.turn_scaled(pe, rows)

                @block.scalar
                def _(act):
                    for t in range(TT):
                        self.square_rows(act, junk, src[:, t, :], stat, t)
                    for t in range(TT):
                        act.wait_ge(updated.sem, updated.at(t + 1))
                        self.square_rows(act, junk, h[:, t, :], stat, TT + t)
                    self.take_turned_scalar(act, gain, dst)

                @block.vector
                def _(dve):
                    dve.wait_ge(self.gain_loaded.sem, self.gain_loaded.at(16))
                    for t in range(TT):
                        dve.wait_ge(self.rstd_ready.sem, self.rstd_ready.at(t + 1))
                        scale = stat[:, 2, t:t + 1]
                        if add:
                            chain.link(dve.scalar_tensor_tensor(normed[:, t, :], src[:, t, :], scale, self.gain_row[:], ALU.mult, ALU.mult))
                            dve.tensor_tensor(h[:, t, :], h[:, t, :], normed[:, t, :], ALU.add).then_inc(updated.sem, 1)
                        else:
                            dve.scalar_tensor_tensor(h[:, t, :], src[:, t, :], scale, self.gain_row[:], ALU.mult, ALU.mult).then_inc(updated.sem, 1)
                    for t in range(TT):
                        dve.wait_ge(self.rstd_ready.sem, self.rstd_ready.at(TT + t + 1))
                        dve.wait_ge(updated.sem, updated.at(t + 1))
                        dve.tensor_scalar(rows[:, t, :], h[:, t, :], stat[:, 2, TT + t:TT + t + 1], None, ALU.mult).then_inc(self.rows_scaled.sem, 1)
                    self.take_turned_vector(dve, gain, dst)
            self.gain_loaded.over(16)
            updated.over(TT)
            self.vec_step.over(chain.n)
            self.squares_summed.over(2 * TT)
            self.pool_step.over(2 * TT)
            self.rstd_ready.over(2 * TT)
            self.rows_scaled.over(TT)
            self.turned.over(KC)

    def norm_beside(self, ctx, src, dst, gain, jobs, load=None):
        junk = self.tmp(ctx, "junk", [P, D])
        rows = self.tmp(ctx, "rows", [P, TT, D])
        stat = self.tmp(ctx, "stat", [P, 3, TT])
        rstd, scaled, turned, side = self.rstd_ready, self.rows_scaled, self.turned, self.side_loaded

        def scale(c):
            return self.ones[:, 0:1] if gain is None else self.col(gain, c)

        def sync(sp):
            if load is not None:
                load(sp)

        def scalar_first(act):
            if load is not None:
                act.wait_ge(side.sem, side.at(16))
            for t in range(TT):
                self.square_rows(act, junk, src[:, t, :], stat, t)

        def gpsimd(pool):
            for t in range(TT):
                self.rstd_of_rows(pool, stat, t)

        def vector_first(dve, chain):
            for t in range(TT):
                dve.wait_ge(rstd.sem, rstd.at(t + 1))
                dve.tensor_scalar(rows[:, t, :], src[:, t, :], stat[:, 2, t:t + 1], None, ALU.mult).then_inc(scaled.sem, 1)

        def tensor(pe, n):
            if n == jobs - 2:
                pe.wait_ge(scaled.sem, scaled.at(TT))
                for c in range(KC):
                    for t in range(TT):
                        last = pe.transpose(self.turned_cols(c, 4)[:, t * P:(t + 1) * P], rows[:, t, c * P:(c + 1) * P], self.ident[:])
                    last.then_inc(turned.sem, 1)

        def vector(dve, chain):
            for c in (0, 1, 4, 5):
                dve.wait_ge(turned.sem, turned.at((c | 1) + 1))
                dve.tensor_scalar(dst[:, c, :], self.turned_cols(c, 4), scale(c), None, ALU.mult)

        def scalar(act):
            for c in (2, 3, 6, 7):
                act.wait_ge(turned.sem, turned.at((c | 1) + 1))
                act.activation(dst[:, c, :], self.turned_cols(c, 4), ACT.Copy, scale=scale(c))

        def close():
            if load is not None:
                side.over(16)
            self.squares_summed.over(TT)
            self.pool_step.over(TT)
            rstd.over(TT)
            scaled.over(TT)
            turned.over(KC)

        return {"sync": sync, "scalar_first": scalar_first, "gpsimd": gpsimd, "vector_first": vector_first,
                "tensor": tensor, "vector": vector, "scalar": scalar}, close

    def products(self, jobs, extra=None, banks=8, by_vector=None, funcs=None, beside=None):
        run = self.run
        first = run.taken
        pieces = sorted({j[0] for j in jobs})
        assert pieces == list(range(len(pieces)))
        last_job = {p: max(n for n, j in enumerate(jobs) if j[0] == p) for p in pieces}
        funcs, beside = funcs or {}, beside or {}
        for p in pieces:
            run.used_at[first + p] = self.product_done.at(last_job[p] + 1)
        vector = {n for n, j in enumerate(jobs) if j[3] or (n % 2 == 0 if by_vector is None else n in by_vector)}
        taken_by, count = [], {True: 0, False: 0}
        for n in range(len(jobs)):
            mine = n in vector
            count[mine] += 1
            taken_by.append((self.evac_dve if mine else self.evac_act, count[mine]))

        def bank(n, dst):
            m, w = dst.shape[0], dst.shape[1]
            return self.ps[0:m, n % banks, 0:w]

        chain = Chain(self.nc.vector, self.vec_step)
        with self.block() as block:
            @block.sync
            def _(sp):
                if "sync" in beside:
                    beside["sync"](sp)
                run.load_until(sp, first + len(pieces) + RING)

            @block.tensor
            def _(pe):
                seen = set()
                for n, (p, pairs, dst, add) in enumerate(jobs):
                    u = first + p
                    if p not in seen:
                        pe.wait_ge(self.piece_loaded[(run.first + u) % RING], run.value[u])
                        seen.add(p)
                    if n >= banks:
                        who, k = taken_by[n - banks]
                        pe.wait_ge(who.sem, who.at(k))
                    here = run.place(u)
                    for i, (left, right) in enumerate(pairs):
                        mm = pe.matmul(bank(n, dst), left(here), right(here), start=(i == 0), stop=(i == len(pairs) - 1))
                    mm.then_inc(self.product_done.sem, 1)
                    if "tensor" in beside:
                        beside["tensor"](pe, n)

            if "gpsimd" in beside:
                block.gpsimd(beside["gpsimd"])

            @block.vector
            def _(dve):
                if extra is not None:
                    extra(dve, chain)
                if "vector_first" in beside:
                    beside["vector_first"](dve, chain)
                for n, (p, pairs, dst, add) in enumerate(jobs):
                    if n not in vector:
                        continue
                    dve.wait_ge(self.product_done.sem, self.product_done.at(n + 1))
                    if add:
                        dve.tensor_tensor(dst, dst, bank(n, dst), ALU.add).then_inc(self.evac_dve.sem, 1)
                    else:
                        dve.tensor_copy(dst, bank(n, dst)).then_inc(self.evac_dve.sem, 1)
                if "vector" in beside:
                    beside["vector"](dve, chain)

            @block.scalar
            def _(act):
                if "scalar_first" in beside:
                    beside["scalar_first"](act)
                for n, (p, pairs, dst, add) in enumerate(jobs):
                    if n in vector:
                        continue
                    act.wait_ge(self.product_done.sem, self.product_done.at(n + 1))
                    act.activation(dst, bank(n, dst), funcs.get(n, ACT.Copy)).then_inc(self.evac_act.sem, 1)
                if "scalar" in beside:
                    beside["scalar"](act)
        run.taken += len(pieces)
        self.vec_step.over(chain.n)
        self.product_done.over(len(jobs))
        self.evac_dve.over(count[True])
        self.evac_act.over(count[False])

    def sig(self, name):
        if name not in self.named:
            self.named[name] = self.sem(name)
        return self.named[name]

    def mixer_jobs(self, a_cols, b_cols, c_rows):
        jobs = []
        x = self.xT

        def turned_job(p, o, m, dst):
            jobs.append((p, [(lambda w, c=c: w[:, c, o:o + m], lambda w, c=c: x[:, c, :]) for c in range(KC)], dst, False))

        for p in range(3):
            for i in range(2):
                turned_job(p, i * P, P, a_cols[:, 2 * p + i, :])
        for p, (o, m) in enumerate(C_PIECES):
            for t in range(TT):
                jobs.append((3 + p, [(lambda w, c=c, t=t: x[:, c, t * P:(t + 1) * P], lambda w, c=c: w[:, c, :])
                                     for c in range(KC)], c_rows[:, t, o:o + m], False))
        for n, part in enumerate(B_ORDER):
            for i, (o, m) in enumerate(B_TILES):
                turned_job(6 + 2 * n + i // 2, o if i < 2 else 0, m, b_cols[0:m, 3 * part + i, :])
        return jobs

    def add_rows(self, x, width, dst, add=True, extra=None, beside=None):
        jobs = []
        for p in range(D // width):
            for t in range(TT):
                jobs.append((p, [(lambda w, c=c, t=t: x[:, c, t * P:(t + 1) * P], lambda w, c=c: w[:, c, :])
                                 for c in range(KC)], dst[:, t, p * width:(p + 1) * width], add))
        self.products(jobs, extra, banks=4 if beside else 8, beside=beside)

    def cols_jobs(self, x, p, n, dst, first):
        return [(p, [(lambda w, c=c, i=i: w[:, c, i * P:(i + 1) * P], lambda w, c=c: x[:, c, :]) for c in range(KC)],
                 dst[:, first + i, :], False) for i in range(n)]

    def hybrid_mixer(self, l, memory_rows=None, memory=None):
        self.norm_turn(self.h, f"norm_mix_g{l}", self.xT)
        with ExitStack() as ctx:
            y = self.tmp(ctx, "y", [P, TT, D])
            c_rows = self.tmp(ctx, "c_rows", [P, TT, 2 * C_W])
            with ExitStack() as inner:
                a_cols = self.tmp(inner, "a_cols", [P, 2 * A_TILES, SEQ])
                b_cols = self.tmp(inner, "b_cols", [P, 9, SEQ])
                self.mixer_middle(l, a_cols, b_cols, c_rows, y, inner)
            self.group_norm_turn(y, f"mix_out_g{l}", self.xT)
        if memory_rows is None:
            self.add_rows(self.xT, 256, self.h)
        else:
            with ExitStack() as ctx:
                def load(sp):
                    sp.dma_start(memory_rows[:], self.I["mem"].rearrange("a (t p) d -> p (a t) d", p=P)).then_inc(self.side_loaded.sem, 16)

                work, close = self.norm_beside(ctx, memory_rows, memory, None, 8, load)
                self.add_rows(self.xT, 256, self.h, beside=work)
                close()

    def mixer_middle(self, l, a_cols, b_cols, c_rows, y, ctx):
        I = self.I
        pad_a, pad_b = A_TAPS - 1, B_TAPS - 1
        gated = self.tmp(ctx, "gated", [P, A_TILES, pad_a + SEQ])
        conv = self.tmp(ctx, "conv", [P, A_TILES, SEQ])
        cb = self.tmp(ctx, "cb", [P, 3, pad_b + SEQ])
        conv_b = self.tmp(ctx, "conv_b", [P, 3, SEQ])
        ws = self.tmp(ctx, "ws", [P, C_GROUPS, P])
        wsT = self.tmp(ctx, "wsT", [P, C_GROUPS, P])
        gains = self.tmp(ctx, "gains", [P, 2 * A_W + 2 * C_W])
        ga, ba = gains[:, 0:A_W], gains[:, A_W:2 * A_W]
        gc, bc = gains[:, 2 * A_W:2 * A_W + C_W], gains[:, 2 * A_W + C_W:]
        stats = self.tmp(ctx, "stats", [P, 4, 6])
        mv = self.tmp(ctx, "mv", [P, 4, 2])
        rstd = self.tmp(ctx, "rstd", [P, 4])
        var = self.tmp(ctx, "var", [P, 4])
        vnorm = self.tmp(ctx, "vnorm", [P, TT, C_W])
        side, conv_ready, turned = self.side_loaded, self.sig("conv_ready"), self.turned
        wsT_ready, v_ready, var_ready, vnorm_ready = (self.sig(n) for n in ("wsT_ready", "v_ready", "var_ready", "vnorm_ready"))
        mixed, affine_ready = self.sig("gate_mixed"), self.sig("affine_ready")
        ps = self.ps
        BANKS = 2
        rows_a = [ps[:, 4 + t, 0:A_W] for t in range(TT)]
        rows_b = [ps[:, 6 + t, 0:B_W] for t in range(TT)]
        mix_c = [ps[:, 2 + t, 0:C_W] for t in range(TT)]
        wsT_ps = ps[:, 6:8, :]
        jobs = self.mixer_jobs(a_cols, b_cols, c_rows)
        A_JOBS, C_JOBS, B_JOBS = 6, 6, 9
        assert len(jobs) == A_JOBS + C_JOBS + B_JOBS
        by_vector = range(A_TILES)
        by_scalar = len(jobs) - A_TILES
        funcs = {n: ACT.Sigmoid for n in range(A_TILES, A_JOBS)}
        funcs.update({n: ACT.Gelu_apprx_tanh for n in range(A_JOBS, A_JOBS + C_JOBS)})

        def loads(sp):
            sp.dma_start(ws[:], I["gmlp_ws"][l].rearrange("g i j -> i g j")).then_inc(side.sem, 16)
            for dst, name, n in ((ga, "ln_a_g", A_W), (ba, "ln_a_b", A_W), (gc, "ln_c_g", C_W), (bc, "ln_c_b", C_W)):
                sp.dma_start(dst, I[name][l:l + 1, :].broadcast_to([P, n])).then_inc(side.sem, 16)

        def tensor(pe, n):
            if n == A_JOBS + 2:
                pe.wait_ge(side.sem, side.at(16 * 5))
                for g in range(C_GROUPS):
                    last = pe.transpose(wsT_ps[:, g // 4, (g % 4) * P:(g % 4 + 1) * P], ws[:, g, :], self.ident[:])
                last.then_inc(turned.sem, 1)
            if n == A_JOBS + C_JOBS + 4:
                pe.wait_ge(conv_ready.sem, conv_ready.at(1))
                for t in range(TT):
                    for i in range(A_TILES):
                        last = pe.transpose(rows_a[t][:, i * P:(i + 1) * P], conv[:, i, t * P:(t + 1) * P], self.ident[:])
                last.then_inc(turned.sem, 1)
            if n == A_JOBS + C_JOBS + 6:
                pe.wait_ge(wsT_ready.sem, wsT_ready.at(1))
                for t in range(TT):
                    pe.wait_ge(vnorm_ready.sem, vnorm_ready.at(t + 1))
                    for g in range(C_GROUPS):
                        last = pe.matmul(mix_c[t][:, g * HEAD:(g + 1) * HEAD], wsT[:, g, :], vnorm[:, t, g * HEAD:(g + 1) * HEAD], start=True, stop=True)
                    last.then_inc(mixed.sem, 1)
            if n == len(jobs) - 1:
                pe.wait_ge(conv_ready.sem, conv_ready.at(2))
                for t in range(TT):
                    for i, (o, m) in enumerate(B_TILES):
                        last = pe.transpose(rows_b[t][:, o:o + m], conv_b[0:m, i, t * P:(t + 1) * P], self.ident[0:m, 0:m])
                last.then_inc(turned.sem, 1)

        def scalar(act):
            for t in range(TT):
                act.wait_ge(affine_ready.sem, affine_ready.at(t + 1))
                act.activation(y[:, t, 0:A_W], y[:, t, 0:A_W], ACT.Silu)

        def gpsimd(pool):
            for i in range(4):
                pool.wait_ge(v_ready.sem, v_ready.at(i + 1))
                pool.tensor_scalar(var[:, i:i + 1], mv[:, i, 1:2], EPS, 1.0, ALU.add, ALU.mult).then_inc(self.pool_step.sem, 1)
                pool.wait_ge(self.pool_step.sem, self.pool_step.at(i + 1))
                pool.tensor_tensor(rstd[:, i:i + 1], var[:, i:i + 1], self.neg_half[:, 0:1], ALU.pow).then_inc(var_ready.sem, 1)

        def vector(dve, chain):
            dve.memset(gated[:, :, 0:pad_a], 0.0)
            dve.memset(cb[:, :, 0:pad_b], 0.0)
            dve.wait_ge(self.evac_dve.sem, self.evac_dve.at(A_TILES))
            dve.wait_ge(self.evac_act.sem, self.evac_act.at(A_TILES))
            chain.link(dve.tensor_tensor(gated[:, :, pad_a:], a_cols[:, 0:A_TILES, :], a_cols[:, A_TILES:, :], ALU.mult))
            for k in range(A_TAPS):
                for i in range(A_TILES):
                    w = self.col(f"conv_a{l}{i}", k)
                    if k == 0:
                        chain.do(dve.tensor_scalar(conv[:, i, :], gated[:, i, 0:SEQ], w, self.col(f"conv_a_b{l}", i), ALU.mult, ALU.add))
                    else:
                        chain.wait(chain.n - A_TILES + 1)
                        ins = dve.scalar_tensor_tensor(conv[:, i, :], gated[:, i, k:k + SEQ], w, conv[:, i, :], ALU.mult, ALU.add)
                        if (k, i) == (A_TAPS - 1, A_TILES - 1):
                            ins.then_inc(conv_ready.sem, 1)
                        else:
                            chain.do(ins)
            dve.wait_ge(turned.sem, turned.at(1))
            chain.link(dve.tensor_copy(wsT[:], wsT_ps.rearrange("p a b -> p (a b)")[:, 0:C_GROUPS * P].rearrange("p (g i) -> p g i", g=C_GROUPS)))
            dve.memset(wsT[HEAD:P, :, 0:HEAD], 0.0).then_inc(wsT_ready.sem, 1)
            dve.wait_ge(side.sem, side.at(16 * 5))

            def layer_norm(i, src, dst, g, b):
                chain.link(dve.bn_stats(stats[:, i, :], src))
                dve.bn_aggr(mv[:, i, :], stats[:, i, :]).then_inc(v_ready.sem, 1)
                dve.wait_ge(var_ready.sem, var_ready.at(i + 1))
                chain.link(dve.tensor_scalar(dst, src, mv[:, i, 0:1], rstd[:, i:i + 1], ALU.subtract, ALU.mult))
                chain.link(dve.tensor_tensor(dst, dst, g, ALU.mult))
                return dve.tensor_tensor(dst, dst, b, ALU.add)

            dve.wait_ge(self.evac_act.sem, self.evac_act.at(A_TILES + C_JOBS))
            for t in range(TT):
                layer_norm(t, c_rows[:, t, C_W:], vnorm[:, t, :], gc, bc).then_inc(vnorm_ready.sem, 1)
            dve.wait_ge(turned.sem, turned.at(2))
            for t in range(TT):
                layer_norm(TT + t, rows_a[t], y[:, t, 0:A_W], ga, ba).then_inc(affine_ready.sem, 1)
            dve.wait_ge(self.evac_act.sem, self.evac_act.at(A_TILES + C_JOBS + 2 * len(B_TILES)))
            for i, (_, m) in enumerate(B_TILES):
                chain.do(dve.tensor_tensor(cb[0:m, i, pad_b:], b_cols[0:m, 3 + i, :], b_cols[0:m, 6 + i, :], ALU.mult))
            chain.wait()
            for k in range(B_TAPS):
                for i, (_, m) in enumerate(B_TILES):
                    w = self.col(f"conv_b{l}{i}", k)[0:m]
                    if k == 0:
                        chain.do(dve.tensor_scalar(conv_b[0:m, i, :], cb[0:m, i, 0:SEQ], w, None, ALU.mult))
                    else:
                        chain.wait(chain.n - 2)
                        chain.do(dve.scalar_tensor_tensor(conv_b[0:m, i, :], cb[0:m, i, k:k + SEQ], w, conv_b[0:m, i, :], ALU.mult, ALU.add))
            for t in range(TT):
                dve.wait_ge(mixed.sem, mixed.at(t + 1))
                for g in range(C_GROUPS):
                    o = A_W + B_W + g * HEAD
                    dve.scalar_tensor_tensor(y[:, t, o:o + HEAD], mix_c[t][:, g * HEAD:(g + 1) * HEAD], self.col(f"gmlp_b{l}", g),
                                             c_rows[:, t, g * HEAD:(g + 1) * HEAD], ALU.add, ALU.mult)
            chain.wait()
            dve.wait_ge(self.evac_act.sem, self.evac_act.at(by_scalar))
            for i, (_, m) in enumerate(B_TILES):
                last = dve.tensor_tensor(conv_b[0:m, i, :], conv_b[0:m, i, :], b_cols[0:m, i, :], ALU.mult)
            last.then_inc(conv_ready.sem, 1)
            dve.wait_ge(turned.sem, turned.at(3))
            for t in range(TT):
                dve.tensor_copy(y[:, t, A_W:A_W + B_W], rows_b[t])

        self.products(jobs, banks=BANKS, by_vector=by_vector, funcs=funcs,
                      beside={"sync": loads, "tensor": tensor, "scalar": scalar, "gpsimd": gpsimd, "vector": vector})
        side.over(16 * 5)
        for s, n in ((affine_ready, TT), (v_ready, 4), (self.pool_step, 4), (var_ready, 4), (turned, 3), (conv_ready, 2),
                     (wsT_ready, 1), (vnorm_ready, TT), (mixed, TT)):
            s.over(n)

    def group_norm_turn(self, y, gain, dst):
        G = D // HEAD
        squared, rstd_ready = self.sig("groups_squared"), self.sig("groups_rstd")
        with ExitStack() as ctx:
            sq = self.tmp(ctx, "sq", [P, TT, D])
            s = self.tmp(ctx, "s", [P, 3, TT, G])
            with self.block() as block:
                @block.sync
                def _(sp):
                    self.run.load_until(sp, self.run.taken + RING)

                @block.scalar
                def _(act):
                    for t in range(TT):
                        act.activation(sq[:, t, :], y[:, t, :], ACT.Square).then_inc(squared.sem, 1)
                    self.take_turned_scalar(act, gain, dst)

                @block.gpsimd
                def _(pool):
                    for t in range(TT):
                        pool.wait_ge(self.vec_step.sem, self.vec_step.at(t + 1))
                        pool.tensor_scalar(s[:, 1, t, :], s[:, 0, t, :], 1.0 / HEAD, EPS, ALU.mult, ALU.add).then_inc(self.pool_step.sem, 1)
                        pool.wait_ge(self.pool_step.sem, self.pool_step.at(t + 1))
                        pool.tensor_tensor(s[:, 2, t, :], s[:, 1, t, :], self.neg_half[:, 0:G], ALU.pow).then_inc(rstd_ready.sem, 1)

                @block.tensor
                def _(pe):
                    self.turn_scaled(pe, y)

                @block.vector
                def _(dve):
                    for t in range(TT):
                        dve.wait_ge(squared.sem, squared.at(t + 1))
                        dve.tensor_reduce(s[:, 0, t, :], sq[:, t, :].rearrange("p (g e) -> p g e", g=G), AX_X, ALU.add).then_inc(self.vec_step.sem, 1)
                    for t in range(TT):
                        dve.wait_ge(rstd_ready.sem, rstd_ready.at(t + 1))
                        v = y[:, t, :].rearrange("p (g e) -> p g e", g=G)
                        dve.tensor_tensor(v, v, s[:, 2, t, :].unsqueeze(2).to_broadcast([P, G, HEAD]), ALU.mult).then_inc(self.rows_scaled.sem, 1)
                    self.take_turned_vector(dve, gain, dst)
        squared.over(TT)
        self.pool_step.over(TT)
        rstd_ready.over(TT)
        self.vec_step.over(TT)
        self.rows_scaled.over(TT)
        self.turned.over(KC)

    def attend(self, heads, o_rows, scale, qT, kT, v, bias=None, sink=None):
        with ExitStack() as ctx:
            s_sb = self.tmp(ctx, "scores", [P, 2, TT, SEQ])
            p_sb = self.tmp(ctx, "probs", [P, 2, TT, SEQ])
            pT = self.tmp(ctx, "probsT", [P, 2, TT, SEQ])
            mx = self.tmp(ctx, "mx", [P, heads, TT])
            nm = self.tmp(ctx, "nm", [P, heads, TT])
            den = self.tmp(ctx, "den", [P, heads, TT])
            rden = self.tmp(ctx, "rden", [P, heads, TT])
            es = self.tmp(ctx, "es", [P, heads, TT])
            ps = self.ps
            sc = [ps[:, b, :].rearrange("p (t m) -> p t m", t=TT) for b in range(2)]
            tp = [ps[:, 2 + b, :].rearrange("p (t m) -> p t m", t=TT) for b in range(2)]
            dh = v(0, 0).shape[1]
            op = [[ps[:, 4 + 2 * b + t, 0:dh] for t in range(TT)] for b in range(2)]
            scores, mxr, probs, turned, pT_ready, o_done, o_stored = (
                self.scores_done, self.max_ready, self.probs_ready, self.probs_turned, self.probsT_ready, self.heads_done, self.head_stored)
            chain = Chain(self.nc.vector, self.vec_step)
            per_tile = TT
            bias_used = self.sig("bias_used")
            sinks = [h for h in range(heads) if sink is not None and sink(h) is not None]
            with self.block() as block:
                @block.sync
                def _(sp):
                    if bias is not None:
                        self.load_gain(sp)
                        bias.load(sp, bias_used)
                    self.run.load_until(sp, self.run.taken + RING)

                @block.tensor
                def _(pe):
                    def score(h):
                        if h >= 2:
                            if bias is None:
                                pe.wait_ge(probs.sem, probs.at(per_tile * (h - 1)))
                            else:
                                pe.wait_ge(bias_used.sem, bias_used.at(h - 1))
                        for t in range(TT):
                            pairs = list(zip(qT(h, t), kT(h)))
                            for i, (q, k) in enumerate(pairs):
                                mm = pe.matmul(sc[h % 2][:, t, :], q, k, start=(i == 0), stop=(i == len(pairs) - 1))
                        mm.then_inc(scores.sem, 1)

                    def turn(h):
                        pe.wait_ge(probs.sem, probs.at(per_tile * (h + 1)))
                        if h >= 2:
                            pe.wait_ge(pT_ready.sem, pT_ready.at(h - 1))
                        for m in range(TT):
                            for t in range(TT):
                                mm = pe.transpose(tp[h % 2][:, m, t * P:(t + 1) * P], p_sb[:, h % 2, t, m * P:(m + 1) * P], self.ident[:])
                        mm.then_inc(turned.sem, 1)

                    score(0)
                    score(1)
                    turn(0)
                    for h in range(heads):
                        if h + 2 < heads:
                            score(h + 2)
                        if h + 1 < heads:
                            turn(h + 1)
                        pe.wait_ge(pT_ready.sem, pT_ready.at(h + 1))
                        if h >= 2:
                            pe.wait_ge(o_stored.sem, o_stored.at(h - 1))
                        for t in range(TT):
                            for m in range(TT):
                                mm = pe.matmul(op[h % 2][t], pT[:, h % 2, m, t * P:(t + 1) * P], v(h, m), start=(m == 0), stop=(m == TT - 1))
                        mm.then_inc(o_done.sem, 1)

                @block.scalar
                def _(act):
                    def exps(h):
                        src = sc[h % 2] if bias is None else s_sb[:, h % 2]
                        act.wait_ge(mxr.sem, mxr.at(h + 1))
                        if h >= 2:
                            act.wait_ge(turned.sem, turned.at(h - 1))
                        for t in range(TT):
                            act.activation(p_sb[:, h % 2, t, :], src[:, t, :], ACT.Exp, bias=nm[:, h, t:t + 1], scale=scale if bias is None else 1.0,
                                           accum_out=den[:, h, t:t + 1]).then_inc(probs.sem, 1)
                        if h in sinks:
                            for t in range(TT):
                                act.activation(es[:, h, t:t + 1], sink(h), ACT.Exp, bias=nm[:, h, t:t + 1]).then_inc(self.sig("sink_exp").sem, 1)

                    exps(0)
                    for h in range(heads):
                        if h + 1 < heads:
                            exps(h + 1)
                        act.wait_ge(turned.sem, turned.at(h + 1))
                        if h >= 2:
                            act.wait_ge(o_done.sem, o_done.at(h - 1))
                        act.activation(pT[:, h % 2], tp[h % 2], ACT.Copy).then_inc(pT_ready.sem, 1)

                @block.vector
                def _(dve):
                    def maximum(h):
                        dve.wait_ge(scores.sem, scores.at(h + 1))
                        src = sc[h % 2]
                        if bias is not None:
                            bias.wait(dve, h)
                            if h >= 2:
                                dve.wait_ge(probs.sem, probs.at(per_tile * (h - 1)))
                            src = s_sb[:, h % 2]
                            dve.scalar_tensor_tensor(src, sc[h % 2], scale, bias.tile(h), ALU.mult, ALU.add).then_inc(bias_used.sem, 1)
                            dve.wait_ge(bias_used.sem, bias_used.at(h + 1))
                        chain.link(dve.tensor_reduce(mx[:, h, :], src, AX_X, ALU.max))
                        if h in sinks:
                            chain.link(dve.tensor_scalar(mx[:, h, :], mx[:, h, :], sink(h), None, ALU.max))
                        dve.tensor_scalar(nm[:, h, :], mx[:, h, :], -scale if bias is None else -1.0, None, ALU.mult).then_inc(mxr.sem, 1)

                    maximum(0)
                    maximum(1)
                    for h in range(heads):
                        if h + 2 < heads:
                            maximum(h + 2)
                        dve.wait_ge(probs.sem, probs.at(per_tile * (h + 1)))
                        if h in sinks:
                            dve.wait_ge(self.sig("sink_exp").sem, self.sig("sink_exp").at(TT * (sinks.index(h) + 1)))
                            chain.link(dve.tensor_tensor(den[:, h, :], den[:, h, :], es[:, h, :], ALU.add))
                        chain.link(dve.reciprocal(rden[:, h, :], den[:, h, :]))
                        dve.wait_ge(o_done.sem, o_done.at(h + 1))
                        for t in range(TT):
                            last = dve.tensor_scalar(o_rows[:, t, h * dh:(h + 1) * dh], op[h % 2][t], rden[:, h, t:t + 1], None, ALU.mult)
                        last.then_inc(o_stored.sem, 1)
            if bias is not None:
                bias_used.over(heads)
            self.vec_step.over(chain.n)
            for s, n in ((scores, heads), (mxr, heads), (probs, per_tile * heads), (turned, heads), (pT_ready, heads), (o_done, heads), (o_stored, heads)):
                s.over(n)
            if sinks:
                self.sig("sink_exp").over(TT * len(sinks))

    def turn_only(self, rows, dst):
        with self.block() as block:
            @block.sync
            def _(sp):
                self.run.load_until(sp, self.run.taken + RING)

            @block.tensor
            def _(pe):
                for c in range(KC):
                    for t in range(TT):
                        last = pe.transpose(self.ps[:, c // 2, (c % 2) * SEQ + t * P:(c % 2) * SEQ + (t + 1) * P],
                                            rows[:, t, c * P:(c + 1) * P], self.ident[:])
                    last.then_inc(self.turned.sem, 1)

            @block.vector
            def _(dve):
                for b in range(0, KC // 2, 2):
                    dve.wait_ge(self.turned.sem, self.turned.at(2 * b + 2))
                    dve.tensor_copy(dst[:, 2 * b:2 * b + 2, :], self.ps[:, b, :].rearrange("p (a s) -> p a s", a=2))

            @block.scalar
            def _(act):
                for b in range(1, KC // 2, 2):
                    act.wait_ge(self.turned.sem, self.turned.at(2 * b + 2))
                    act.activation(dst[:, 2 * b:2 * b + 2, :], self.ps[:, b, :].rearrange("p (a s) -> p a s", a=2), ACT.Copy)
        self.turned.over(KC)

    def cross_attention(self, l, memory, beside=None):
        XH, XD = 4, D // 4
        with ExitStack() as ctx:
            kT = self.tmp(ctx, "kT", [P, KC, SEQ])
            v = self.tmp(ctx, "v", [P, TT, D])
            qT = self.tmp(ctx, "qT", [P, KC, SEQ])
            memory_g = self.tmp(ctx, "memory_g", [P, KC, SEQ])
            with self.block() as block:
                @block.vector
                def _(dve):
                    for c in range(0, KC, 2):
                        dve.tensor_scalar(memory_g[:, c, :], memory[:, c, :], self.col(f"norm_mem_g{l}", c), None, ALU.mult)

                @block.scalar
                def _(act):
                    for c in range(1, KC, 2):
                        act.activation(memory_g[:, c, :], memory[:, c, :], ACT.Copy, scale=self.col(f"norm_mem_g{l}", c))
            jobs = []
            for p in range(4):
                jobs += self.cols_jobs(memory_g, p, 2, kT, 2 * p)
            self.products(jobs, banks=7 if beside else 8, beside=beside)
            with ExitStack() as inner:
                work, close = self.norm_beside(inner, self.h, self.xT, f"norm_x_g{l}", 8)
                self.add_rows(memory_g, 256, v, add=False, beside=work)
                close()
            jobs = []
            for p in range(4):
                jobs += self.cols_jobs(self.xT, p, 2, qT, 2 * p)
            self.products(jobs)
            o = self.tmp(ctx, "o", [P, TT, D])
            self.attend(XH, o, XD ** -0.5,
                        lambda h, t: [qT[:, 2 * h + c, t * P:(t + 1) * P] for c in range(2)],
                        lambda h: [kT[:, 2 * h + c, :] for c in range(2)],
                        lambda h, m: v[:, m, h * XD:(h + 1) * XD])
            self.turn_only(o, self.xT)
        self.add_rows(self.xT, 256, self.h)

    def ffn(self, chunks, gate, up, down, next_run, dst, add):
        s = self.mlp
        n = chunks
        pairs = (n - 2) // 2
        slots = [[self.ring[:, 2 * k + p, 0:KC * CHUNK] for p in range(2)] for k in range(3)]
        gate_w = [x.rearrange("p (c f) -> p c f", c=KC) for x in slots[0]]
        up_w = [x.rearrange("p (c f) -> p c f", c=KC) for x in slots[1]]
        down_w = [x.rearrange("p (c f) -> p c f", c=2) for x in slots[2]]
        ps = self.ps
        gb = [ps[:, p, :] for p in range(2)]
        ub = [ps[:, 2 + p, :] for p in range(2)] if up else gb
        kinds = [(0, gate, gate_w, s["gate_done"])] + ([(1, up, up_w, s["up_done"])] if up else []) + [(2, down, down_w, s["down_done"])]
        with ExitStack() as ctx:
            acted = self.tmp(ctx, "acted", [P, 2, 2 * SEQ])
            hidden = self.tmp(ctx, "hidden", [P, 2, 2, SEQ])
            with self.block() as block:
                @block.sync
                def _(sp):
                    def load(kinds, j, p, first=False):
                        for k, src, w, done in kinds:
                            if not first:
                                sp.wait_ge(done.sem, done.at(j - 1))
                            sp.dma_start(w[p], src(j)).then_inc(s["loaded"][k][p].sem, 16)

                    if self.next_gain is not None:
                        self.load_gain(sp)
                    into, out = kinds[:-1], kinds[-1:]
                    load(into, 0, 0, True)
                    load(into, 1, 1, True)
                    load(out, 0, 0, True)
                    load(into, 2, 0)
                    load(out, 1, 1, True)
                    with sp.Fori(1, pairs) as i:
                        load(into, 2 * i + 1, 1)
                        load(out, 2 * i, 0)
                        load(into, 2 * i + 2, 0)
                        load(out, 2 * i + 1, 1)
                    if n % 2:
                        load(into, n - 2, 1)
                        load(out, n - 3, 0)
                        load(into, n - 1, 0)
                        load(out, n - 2, 1)
                        load(out, n - 1, 0)
                    else:
                        load(into, n - 1, 1)
                        load(out, n - 2, 0)
                        load(out, n - 1, 1)
                    if next_run is not None:
                        next_run.load_until(sp, 2)
                        sp.wait_ge(s["down_done"].sem, s["down_done"].at(n))
                        next_run.load_until(sp, RING)

                @block.tensor
                def _(pe):
                    def in_part(j, p, i=0):
                        arrived = (j - p) // 2 if isinstance(j, int) else i + 1
                        if not (isinstance(j, int) and j < 2):
                            pe.wait_ge(s["hidden_ready"].sem, s["hidden_ready"].at(j - 1))
                        for k, _, w, done in kinds[:-1]:
                            pe.wait_ge(s["loaded"][k][p].sem, s["loaded"][k][p].at(16 * (arrived + 1)))
                            bank = (gb, ub)[k][p]
                            for m in range(2):
                                for c in range(KC):
                                    mm = pe.matmul(bank[:, m * SEQ:(m + 1) * SEQ], w[p][:, c, m * P:(m + 1) * P], self.xT[:, c, :],
                                                   start=(c == 0), stop=(c == KC - 1))
                            mm.then_inc(done.sem, 1)

                    def out_part(j, p, i=0, first=False, last=False):
                        arrived = (j - p) // 2 if isinstance(j, int) else (i if p else i + 1)
                        pe.wait_ge(s["loaded"][2][p].sem, s["loaded"][2][p].at(16 * (arrived + 1)))
                        pe.wait_ge(s["hidden_ready"].sem, s["hidden_ready"].at(j + 1))
                        for f in range(2):
                            for t in range(TT):
                                for half in range(2):
                                    mm = pe.matmul(ps[:, 4 + 2 * t + half, :], hidden[:, p, f, t * P:(t + 1) * P],
                                                   down_w[p][:, f, half * 512:(half + 1) * 512], start=first and f == 0, stop=last and f == 1,
                                                   skip_group_check=True)
                        mm.then_inc(s["down_done"].sem, 1)

                    in_part(0, 0)
                    in_part(1, 1)
                    out_part(0, 0, first=True)
                    with pe.Fori(0, pairs) as i:
                        in_part(2 * i + 2, 0, i)
                        out_part(2 * i + 1, 1, i)
                        in_part(2 * i + 3, 1, i)
                        out_part(2 * i + 2, 0, i)
                    if n % 2:
                        in_part(n - 1, 0)
                        out_part(n - 2, 1)
                    out_part(n - 1, (n - 1) % 2, last=True)

                @block.scalar
                def _(act):
                    def activate(j, p):
                        act.wait_ge(s["gate_done"].sem, s["gate_done"].at(j + 1))
                        if not (isinstance(j, int) and j < 2):
                            act.wait_ge(s["hidden_ready"].sem, s["hidden_ready"].at(j - 1))
                        act.activation(acted[:, p, :], gb[p], ACT.Silu if up else ACT.Relu).then_inc(s["act_done"].sem, 1)

                    activate(0, 0)
                    activate(1, 1)
                    with act.Fori(0, pairs) as i:
                        activate(2 * i + 2, 0)
                        activate(2 * i + 3, 1)
                    if n % 2:
                        activate(n - 1, 0)

                @block.vector
                def _(dve):
                    def multiply(j, p):
                        dve.wait_ge(s["act_done"].sem, s["act_done"].at(j + 1))
                        if up:
                            dve.wait_ge(s["up_done"].sem, s["up_done"].at(j + 1))
                        if not (isinstance(j, int) and j < 2):
                            dve.wait_ge(s["down_done"].sem, s["down_done"].at(j - 1))
                        dve.tensor_tensor(hidden[:, p].rearrange("p f s -> p (f s)"), acted[:, p, :], ub[p], ALU.mult).then_inc(s["hidden_ready"].sem, 1)

                    multiply(0, 0)
                    multiply(1, 1)
                    with dve.Fori(0, pairs) as i:
                        multiply(2 * i + 2, 0)
                        multiply(2 * i + 3, 1)
                    if n % 2:
                        multiply(n - 1, 0)
                    dve.wait_ge(s["down_done"].sem, s["down_done"].at(n))
                    for t in range(TT):
                        for half in range(2):
                            d = dst[:, t, half * 512:(half + 1) * 512]
                            if add:
                                dve.tensor_tensor(d, d, ps[:, 4 + 2 * t + half, :], ALU.add)
                            else:
                                dve.tensor_copy(d, ps[:, 4 + 2 * t + half, :])
        for k in range(3):
            if k == 1 and not up:
                continue
            s["loaded"][k][0].over(16 * ((n + 1) // 2))
            s["loaded"][k][1].over(16 * (n // 2))
        for name in ("gate_done", "down_done", "act_done", "hidden_ready") + (("up_done",) if up else ()):
            s[name].over(n)
        if next_run is not None:
            self.run = next_run

    def store_rows(self, src):
        with self.block() as block:
            @block.sync
            def _(sp):
                sp.dma_start(self.out.rearrange("a (t p) d -> p (a t) d", p=P), src[:]).then_inc(self.out_stored.sem, 16)
                sp.wait_ge(self.out_stored.sem, self.out_stored.at(16))

    def layer_pieces(self, l):
        I = self.I
        w = I["w_in"][l]
        pieces = by_cols(w[:, 0:2 * A_W], 256)
        for o, m in C_PIECES:
            pieces += by_cols(w[:, 2 * A_W + 3 * B_W + o:2 * A_W + 3 * B_W + o + m], m)
        for part in B_ORDER:
            o = 2 * A_W + part * B_W
            pieces += by_cols(w[:, o:o + 192], 192) + by_cols(w[:, o + 192:o + B_W], 128)
        pieces += by_cols(I["w_mix_out"][l], 256) + by_cols(I["w_xkv"][l], 256)
        return pieces + by_cols(I["w_xq"][l], 256) + by_cols(I["w_xo"][l], 256)

    def ffn_sources(self, gate, up, down):
        def cols(w):
            v = w.rearrange("(c p) f -> p c f", p=P)
            return lambda j: v[:, :, bass.ds(j * CHUNK, CHUNK)]
        d = down.rearrange("(c p) n -> p c n", p=P)
        return cols(gate), cols(up) if up is not None else None, lambda j: d[:, bass.ds(j * 2, 2), :]

    def experts(self, next_run):
        V, K = VIRTUAL, MAX_ITEMS + 1
        with ExitStack() as ctx:
            rows = self.tmp(ctx, "rows", [P, TT, D])
            self.norm_turn(self.h, "norm_ffn_g1", self.xT, keep_rows=rows)
            table = self.tmp(ctx, "table", [P, TT, V, 2])
            items_e = self.tmp(ctx, "items_e", [1, K], I32)
            items_v = self.tmp(ctx, "items_v", [1, K], I32)
            n_items = self.tmp(ctx, "n_items", [1, 1], I32)
            slot_no = self.tmp(ctx, "slot_no", [P, SLOTS])
            with ExitStack() as inner:
                self.route(inner, table, items_e, items_v, n_items, slot_no)
            self.expert_items(ctx, rows, table, items_e, items_v, n_items, slot_no, next_run)
        self.run = next_run

    def route(self, ctx, table, items_e, items_v, n_items, slot_no):
        I, ps = self.I, self.ps
        V, K, E = VIRTUAL, MAX_ITEMS + 1, N_EXPERTS
        tmp = self.tmp
        router = tmp(ctx, "router", [P, KC, E])
        before = tmp(ctx, "before", [P, P])
        v_no = tmp(ctx, "v_no", [1, V])
        e_no = tmp(ctx, "e_no", [1, V])
        k_no = tmp(ctx, "k_no", [1, K, V])
        logits = tmp(ctx, "logits", [P, TT, E])
        top = tmp(ctx, "top", [P, TT, E])
        top_i = tmp(ctx, "top_i", [P, TT, E], U32)
        top_f = tmp(ctx, "top_f", [P, TT, 2])
        first, second, chosen, wts, rank = (tmp(ctx, n, [P, TT, E]) for n in ("first", "second", "chosen", "wts", "rank"))
        gap, ex, den, w1, w2 = (tmp(ctx, n, [P, TT, 1]) for n in ("gap", "ex", "den", "w1", "w2"))
        count = tmp(ctx, "count", [1, E])
        active, upto, key = (tmp(ctx, n, [1, V]) for n in ("active", "upto", "key"))
        match, pickv = (tmp(ctx, n, [1, K, V]) for n in ("match", "pickv"))
        found = tmp(ctx, "found", [1, 2, K])
        logits_done, gap_ready, exp_ready, chosen_ready, ranks_done = (
            self.sig(n) for n in ("logits_done", "gap_ready", "exp_ready", "chosen_ready", "ranks_done"))
        chain = Chain(self.nc.vector, self.vec_step)
        with self.block() as block:
            @block.sync
            def _(sp):
                sp.dma_start(router[:], I["moe_router"][0].rearrange("(c p) e -> p c e", p=P)).then_inc(self.side_loaded.sem, 16)

            @block.gpsimd
            def _(pool):
                pool.iota(slot_no[:], [[1, SLOTS]], base=0, channel_multiplier=0, allow_small_or_imprecise_dtypes=True)
                pool.iota(v_no[:], [[1, V]], base=0, channel_multiplier=0, allow_small_or_imprecise_dtypes=True)
                pool.iota(e_no[:], [[0, MAX_TILES], [1, E]], base=0, channel_multiplier=0, allow_small_or_imprecise_dtypes=True)
                pool.iota(k_no[:], [[1, K], [0, V]], base=0, channel_multiplier=0, allow_small_or_imprecise_dtypes=True)
                pool.affine_select(out=before[:], in_=self.ones[:], compare_op=ALU.is_gt, fill=0.0, base=0,
                                   pattern=[[1, P]], channel_multiplier=-1).then_inc(self.pool_done.sem, 1)

            @block.tensor
            def _(pe):
                pe.wait_ge(self.side_loaded.sem, self.side_loaded.at(16))
                for t in range(TT):
                    for c in range(KC):
                        mm = pe.matmul(ps[:, t, 0:E], self.xT[:, c, t * P:(t + 1) * P], router[:, c, :], start=(c == 0), stop=(c == KC - 1))
                mm.then_inc(logits_done.sem, 1)
                pe.wait_ge(chosen_ready.sem, chosen_ready.at(1))
                pe.wait_ge(self.pool_done.sem, self.pool_done.at(1))
                pe.matmul(ps[:, 2, 0:E], before[:], chosen[:, 0, :], start=True, stop=True)
                pe.matmul(ps[:, 3, 0:E], before[:], chosen[:, 1, :], start=True, stop=False)
                pe.matmul(ps[:, 3, 0:E], self.ones[:], chosen[:, 0, :], start=False, stop=True)
                pe.matmul(ps[0:1, 4, 0:E], self.ones[:, 0:1], chosen[:, 0, :], start=True, stop=False)
                pe.matmul(ps[0:1, 4, 0:E], self.ones[:, 0:1], chosen[:, 1, :], start=False, stop=True).then_inc(ranks_done.sem, 1)

            @block.scalar
            def _(act):
                act.wait_ge(gap_ready.sem, gap_ready.at(1))
                act.activation(ex[:], gap[:], ACT.Exp).then_inc(exp_ready.sem, 1)

            @block.vector
            def _(dve):
                tt, ts, stt, link = dve.tensor_tensor, dve.tensor_scalar, dve.scalar_tensor_tensor, chain.link
                dve.wait_ge(logits_done.sem, logits_done.at(1))
                for t in range(TT):
                    chain.do(dve.tensor_copy(logits[:, t, :], ps[:, t, 0:E]))
                chain.wait()
                for t in range(TT):
                    link(dve.max(top[:, t, :], logits[:, t, :]))
                    link(dve.max_index(top_i[:, t, :], top[:, t, :], logits[:, t, :]))
                link(dve.tensor_copy(top_f[:], top_i[:, :, 0:2]))
                tt(gap[:], top[:, :, 1:2], top[:, :, 0:1], ALU.subtract).then_inc(gap_ready.sem, 1)
                dve.wait_ge(self.pool_done.sem, self.pool_done.at(1))
                for t in range(TT):
                    chain.do(ts(first[:, t, :], slot_no[:, 0:E], top_f[:, t, 0:1], None, ALU.is_equal))
                    chain.do(ts(second[:, t, :], slot_no[:, 0:E], top_f[:, t, 1:2], None, ALU.is_equal))
                chain.wait()
                tt(chosen[:], first[:], second[:], ALU.add).then_inc(chosen_ready.sem, 1)
                dve.wait_ge(exp_ready.sem, exp_ready.at(1))
                link(ts(den[:], ex[:], 1.0, None, ALU.add))
                link(dve.reciprocal(w1[:], den[:]))
                link(tt(w2[:], ex[:], w1[:], ALU.mult))
                for t in range(TT):
                    chain.do(ts(wts[:, t, :], first[:, t, :], w1[:, t], None, ALU.mult))
                chain.wait()
                for t in range(TT):
                    chain.do(stt(wts[:, t, :], second[:, t, :], w2[:, t], wts[:, t, :], ALU.mult, ALU.add))
                dve.wait_ge(ranks_done.sem, ranks_done.at(1))
                for t in range(TT):
                    chain.do(stt(rank[:, t, :], ps[:, 2 + t, 0:E], 1.0, chosen[:, t, :], ALU.add, ALU.mult))
                chain.do(dve.tensor_copy(count[:], ps[0:1, 4, 0:E]))
                chain.wait()
                for k in range(MAX_TILES):
                    chain.do(ts(table[:, :, k * E:(k + 1) * E, 0], rank[:], -1.0 - SLOTS * k, None, ALU.add))
                    chain.do(dve.tensor_copy(table[:, :, k * E:(k + 1) * E, 1], wts[:]))
                    chain.do(ts(active[:, k * E:(k + 1) * E], count[:], float(SLOTS * k) if k else -1.0, None, ALU.is_gt))
                chain.wait()
                link(dve.tensor_tensor_scan(upto[:], self.ones[0:1, 0:V], active[:], 0.0, ALU.mult, ALU.add))
                link(tt(key[:], upto[:], active[:], ALU.mult))
                link(ts(key[:], key[:], -1.0, None, ALU.add))
                link(tt(match[:], key[:].unsqueeze(1).to_broadcast([1, K, V]), k_no[:], ALU.is_equal))
                for n, no in enumerate((e_no, v_no)):
                    link(tt(pickv[:], match[:], no[:].unsqueeze(1).to_broadcast([1, K, V]), ALU.mult))
                    link(dve.tensor_reduce(found[:, n, :], pickv[:], AX_X, ALU.add))
                chain.do(dve.tensor_copy(items_e[:], found[:, 0, :]))
                chain.do(dve.tensor_copy(items_v[:], found[:, 1, :]))
                chain.do(dve.tensor_copy(n_items[:], upto[:, V - 1:V]))
        self.side_loaded.over(16)
        self.pool_done.over(1)
        self.vec_step.over(chain.n)
        for s in (logits_done, gap_ready, exp_ready, chosen_ready, ranks_done):
            s.over(1)

    def expert_items(self, ctx, rows, table, items_e, items_v, n_items, slot_no, next_run):
        I, ps, s = self.I, self.ps, self.moe
        K, V, E = MAX_ITEMS, VIRTUAL, N_EXPERTS
        n = I["moe_w_gate"].shape[3] // CHUNK
        assert n % 2 == 0
        per, pairs = n // 2, (n - 2) // 2
        tmp = self.tmp
        cur = tmp(ctx, "cur", [P, TT, 1, 2])
        pick = tmp(ctx, "pick", [P, TT, SLOTS])
        pick_w = tmp(ctx, "pick_w", [P, TT, SLOTS])
        pickT = tmp(ctx, "pickT", [SLOTS, TT, P])
        xg = tmp(ctx, "xg", [P, KC, SLOTS])
        acted = tmp(ctx, "acted", [P, 2, 2 * SLOTS])
        hidden = tmp(ctx, "hidden", [P, 2, 2, SLOTS])
        y = tmp(ctx, "y", [SLOTS, D])
        slots = [[self.ring[:, 2 * k + p, 0:KC * CHUNK] for p in range(2)] for k in range(3)]
        w_in = [[x.rearrange("p (c f) -> p c f", c=KC) for x in slots[k]] for k in range(2)]
        w_out = [x.rearrange("p (c f) -> p c f", c=2) for x in slots[2]]
        gate_v = I["moe_w_gate"][0].rearrange("e (c p) f -> e p c f", p=P)
        up_v = I["moe_w_up"][0].rearrange("e (c p) f -> e p c f", p=P)
        down_v = I["moe_w_down"][0].rearrange("e (c p) n -> e p c n", p=P)
        gb = [ps[:, p, 0:2 * SLOTS] for p in range(2)]
        ub = [ps[:, 2 + p, 0:2 * SLOTS] for p in range(2)]
        yb = [ps[0:SLOTS, 4 + half, :] for half in range(2)]
        xb = [ps[:, 6 + b, 0:4 * SLOTS].rearrange("p (c s) -> p c s", c=4) for b in range(2)]
        tb = ps[0:SLOTS, 6, 0:TT * P].rearrange("p (t s) -> p t s", t=TT)
        gate_done, up_done, down_done, act_done, hidden_ready = (s[k] for k in ("gate_done", "up_done", "down_done", "act_done", "hidden_ready"))
        pick_ready, gathered, xg_ready, pick_turned, pickT_ready, y_copied, combined, added = (
            x.sem for x in (self.pick_ready, self.gathered, self.xg_ready, self.pick_turned, self.pickT_ready, self.y_copied, self.combined, self.added))
        loaded = s["loaded"]
        FREE, ADDS = 2, 2 * TT
        step = self.sig("moe_vec_step").sem

        def items(eng):
            return eng.value_load(n_items[0:1, 0:1], min_val=1, max_val=K)

        with self.block() as block:
            @block.sync
            def _(sp):
                self.load_gain(sp)
                count = items(sp)
                with sp.Fori(0, count) as i:
                    e = sp.value_load(items_e[0:1, bass.ds(i, 1)], min_val=0, max_val=E - 1)

                    def load_in(j, p, f):
                        sp.wait_ge(gate_done.sem, j + 1)
                        sp.dma_start(w_in[0][p], gate_v[bass.ds(e, 1), :, :, f].rearrange("a p c f -> p (a c) f")).then_inc(loaded[0][p].sem, 16)
                        sp.wait_ge(up_done.sem, j + 1)
                        sp.dma_start(w_in[1][p], up_v[bass.ds(e, 1), :, :, f].rearrange("a p c f -> p (a c) f")).then_inc(loaded[1][p].sem, 16)

                    def load_out(j, p, c):
                        sp.wait_ge(down_done.sem, j + 1)
                        sp.dma_start(w_out[p], down_v[bass.ds(e, 1), :, c, :].rearrange("a p c f -> p (a c) f")).then_inc(loaded[2][p].sem, 16)

                    J = i * n
                    load_in(J, 0, slice(0, CHUNK))
                    with sp.Fori(0, per - 1) as q:
                        j = i * n + q * 2
                        load_in(j + 1, 1, bass.ds(q * (2 * CHUNK) + CHUNK, CHUNK))
                        load_out(j, 0, bass.ds(q * 4, 2))
                        load_in(j + 2, 0, bass.ds(q * (2 * CHUNK) + 2 * CHUNK, CHUNK))
                        load_out(j + 1, 1, bass.ds(q * 4 + 2, 2))
                    load_in(J + (n - 1), 1, slice((n - 1) * CHUNK, n * CHUNK))
                    load_out(J + (n - 2), 0, slice(2 * n - 4, 2 * n - 2))
                    load_out(J + (n - 1), 1, slice(2 * n - 2, 2 * n))
                next_run.load_until(sp, 2)
                sp.wait_ge(down_done.sem, count * n + FREE)
                next_run.load_until(sp, RING)

            @block.tensor
            def _(pe):
                for sg in (gate_done, up_done, down_done):
                    pe.sem_inc(sg.sem, FREE)

                def gather():
                    for b in range(2):
                        for c in range(4):
                            for t in range(TT):
                                mm = pe.matmul(xb[b][:, c, :], rows[:, t, (4 * b + c) * P:(4 * b + c + 1) * P], pick[:, t, :],
                                               start=(t == 0), stop=(t == TT - 1))
                        mm.then_inc(gathered, 1)

                def combine(t, bank):
                    for half in range(2):
                        pe.matmul(ps[:, bank + half, :], pickT[:, t, :], y[:, half * 512:(half + 1) * 512], start=True, stop=True).then_inc(combined, 1)

                pe.wait_ge(pick_ready, 1)
                gather()
                count = items(pe)
                with pe.Fori(0, count) as i:
                    def in_part(j, p, pair):
                        pe.wait_ge(hidden_ready.sem, j + (FREE - 1))
                        for k, bank, done in ((0, gb, gate_done), (1, ub, up_done)):
                            pe.wait_ge(loaded[k][p].sem, pair * 16 + 16)
                            for m in range(2):
                                for c in range(KC):
                                    mm = pe.matmul(bank[p][:, m * SLOTS:(m + 1) * SLOTS], w_in[k][p][:, c, m * P:(m + 1) * P], xg[:, c, :],
                                                   start=(c == 0), stop=(c == KC - 1))
                            mm.then_inc(done.sem, 1)

                    def out_part(j, p, pair, first=False, last=False):
                        pe.wait_ge(loaded[2][p].sem, pair * 16 + 16)
                        pe.wait_ge(hidden_ready.sem, j + (1 + FREE))
                        for f in range(2):
                            for half in range(2):
                                mm = pe.matmul(yb[half], hidden[:, p, f, :], w_out[p][:, f, half * 512:(half + 1) * 512],
                                               start=first and f == 0, stop=last and f == 1, skip_group_check=True)
                        mm.then_inc(down_done.sem, 1)

                    J, Q = i * n, i * per
                    pe.wait_ge(xg_ready, i * 2 + 2)
                    in_part(J, 0, Q)
                    in_part(J + 1, 1, Q)
                    pe.wait_ge(y_copied, i * 2 + 2)
                    out_part(J, 0, Q, first=True)
                    pe.wait_ge(pickT_ready, i + 1)
                    combine(0, 6)
                    in_part(J + 2, 0, Q + 1)
                    pe.wait_ge(added, i * ADDS + 2)
                    combine(1, 6)
                    out_part(J + 1, 1, Q)
                    in_part(J + 3, 1, Q + 1)
                    pe.wait_ge(added, i * ADDS + 4)
                    for t in range(TT):
                        mm = pe.transpose(tb[:, t, :], pick_w[:, t, :], self.ident[:])
                    mm.then_inc(pick_turned, 1)
                    out_part(J + 2, 0, Q + 1)
                    with pe.Fori(1, pairs) as r:
                        j, q = i * n + r * 2, i * per + r
                        in_part(j + 2, 0, q + 1)
                        out_part(j + 1, 1, q)
                        in_part(j + 3, 1, q + 1)
                        out_part(j + 2, 0, q + 1)
                    pe.wait_ge(pick_ready, i + 2)
                    pe.wait_ge(pickT_ready, i + 2)
                    gather()
                    out_part(J + (n - 1), 1, Q + (per - 1), last=True)
                pe.wait_ge(y_copied, count * 2 + 2)
                combine(0, 0)
                combine(1, 2)

            @block.scalar
            def _(act):
                def take_gathered(value):
                    act.wait_ge(gathered, value)
                    for c in range(4):
                        ins = act.activation(xg[:, 4 + c, :], xb[1][:, c, :], ACT.Copy, scale=self.col("norm_ffn_g1", 4 + c))
                    ins.then_inc(xg_ready, 1)

                take_gathered(2)
                with act.Fori(0, items(act)) as i:
                    with act.Fori(0, per) as r:
                        for p in range(2):
                            j = i * n + r * 2 + p
                            act.wait_ge(gate_done.sem, j + (1 + FREE))
                            act.wait_ge(hidden_ready.sem, j + (FREE - 1))
                            act.activation(acted[:, p, :], gb[p], ACT.Silu).then_inc(act_done.sem, 1)
                    take_gathered(i * 2 + 4)
                    act.wait_ge(down_done.sem, i * n + (n + FREE))
                    act.activation(y[:, 512:D], yb[1], ACT.Copy).then_inc(y_copied, 1)

            @block.vector
            def _(dve):
                def make_pick(at, steps):
                    v = dve.value_load(items_v[0:1, at], min_val=0, max_val=V - 1)
                    dve.tensor_copy(cur[:], table[:, :, bass.ds(v, 1), :]).then_inc(step, 1)
                    dve.wait_ge(step, steps)
                    for t in range(TT):
                        dve.tensor_scalar(pick[:, t, :], slot_no[:], cur[:, t, 0, 0:1], None, ALU.is_equal)
                        ins = dve.tensor_scalar(pick_w[:, t, :], slot_no[:], cur[:, t, 0, 0:1], cur[:, t, 0, 1:2], ALU.is_equal, ALU.mult)
                    ins.then_inc(pick_ready, 1)

                def take_gathered(value):
                    dve.wait_ge(gathered, value)
                    for c in range(4):
                        ins = dve.tensor_scalar(xg[:, c, :], xb[0][:, c, :], self.col("norm_ffn_g1", c), None, ALU.mult)
                    ins.then_inc(xg_ready, 1)

                def add_combined(t, value, bank):
                    for half in range(2):
                        dve.wait_ge(combined, value + half)
                        d = self.h[:, t, half * 512:(half + 1) * 512]
                        dve.tensor_tensor(d, d, ps[:, bank + half, :], ALU.add).then_inc(added, 1)

                dve.sem_inc(hidden_ready.sem, FREE)
                make_pick(slice(0, 1), 1)
                dve.memset(y[:], 0.0).then_inc(y_copied, 2)
                dve.memset(pickT[:], 0.0).then_inc(pickT_ready, 1)
                take_gathered(1)
                count = items(dve)
                with dve.Fori(0, count) as i:
                    def multiply(j, p):
                        dve.wait_ge(act_done.sem, j + 1)
                        dve.wait_ge(up_done.sem, j + (1 + FREE))
                        dve.wait_ge(down_done.sem, j + (FREE - 1))
                        dve.tensor_tensor(hidden[:, p].rearrange("p f s -> p (f s)"), acted[:, p, :], ub[p], ALU.mult).then_inc(hidden_ready.sem, 1)

                    J = i * n
                    multiply(J, 0)
                    multiply(J + 1, 1)
                    add_combined(0, i * ADDS + 1, 6)
                    multiply(J + 2, 0)
                    add_combined(1, i * ADDS + 3, 6)
                    multiply(J + 3, 1)
                    dve.wait_ge(pick_turned, i + 1)
                    dve.tensor_copy(pickT[:], tb).then_inc(pickT_ready, 1)
                    make_pick(bass.ds(i + 1, 1), i + 2)
                    with dve.Fori(2, per) as r:
                        j = i * n + r * 2
                        multiply(j, 0)
                        multiply(j + 1, 1)
                    take_gathered(i * 2 + 3)
                    dve.wait_ge(down_done.sem, i * n + (n + FREE))
                    dve.tensor_copy(y[:, 0:512], yb[0]).then_inc(y_copied, 1)
                add_combined(0, count * ADDS + 1, 0)
                add_combined(1, count * ADDS + 3, 2)

    def add_normed(self, src, dst):
        with ExitStack() as ctx:
            junk = self.tmp(ctx, "junk", [P, D])
            normed = self.tmp(ctx, "normed", [P, TT, D])
            stat = self.tmp(ctx, "stat", [P, 3, TT])
            with self.block() as block:
                @block.sync
                def _(sp):
                    self.run.load_until(sp, self.run.taken + RING)

                @block.scalar
                def _(act):
                    for t in range(TT):
                        self.square_rows(act, junk, src[:, t, :], stat, t)

                @block.gpsimd
                def _(pool):
                    for t in range(TT):
                        self.rstd_of_rows(pool, stat, t)

                @block.vector
                def _(dve):
                    dve.wait_ge(self.gain_loaded.sem, self.gain_loaded.at(16))
                    for t in range(TT):
                        dve.wait_ge(self.rstd_ready.sem, self.rstd_ready.at(t + 1))
                        dve.scalar_tensor_tensor(normed[:, t, :], src[:, t, :], stat[:, 2, t:t + 1], self.gain_row[:], ALU.mult, ALU.mult).then_inc(self.vec_step.sem, 1)
                        dve.wait_ge(self.vec_step.sem, self.vec_step.at(t + 1))
                        dve.tensor_tensor(dst[:, t, :], dst[:, t, :], normed[:, t, :], ALU.add)
        self.gain_loaded.over(16)
        self.squares_summed.over(TT)
        self.pool_step.over(TT)
        self.rstd_ready.over(TT)
        self.vec_step.over(TT)

    def bias_rows(self, ctx):
        I = self.I
        H = 16
        self.bias_line = self.nc.dram_tensor("bias_line", [H, DIST], F32)
        self.bias_many = self.nc.dram_tensor("bias_many", [H, P, DIST], F32)
        loaded, done = self.sig("bias_parts_loaded"), self.sig("bias_made")
        self.bias_written = self.sig("bias_written")
        table = self.tmp(ctx, "table", [32, H])
        of_bucket = self.tmp(ctx, "of_bucket", [32, DIST])
        mask = self.tmp(ctx, "mask", [H, DIST])
        line = self.tmp(ctx, "line", [H, DIST])
        sums = self.ps[0:H, 7, :]

        def sync(sp):
            sp.dma_start(table[:], I["rel_table_2"]).then_inc(loaded.sem, 16)
            sp.dma_start(of_bucket[:], I["bucket_of_distance"]).then_inc(loaded.sem, 16)
            sp.dma_start(mask[:], I["distance_mask"]).then_inc(loaded.sem, 16)
            sp.wait_ge(done.sem, 2)
            sp.dma_start(self.bias_line.ap(), line[:]).then_inc(self.bias_written.sem, 16)
            sp.wait_ge(self.bias_written.sem, 16)
            sp.dma_start(self.bias_many.ap(), self.bias_line.ap().unsqueeze(1).to_broadcast([H, P, DIST])).then_inc(self.bias_written.sem, 16)

        def tensor(pe, n):
            if n == 1:
                pe.wait_ge(loaded.sem, 48)
                pe.matmul(sums, table[:], of_bucket[:], start=True, stop=True).then_inc(done.sem, 1)

        def vector(dve, chain):
            dve.wait_ge(done.sem, 1)
            dve.tensor_tensor(line[:], sums, mask[:], ALU.add).then_inc(done.sem, 1)

        return {"sync": sync, "tensor": tensor, "vector": vector}

    def attention_mixer(self, u):
        I = self.I
        HA, HB = 8, 8
        with ExitStack() as ctx:
            qa, ka, qb = (self.tmp(ctx, n, [P, 4, SEQ]) for n in ("qa", "ka", "qb"))
            kb = self.tmp(ctx, "kb", [P, 2, SEQ])
            va = self.tmp(ctx, "va", [P, TT, HA * HEAD])
            vb = self.tmp(ctx, "vb", [P, TT, 2 * HEAD])
            sinks = self.tmp(ctx, "sinks", [P, HB])
            with ExitStack() as inner:
                swapped = self.tmp(inner, "swapped", [P, KC, 2 * HEAD])
                w_kb = I["attn_w_in_2"][0].rearrange("(c p) n -> p c n", p=P)
                side = self.side_loaded

                def loads(sp):
                    k0 = 2048
                    sp.dma_start(swapped[:, :, 0:HEAD], w_kb[:, :, k0 + HEAD:k0 + 2 * HEAD]).then_inc(side.sem, 16)
                    sp.dma_start(swapped[:, :, HEAD:], w_kb[:, :, k0:k0 + HEAD]).then_inc(side.sem, 16)
                    sp.dma_start(sinks[:], I["attn_sink_2"].broadcast_to([P, HB])).then_inc(side.sem, 16)
                    sp.wait_ge(self.bias_written.sem, 32)

                def side_arrived(pe, n):
                    if n == SWAPPED_JOB - 1:
                        pe.wait_ge(side.sem, side.at(48))

                x = self.xT
                jobs = []
                for dst, p0 in ((qa, 0), (ka, 2)):
                    for p in range(2):
                        jobs += self.cols_jobs(x, p0 + p, 2, dst, 2 * p)
                for p in range(2):
                    for t in range(TT):
                        jobs.append((4 + p, [(lambda w, c=c, t=t: x[:, c, t * P:(t + 1) * P], lambda w, c=c: w[:, c, :]) for c in range(KC)],
                                     va[:, t, p * 256:(p + 1) * 256], False))
                for p in range(2):
                    jobs += self.cols_jobs(x, 6 + p, 2, qb, 2 * p)
                jobs += self.cols_jobs(x, 8, 1, kb, 0)
                SWAPPED_JOB = len(jobs)
                jobs.append((8, [(lambda w, c=c: swapped[:, c, :], lambda w, c=c: x[:, c, :]) for c in range(KC)], kb[:, 1, :], False))
                for t in range(TT):
                    jobs.append((8, [(lambda w, c=c, t=t: x[:, c, t * P:(t + 1) * P], lambda w, c=c: w[:, c, 2 * HEAD:4 * HEAD]) for c in range(KC)],
                                 vb[:, t, :], False))
                self.products(jobs, beside={"sync": loads, "tensor": side_arrived})
                side.over(48)

            def half(h):
                return slice((h % 2) * HEAD, (h % 2 + 1) * HEAD)

            def q_of(h, t):
                src, n = (qa, h) if h < HA else (qb, h - HA)
                return [src[half(n), n // 2, t * P:(t + 1) * P]]

            def k_of(h):
                if h < HA:
                    return [ka[half(h), h // 2, :]]
                n = h - HA
                return [kb[half(n), 0 if n % 2 == n // 4 else 1, :]]

            def v_of(h, m):
                if h < HA:
                    return va[:, m, h * HEAD:(h + 1) * HEAD]
                g = (h - HA) // 4
                return vb[:, m, g * HEAD:(g + 1) * HEAD]

            o = self.tmp(ctx, "o", [P, TT, D])
            bias = Bias(self, self.tmp(ctx, "bias", [P, 4, TT, SEQ]), HA + HB)
            self.attend(HA + HB, o, HEAD ** -0.5, q_of, k_of, v_of, bias=bias,
                        sink=lambda h: None if h < HA else sinks[:, h - HA:h - HA + 1])
            bias.over()
            self.turn_only(o, self.xT)
        self.add_rows(self.xT, 256, u, add=False)

    def second_mlp(self, l, next_run, u):
        I = self.I
        g, _, d = self.ffn_sources(I["mlp_w1_2"][l], None, I["mlp_w2_2"][l])
        self.ffn(I["mlp_w1_2"].shape[2] // CHUNK, g, None, d, next_run, u, False)


class Bias:

    def __init__(self, model, ring, heads):
        self.m, self.ring, self.heads = model, ring, heads
        self.loaded = [model.sig(f"bias_loaded{i}") for i in range(4)]

    def load(self, sp, used):
        for h in range(self.heads):
            if h >= 4:
                sp.wait_ge(used.sem, used.at(h - 3))
            for t in range(TT):
                src = bass.AP(self.m.bias_many.ap().tensor, h * P * DIST + (SEQ - 1) - t * P, [[DIST - 1, P], [1, SEQ]])
                sp.dma_start(self.ring[:, h % 4, t, :], src).then_inc(self.loaded[h % 4].sem, 16)

    def wait(self, eng, h):
        s = self.loaded[h % 4]
        eng.wait_ge(s.sem, s.at(16 * TT * (h // 4 + 1)))

    def tile(self, h):
        return self.ring[:, h % 4]

    def over(self):
        for s in self.loaded:
            s.over(16 * TT * self.heads // 4)


def t5_constants():
    dist = np.arange(DIST) - (SEQ - 1)
    half, exact = 16, 8
    n = np.abs(dist)
    large = exact + (np.log(np.maximum(n, 1).astype(np.float32) / np.float32(exact)) / np.float32(np.log(1024 / exact)) * (half - exact)).astype(np.int32)
    bucket = np.where(dist > 0, half, 0) + np.where(n < exact, n, np.minimum(large, half - 1))
    one_hot = (np.arange(32)[:, None] == bucket[None, :]).astype(np.float32)
    branches = (n <= 64).astype(int) + (dist % 4 == 0) + (dist % 16 == 0)
    a = np.where(branches > 0, np.log(np.maximum(branches, 1)), -1e30)
    b = np.where(n <= 128, 0.0, -1e30)
    return one_hot, np.concatenate([np.tile(a, (8, 1)), np.tile(b, (8, 1))]).astype(np.float32)


KAPPA = float(np.exp(-0.5))
LEVELS = 7


def rwkv_constants():
    r, c = np.arange(P)[:, None], np.arange(P)[None, :]
    keep = []
    for strict, incl in ((c > r, c >= r), (c < r, c <= r)):
        keep.append(np.concatenate([-1.0 * strict, 1.0 * incl, 1.0 * strict, 1.0 * incl], axis=1))
    level = []
    for k in range(LEVELS):
        b = 1 << k
        level.append((r // (2 * b) == c // (2 * b)) & (r // b == c // b + 1))
    level += [m.T for m in level]
    pair = (r // HEAD == c // HEAD)
    row_head = np.arange(D) // HEAD
    heads_of_rows = (np.arange(D // HEAD)[:, None] == row_head[None, :]).astype(np.float32)
    rows_of_heads = np.ascontiguousarray(heads_of_rows.T.reshape(KC, P, D // HEAD).transpose(1, 0, 2))
    return {"kept_places": np.stack(keep).astype(np.float32), "level_places": np.stack(level).astype(np.int32),
            "same_head": pair.astype(np.float32), "heads_of_rows": heads_of_rows, "rows_of_heads": rows_of_heads}


class Rwkv:

    def __init__(self, model):
        self.m = model

    def run(self, u):
        m = self.m
        I, nc = m.I, m.nc
        with ExitStack() as ctx:
            tmp = m.tmp
            r, k = tmp(ctx, "r", [P, KC, SEQ]), tmp(ctx, "k", [P, KC, SEQ])
            v, y = tmp(ctx, "v", [P, TT, D]), u
            g_low = tmp(ctx, "g_low", [P, 2, SEQ])
            with ExitStack() as inner:
                dp, dn = tmp(inner, "dp", [P, KC, SEQ]), tmp(inner, "dn", [P, KC, SEQ])
                mixed = [tmp(inner, f"mixed{i}", [P, KC, SEQ]) for i in range(2)]
                w1, a1 = tmp(inner, "w1", [P, KC, 2, HEAD]), tmp(inner, "a1", [P, KC, 2, HEAD])
                g1 = tmp(inner, "g1", [P, KC, 2, P])
                w2, a2 = tmp(inner, "w2", [P, D]), tmp(inner, "a2", [P, D])
                w_low, a_low = tmp(inner, "w_low", [P, SEQ]), tmp(inner, "a_low", [P, SEQ])
                self.low_loaded = m.sig("low_ranks_loaded")
                side = self.low_loaded
                x = m.xT
                with m.block() as block:
                    @block.sync
                    def _(sp):
                        for d in range(2):
                            for dst, name in ((w1, "rk_w1_2"), (a1, "rk_a1_2"), (g1, "rk_g1_2")):
                                sp.dma_start(dst[:, :, d, :], I[name][0, d].rearrange("(c p) l -> p c l", p=P)).then_inc(side.sem, 16)
                        for dst, name in ((w2, "rk_w2_2"), (a2, "rk_a2_2")):
                            sp.dma_start(dst[:], I[name][0].rearrange("d l n -> (d l) n")).then_inc(side.sem, 16)

                    @block.vector
                    def _(dve):
                        dve.tensor_tensor(dp[:, :, 1:SEQ], x[:, :, 0:SEQ - 1], x[:, :, 1:SEQ], ALU.subtract)
                        dve.tensor_tensor(dn[:, :, 0:SEQ - 1], x[:, :, 1:SEQ], x[:, :, 0:SEQ - 1], ALU.subtract)
                        dve.tensor_scalar(dp[:, :, 0:1], x[:, :, 0:1], -1.0, None, ALU.mult)
                        dve.tensor_scalar(dn[:, :, SEQ - 1:SEQ], x[:, :, SEQ - 1:SEQ], -1.0, None, ALU.mult)

                def mixing(n, dst):
                    def steps(dve, chain):
                        for c in range(KC):
                            chain.do(dve.scalar_tensor_tensor(dst[:, c, :], dp[:, c, :], m.col(f"mu_prev{n}", c), x[:, c, :], ALU.mult, ALU.add))
                        for c in range(KC):
                            chain.wait(chain.n - KC + 1)
                            chain.do(dve.scalar_tensor_tensor(dst[:, c, :], dn[:, c, :], m.col(f"mu_next{n}", c), dst[:, c, :], ALU.mult, ALU.add))
                    return steps

                chain = Chain(nc.vector, m.vec_step)
                with m.block() as block:
                    @block.vector
                    def _(dve):
                        mixing(0, mixed[0])(dve, chain)
                m.vec_step.over(chain.n)

                def cols_products(src, dst, extra):
                    jobs = []
                    for p in range(4):
                        jobs += m.cols_jobs(src, p, 2, dst, 2 * p)
                    m.products(jobs, extra)

                cols_products(mixed[0], r, mixing(2, mixed[1]))
                cols_products(mixed[1], k, mixing(3, mixed[0]))
                m.add_rows(mixed[0], 256, v, add=False, extra=mixing(1, mixed[1]))
                self.sig_w = [m.ring[:, s, :].rearrange("p (c s) -> p c s", c=KC) for s in (6, 7)]
                self.rate = [m.ring[:, s, :].rearrange("p (c s) -> p c s", c=KC) for s in (0, 1)]
                self.low_rank(mixed[1], w1, w_low, ACT.Tanh, w2, "w0", self.sig_w, mixing(4, mixed[0]))
                self.low_rank(mixed[0], a1, a_low, ACT.Copy, a2, "a0", self.rate, mixing(5, mixed[1]))
                self.gate_low(mixed[1], g1, g_low)
            kk = m.xT
            self.normed_keys(k, kk)
            with ExitStack() as inner:
                self.chunks(inner, r, k, kk, v, g_low, y)
            m.turn_only(y, m.xT)
        m.add_rows(m.xT, 256, u, add=False)

    def low_rank(self, x, w1, low, func, w2, bias, dst, extra):
        m = self.m
        ps = m.ps
        low_done, low_ready, done, taken = (m.sig(n) for n in ("low_done", "low_ready", "rank_done", "rank_taken"))
        chain = Chain(m.nc.vector, m.vec_step)
        with m.block() as block:
            @block.tensor
            def _(pe):
                pe.wait_ge(self.low_loaded.sem, self.low_loaded.at(16 * 8))
                for c in range(KC):
                    mm = pe.matmul(ps[:, 0, 0:SEQ], w1[:, c].rearrange("p d l -> p (d l)"), x[:, c, :], start=(c == 0), stop=(c == KC - 1))
                mm.then_inc(low_done.sem, 1)
                pe.wait_ge(low_ready.sem, low_ready.at(1))
                for n in range(2 * KC):
                    d, c = n // KC, n % KC
                    if n >= 6:
                        pe.wait_ge(taken.sem, taken.at(n - 5))
                    h = slice(d * HEAD, (d + 1) * HEAD)
                    pe.matmul(ps[:, 2 + n % 6, 0:SEQ], w2[h, c * P:(c + 1) * P], low[h, :], start=True, stop=True).then_inc(done.sem, 1)

            @block.scalar
            def _(act):
                act.wait_ge(low_done.sem, low_done.at(1))
                act.activation(low[:], ps[:, 0, 0:SEQ], func).then_inc(low_ready.sem, 1)
                for n in range(2 * KC):
                    d, c = n // KC, n % KC
                    act.wait_ge(done.sem, done.at(n + 1))
                    act.activation(dst[d][:, c, :], ps[:, 2 + n % 6, 0:SEQ], ACT.Sigmoid, bias=m.col(f"{bias}{d}", c)).then_inc(taken.sem, 1)

            @block.vector
            def _(dve):
                extra(dve, chain)
        m.vec_step.over(chain.n)
        low_done.over(1)
        low_ready.over(1)
        done.over(2 * KC)
        taken.over(2 * KC)

    def gate_low(self, x, g1, low):
        m = self.m
        done = m.sig("gate_low_done")
        with m.block() as block:
            @block.tensor
            def _(pe):
                for d in range(2):
                    for c in range(KC):
                        mm = pe.matmul(m.ps[:, d, 0:SEQ], g1[:, c, d, :], x[:, c, :], start=(c == 0), stop=(c == KC - 1))
                    mm.then_inc(done.sem, 1)

            @block.scalar
            def _(act):
                for d in range(2):
                    act.wait_ge(done.sem, done.at(d + 1))
                    act.activation(low[:, d, :], m.ps[:, d, 0:SEQ], ACT.Sigmoid)
        done.over(2)

    def normed_keys(self, k, kk):
        m = self.m
        ps = m.ps
        H = D // HEAD
        raw, squared, summed, rooted, inverted, spread = (
            m.sig(n) for n in ("keys_raw", "keys_squared", "keys_summed", "keys_rooted", "keys_inverted", "keys_spread"))
        chain = Chain(m.nc.vector, m.vec_step)
        with ExitStack() as ctx:
            sq = m.tmp(ctx, "sq", [P, KC, SEQ])
            scale = m.tmp(ctx, "scale", [H, SEQ])
            into = m.tmp(ctx, "into_heads", [P, KC, H])
            outof = m.tmp(ctx, "out_of_heads", [H, D])
            with m.block() as block:
                @block.sync
                def _(sp):
                    sp.dma_start(into[:], m.I["rows_of_heads"]).then_inc(m.side_loaded.sem, 16)
                    sp.dma_start(outof[:], m.I["heads_of_rows"]).then_inc(m.side_loaded.sem, 16)

                @block.tensor
                def _(pe):
                    pe.wait_ge(m.side_loaded.sem, m.side_loaded.at(32))
                    for c in range(KC):
                        pe.wait_ge(squared.sem, squared.at(c + 1))
                        mm = pe.matmul(ps[0:H, 0, 0:SEQ], into[:, c, :], sq[:, c, :], start=(c == 0), stop=(c == KC - 1))
                    mm.then_inc(summed.sem, 1)
                    pe.wait_ge(inverted.sem, inverted.at(1))
                    for c in range(KC):
                        pe.matmul(ps[:, c, 0:SEQ], outof[:, c * P:(c + 1) * P], scale[:], start=True, stop=True).then_inc(spread.sem, 1)

                @block.scalar
                def _(act):
                    for c in range(KC):
                        act.wait_ge(raw.sem, raw.at(c + 1))
                        act.activation(sq[:, c, :], kk[:, c, :], ACT.Square).then_inc(squared.sem, 1)
                    act.wait_ge(summed.sem, summed.at(1))
                    act.activation(scale[:], ps[0:H, 0, 0:SEQ], ACT.Sqrt).then_inc(rooted.sem, 1)

                @block.vector
                def _(dve):
                    for c in range(KC):
                        dve.tensor_scalar(kk[:, c, :], k[:, c, :], m.col("k_k", c), None, ALU.mult).then_inc(raw.sem, 1)
                    dve.wait_ge(rooted.sem, rooted.at(1))
                    chain.link(dve.tensor_scalar(scale[:], scale[:], 1e-12, None, ALU.max))
                    dve.reciprocal(scale[:], scale[:]).then_inc(inverted.sem, 1)
                    dve.wait_ge(squared.sem, squared.at(KC))
                    for c in range(KC):
                        dve.wait_ge(spread.sem, spread.at(c + 1))
                        dve.tensor_tensor(kk[:, c, :], kk[:, c, :], ps[:, c, 0:SEQ], ALU.mult)
        m.side_loaded.over(32)
        m.vec_step.over(chain.n)
        for s, n in ((raw, KC), (squared, KC), (summed, 1), (rooted, 1), (inverted, 1), (spread, KC)):
            s.over(n)

    def chunks(self, ctx, r, k, kk, v, g_low, y):
        m = self.m
        I, ps = m.I, m.ps
        tmp, sig = m.tmp, m.sig
        keep = tmp(ctx, "keep", [P, 2, 4 * P])
        level = tmp(ctx, "level", [P, 2 * LEVELS, P], I32)
        same = tmp(ctx, "same", [P, P])
        head_of = same[:].rearrange("p (h e) -> p h e", h=2)[:, :, 0]
        gn = tmp(ctx, "gn", [P, 2, D])
        g2 = tmp(ctx, "g2", [P, 2, P])
        cc = tmp(ctx, "cc", [P, 2])
        vc = tmp(ctx, "vc", [P, TT, P])
        S, X, Y = (tmp(ctx, n, [P, TT, P]) for n in "SXY")
        MT = tmp(ctx, "MT", [P, 4])
        eK, eR, eB = (tmp(ctx, n, [P, TT, P]) for n in ("eK", "eR", "eB"))
        kd, bb, fa = (tmp(ctx, n, [P, TT, P]) for n in ("kd", "bb", "fa"))
        WIDTH = TT * 2 * P
        made = [tmp(ctx, "made", [P, WIDTH + 4]) for _ in range(2)]
        used = [tmp(ctx, "used", [P, WIDTH + 4]) for _ in range(2)]
        KRn, KR = ([x[:, 0:WIDTH].rearrange("p (t k s) -> p t k s", t=TT, k=2) for x in xs] for xs in (made, used))
        ends = [x[:, WIDTH:] for x in used]
        Bs = [tmp(ctx, "Bs", [P, TT, P]) for _ in range(2)]
        Ks = [tmp(ctx, "Ks", [P, TT, P]) for _ in range(2)]
        rkd = [tmp(ctx, "rkd", [P, TT, P]) for _ in range(2)]
        GM = [tmp(ctx, "GM", [P, 4, 4, P]) for _ in range(2)]
        M1 = [tmp(ctx, "M1", [P, 4, P]) for _ in range(2)]
        Xi = [tmp(ctx, "Xi", [P, 4, P]) for _ in range(2)]
        XT = [tmp(ctx, "XT", [P, 4, P]) for _ in range(2)]
        Pb = M1
        rowsBK = [tmp(ctx, "rowsBK", [P, 2, P]) for _ in range(2)]
        rhs = [tmp(ctx, "rhs", [P, 2, HEAD]) for _ in range(2)]
        sa = [tmp(ctx, "sa", [P, TT, 2, HEAD]) for _ in range(2)]
        S0 = [tmp(ctx, "S0", [P, 2, HEAD]) for _ in range(2)]
        o = [tmp(ctx, "o", [P, TT * P]) for _ in range(2)]
        gb = [tmp(ctx, "gb", [P, TT * P + 4]) for _ in range(2)]
        st = [tmp(ctx, "st", [P, 4, 6]) for _ in range(2)]
        mv = [tmp(ctx, "mv", [P, 4, 2]) for _ in range(2)]
        rs = [tmp(ctx, "rs", [P, 2, 4]) for _ in range(2)]
        gn_eps = tmp(ctx, "gn_eps", [P, 4])

        N = {"shift_ready": 2, "exps_ready": 2, "made_ready": 2, "keys_ready": 2, "vc_ready": 1, "products_done": 8, "m1_done": 2,
             "rows_done": 2, "kept_ready": 2, "xi_ready": 2 * (LEVELS - 1), "x_ready": 2 * LEVELS, "rows_ready": 2, "half_done": 2 * (LEVELS - 1),
             "half_ready": 2 * (LEVELS - 1), "step_done": 2 * (LEVELS - 1), "rhs_done": 4, "rhs_ready": 4, "sa_done": 4, "sa_ready": 4,
             "state_done": 2, "s0_ready": 2, "out_done": 2, "out_ready": 2, "gates_done": 2, "gates_ready": 2, "var_ready": 2,
             "gn_rstd": 2, "output_over": 2, "slice_loaded": 32, "x_begun": 2, "start_step": 2 * 2, "factor_step": 2 + 2 * 8, "output_step": 2 * 5 + 1,
             "rstd_step": 2}
        q = {n: sig("rwkv_" + n) for n in N}
        step_begun = sig("rwkv_step_begun")
        pairs = D // P
        GATES_AT = 4
        with m.block() as block:
            @block.sync
            def _(sp):
                m.load_gain(sp)
                sp.dma_start(keep[:], I["kept_places"].rearrange("d p n -> p d n")).then_inc(m.side_loaded.sem, 16)
                sp.dma_start(level[:], I["level_places"].rearrange("d p n -> p d n")).then_inc(m.side_loaded.sem, 16)
                sp.dma_start(same[:], I["same_head"]).then_inc(m.side_loaded.sem, 16)
                for n, name in enumerate(("rk_gn_w_2", "rk_gn_b_2")):
                    sp.dma_start(gn[:, n, :], I[name][0:1, :].broadcast_to([P, D])).then_inc(m.side_loaded.sem, 16)
                sp.wait_ge(m.side_loaded.sem, m.side_loaded.at(80))

            @block.vector
            def _(dve):
                for d in range(2):
                    dve.memset(S0[d][:], 0.0)
                dve.memset(gn_eps[:], GN_EPS)
        m.side_loaded.over(80)

        def wait(eng, n, i, k):
            eng.wait_ge(q[n].sem, i * N[n] + k)

        def all_pairs(eng, pair):
            pair(0, first=True)
            with eng.Fori(1, pairs - 1) as i:
                pair(i)
            pair(pairs - 1, last=True)

        def half(hh):
            return slice(hh * HEAD, (hh + 1) * HEAD)

        def columns(i):
            return bass.ds(i * P, P)

        with m.block() as block:
            @block.sync
            def _(sp):
                m.run.load_until(sp, m.run.taken + 4)
                g2_src = I["rk_g2_2"][0].rearrange("d l n -> l d n")

                def pair(i, first=False, last=False):
                    if not first:
                        wait(sp, "gates_done", i - 1, 2)
                    for d in range(2):
                        sp.dma_start(g2[:, d, :], g2_src[:, d, columns(i)]).then_inc(q["slice_loaded"].sem, 16)

                all_pairs(sp, pair)

            @block.gpsimd
            def _(pool):
                def rstd(j):
                    for d in range(2):
                        wait(pool, "var_ready", j, d + 1)
                        pool.tensor_tensor(rs[d][:, 0, :], mv[d][:, :, 1], gn_eps[:], ALU.add).then_inc(q["rstd_step"].sem, 1)
                        wait(pool, "rstd_step", j, d + 1)
                        pool.tensor_tensor(rs[d][:, 1, :], rs[d][:, 0, :], m.neg_half[:, 0:4], ALU.pow).then_inc(q["gn_rstd"].sem, 1)

                def pair(i, first=False, last=False):
                    if not first:
                        wait(pool, "out_done", i - 1, 2)
                    pool.tensor_copy(vc[:], v[:, :, columns(i)]).then_inc(q["vc_ready"].sem, 1)
                    if not first:
                        rstd(i - 1)

                all_pairs(pool, pair)
                rstd(pairs - 1)

            @block.scalar
            def _(act):
                def exps(j, d):
                    wait(act, "shift_ready", j, d + 1)
                    if d:
                        wait(act, "made_ready", j, 1)
                    act.activation(eK[:], (X if d else Y)[:], ACT.Exp, scale=KAPPA if d else -KAPPA)
                    act.activation(eR[:], (Y if d else X)[:], ACT.Exp, scale=KAPPA if d else -KAPPA)
                    act.activation(eB[:], (Y if d else X)[:], ACT.Exp, scale=-KAPPA if d else KAPPA)
                    act.activation(made[d][:, WIDTH:], MT[:], ACT.Exp, scale=-KAPPA).then_inc(q["exps_ready"].sem, 1)

                def use(j, d):
                    wait(act, "made_ready", j, d + 1)
                    act.activation(used[d][:], made[d][:], ACT.Copy).then_inc(q["keys_ready"].sem, 1)

                def pair(i, first=False, last=False):
                    for d in range(2):
                        act.activation(Xi[d][:], m.ident[:].unsqueeze(1).to_broadcast([P, 4, P]), ACT.Copy)
                        act.activation(XT[d][:], m.ident[:].unsqueeze(1).to_broadcast([P, 4, P]), ACT.Copy).then_inc(q["x_begun"].sem, 1)
                    for d in range(2):
                        wait(act, "rows_done", i, d + 1)
                        act.activation(rowsBK[d][:], ps[:, 4 * d + 3, 0:2 * P].rearrange("p (a b) -> p a b", a=2), ACT.Copy).then_inc(q["rows_ready"].sem, 1)
                    for k in range(1, LEVELS):
                        for d in range(2):
                            wait(act, "half_done", i, 2 * (k - 1) + d + 1)
                            act.activation(Pb[d][:].rearrange("p a b -> p (a b)"), ps[:, 4 * d, :], ACT.Copy).then_inc(q["half_ready"].sem, 1)
                        if k == GATES_AT:
                            for d in range(2):
                                wait(act, "gates_done", i, d + 1)
                                if not first:
                                    wait(act, "output_over", i - 1, d + 1)
                                act.activation(gb[d][:], ps[:, 4 * d + 3, 0:2 * P + 4], ACT.Copy).then_inc(q["gates_ready"].sem, 1)
                            if not last:
                                exps(i + 1, 0)
                    if not last:
                        exps(i + 1, 1)
                    for step in range(2):
                        for d in range(2):
                            n = 2 * step + d
                            wait(act, "rhs_done", i, n + 1)
                            act.activation(rhs[d][:].rearrange("p a b -> p (a b)"), ps[:, 4 * d, 0:P], ACT.Copy, scale=-1.0).then_inc(q["rhs_ready"].sem, 1)
                        for d in range(2):
                            n = 2 * step + d
                            t = d if step == 0 else 1 - d
                            wait(act, "sa_done", i, n + 1)
                            act.activation(sa[d][:, t].rearrange("p a b -> p (a b)"), ps[:, 4 * d + 1, 0:P], ACT.Copy).then_inc(q["sa_ready"].sem, 1)
                    for d in range(2):
                        wait(act, "out_done", i, d + 1)
                        if not first:
                            wait(act, "output_over", i - 1, d + 1)
                        act.activation(o[d][:], ps[:, 4 * d + 2, 0:2 * P], ACT.Copy).then_inc(q["out_ready"].sem, 1)
                        if not last:
                            use(i + 1, d)

                for d in range(2):
                    exps(0, d)
                    use(0, d)
                all_pairs(act, pair)

            @block.tensor
            def _(pe):
                def pair(i, first=False, last=False):
                    for d in range(2):
                        wait(pe, "keys_ready", i, d + 1)
                        for t in range(TT):
                            for hh in range(2):
                                both = KR[d][half(hh), t].rearrange("p a b -> p (a b)")
                                b = ps[:, 4 * d + 2 * t + hh, :]
                                pe.matmul(b[:, 0:2 * P], Bs[d][half(hh), t, :], both, start=True, stop=True)
                                pe.matmul(b[:, 2 * P:4 * P], Ks[d][half(hh), t, :], both, start=True, stop=True).then_inc(q["products_done"].sem, 1)
                    for d in range(2):
                        wait(pe, "kept_ready", i, d + 1)
                        for t in range(TT):
                            for hh in range(2):
                                mm = pe.matmul(ps[:, 4 * d + hh, t * P:(t + 1) * P], KR[d][half(hh), t, 0, :], Bs[d][half(hh), t, :], start=True, stop=True)
                        mm.then_inc(q["m1_done"].sem, 1)
                        for n, src in enumerate((Bs, Ks)):
                            mm = pe.transpose(ps[:, 4 * d + 3, n * P:(n + 1) * P], src[d][:, d, :], m.ident[:])
                        mm.then_inc(q["rows_done"].sem, 1)
                    for k in range(1, LEVELS):
                        for d in range(2):
                            wait(pe, "xi_ready", i, 2 * (k - 1) + d + 1)
                            for n in range(4):
                                mm = pe.matmul(ps[:, 4 * d, n * P:(n + 1) * P], GM[d][:, n, 0, :], Xi[d][:, n, :], start=True, stop=True)
                            mm.then_inc(q["half_done"].sem, 1)
                        if k == GATES_AT:
                            wait(pe, "slice_loaded", i, 32)
                            for d in range(2):
                                wait(pe, "rows_ready", i, d + 1)
                                for t in range(TT):
                                    pe.matmul(ps[:, 4 * d + 3, t * P:(t + 1) * P], g_low[:, d, t * P:(t + 1) * P], g2[:, d, :], start=True, stop=True)
                                    mm = pe.matmul(ps[:, 4 * d + 3, 2 * P + 2 * t:2 * P + 2 * t + 2], rkd[d][:, t, :], head_of, start=True, stop=True)
                                mm.then_inc(q["gates_done"].sem, 1)
                        for d in range(2):
                            wait(pe, "half_ready", i, 2 * (k - 1) + d + 1)
                            wait(pe, "x_ready", i, 2 * (k - 1) + d + 1)
                            if k < LEVELS - 1:
                                for n in range(4):
                                    pe.matmul(ps[:, 4 * d + 1, n * P:(n + 1) * P], XT[d][:, n, :], Pb[d][:, n, :], start=True, stop=True)
                            for n in range(4):
                                mm = pe.matmul(ps[:, 4 * d + 2, n * P:(n + 1) * P], Pb[d][:, n, :], XT[d][:, n, :], start=True, stop=True)
                            mm.then_inc(q["step_done"].sem, 1)
                    wait(pe, "vc_ready", i, 1)
                    for step in range(2):
                        for d in range(2):
                            t = d if step == 0 else 1 - d
                            if step == 0:
                                wait(pe, "x_ready", i, 2 * (LEVELS - 1) + d + 1)
                            else:
                                wait(pe, "s0_ready", i, d + 1)
                                pe.matmul(ps[:, 4 * d, 0:P], KR[d][:, t, 0, :], S0[d][:].rearrange("p a b -> p (a b)"), start=True, stop=False)
                            for hh in range(2):
                                mm = pe.matmul(ps[:, 4 * d, hh * HEAD:(hh + 1) * HEAD], GM[d][:, 2 * t + hh, 2, :], vc[:, t, half(hh)],
                                               start=(step == 0), stop=(step == 0 or hh == 1))
                            mm.then_inc(q["rhs_done"].sem, 1)
                        for d in range(2):
                            t = d if step == 0 else 1 - d
                            wait(pe, "rhs_ready", i, 2 * step + d + 1)
                            for hh in range(2):
                                mm = pe.matmul(ps[:, 4 * d + 1, hh * HEAD:(hh + 1) * HEAD], XT[d][:, 2 * t + hh, :], rhs[d][:, hh, :], start=True, stop=True)
                            mm.then_inc(q["sa_done"].sem, 1)
                        for d in range(2):
                            t = d if step == 0 else 1 - d
                            wait(pe, "sa_ready", i, 2 * step + d + 1)
                            if step == 0:
                                wait(pe, "gates_ready", i, d + 1)
                                for hh in range(2):
                                    dst = ps[:, 4 * d + 3, 256 + hh * HEAD:256 + (hh + 1) * HEAD]
                                    pe.matmul(dst, rowsBK[d][:, 0, :], sa[d][:, t, hh, :], start=True, stop=False)
                                    mm = pe.matmul(dst, rowsBK[d][:, 1, :], vc[:, t, half(hh)], start=False, stop=True)
                                mm.then_inc(q["state_done"].sem, 1)
                            if step:
                                pe.matmul(ps[:, 4 * d + 2, t * P:(t + 1) * P], KR[d][:, t, 1, :], S0[d][:].rearrange("p a b -> p (a b)"), start=True, stop=False)
                            for hh in range(2):
                                dst = ps[:, 4 * d + 2, (2 * t + hh) * HEAD:(2 * t + hh + 1) * HEAD]
                                pe.matmul(dst, GM[d][:, 2 * t + hh, 1, :], sa[d][:, t, hh, :], start=(step == 0), stop=False)
                                mm = pe.matmul(dst, GM[d][:, 2 * t + hh, 3, :], vc[:, t, half(hh)], start=False, stop=(step == 0 or hh == 1))
                            if step:
                                mm.then_inc(q["out_done"].sem, 1)

                all_pairs(pe, pair)

            @block.vector
            def _(dve):
                tt, ts, stt = dve.tensor_tensor, dve.tensor_scalar, dve.scalar_tensor_tensor

                class Steps:

                    def __init__(self, name, j):
                        self.name, self.j, self.n = name, j, 0

                    def do(self, ins):
                        self.n += 1
                        ins.then_inc(q[self.name].sem, 1)

                    def link(self, ins=None):
                        if ins is not None:
                            self.do(ins)
                        wait(dve, self.name, self.j, self.n)

                def begin_step():
                    dve.sem_inc(step_begun.sem, 1)

                def factors(j, first=False):
                    s = Steps("factor_step", j)
                    do, link = s.do, s.link
                    one = bass.ds(j, 1)
                    do(dve.tensor_copy(cc[:, 0:1], m.cols[:, m.col_at["k_a"][0], bass.ds(j + m.col_at["k_a"][1], 1)]))
                    link(dve.tensor_copy(cc[:, 1:2], m.cols[:, m.col_at["r_k"][0], bass.ds(j + m.col_at["r_k"][1], 1)]))
                    kc, kkc, rc = (z[:, one, :].rearrange("p a (t s) -> p (a t) s", t=TT) for z in (k, kk, r))
                    for d in range(2):
                        sg = self.sig_w[d][:, one, :].rearrange("p a (t s) -> p (a t) s", t=TT)
                        rate = self.rate[d][:, one, :].rearrange("p a (t s) -> p (a t) s", t=TT)
                        if d:
                            wait(dve, "exps_ready", j, 1)
                        for t in range(TT):
                            do(dve.tensor_tensor_scan(S[:, t, :], m.ones[:], self.sig_w[d][:, one, t * P:(t + 1) * P].rearrange("p a s -> p (a s)"), 0.0, ALU.mult, ALU.add))
                        link()
                        mid = S[:, :, P // 2 - 1:P // 2]
                        do(dve.tensor_copy(MT[:, 0:2], mid.rearrange("p t a -> p (t a)")))
                        do(tt(MT[:, 2:4].unsqueeze(2), S[:, :, P - 1:P], mid, ALU.subtract))
                        do(tt(X[:], S[:], mid.to_broadcast([P, TT, P]), ALU.subtract))
                        link()
                        tt(Y[:], X[:], sg, ALU.subtract).then_inc(q["shift_ready"].sem, 1)
                        yield
                        link(ts(fa[:], rate, -1.0, cc[:, 0:1], ALU.add, ALU.mult))
                        do(stt(kd[:], fa[:], 1.0, kc, ALU.add, ALU.mult))
                        link(tt(bb[:], kkc, rate, ALU.mult))
                        if not first:
                            wait(dve, "gates_done", j - 1, d + 1)
                        stt(rkd[d][:], rc, cc[:, 1:2], kd[:], ALU.mult, ALU.mult)
                        wait(dve, "exps_ready", j, d + 1)
                        tt(KRn[d][:, :, 0, :], kkc, eK[:], ALU.mult)
                        tt(KRn[d][:, :, 1, :], rc, eR[:], ALU.mult)
                        tt(Bs[d][:], bb[:], eB[:], ALU.mult)
                        tt(Ks[d][:], kd[:], eB[:], ALU.mult).then_inc(q["made_ready"].sem, 1)
                        if d == 0:
                            wait(dve, "made_ready", j, 1)
                        yield
                    assert s.n == N["factor_step"], s.n

                def output(j):
                    s = Steps("output_step", j)
                    link = s.link
                    yc = y[:, :, columns(j)]
                    for d in range(2):
                        wait(dve, "out_ready", j, d + 1)
                        ov = o[d][:].rearrange("p (n e) -> p n e", n=4)
                        for n in range(4):
                            ins = dve.bn_stats(st[d][:, n, :], ov[:, n, :])
                        link(ins)
                        begin_step()
                        for n in range(4):
                            ins = dve.bn_aggr(mv[d][:, n, :], st[d][:, n, :])
                        ins.then_inc(q["var_ready"].sem, 1)
                        yield
                    for d in range(2):
                        wait(dve, "gn_rstd", j, d + 1)
                        ov = o[d][:].rearrange("p (n e) -> p n e", n=4)
                        for n in range(4):
                            ins = ts(ov[:, n, :], ov[:, n, :], mv[d][:, n, 0:1], rs[d][:, 1, n:n + 1], ALU.subtract, ALU.mult)
                        link(ins)
                        o2 = o[d][:].rearrange("p (t e) -> p t e", t=TT)
                        link(tt(o2, o2, gn[:, 0:1, columns(j)].to_broadcast([P, TT, P]), ALU.mult))
                        link(tt(o2, o2, gn[:, 1:2, columns(j)].to_broadcast([P, TT, P]), ALU.add))
                        yield
                    for d in range(2):
                        wait(dve, "gates_ready", j, d + 1)
                        ov = o[d][:].rearrange("p (n e) -> p n e", n=4)
                        o2 = o[d][:].rearrange("p (t e) -> p t e", t=TT)
                        for n in range(4):
                            t, hh = n // 2, n % 2
                            ins = stt(ov[:, n, :], v[:, t, bass.ds(j * P + hh * HEAD, HEAD)], gb[d][:, 2 * P + n:2 * P + n + 1], ov[:, n, :], ALU.mult, ALU.add)
                        link(ins)
                        gates = gb[d][:, 0:2 * P].rearrange("p (t e) -> p t e", t=TT)
                        if d == 0:
                            tt(yc, o2, gates, ALU.mult).then_inc(q["output_over"].sem, 1)
                        else:
                            link(tt(o2, o2, gates, ALU.mult))
                            wait(dve, "output_over", j, 1)
                            tt(yc, yc, o2, ALU.add).then_inc(q["output_over"].sem, 1)
                        yield
                    assert s.n == N["output_step"], s.n

                def pair(i, first=False, last=False):
                    before = output(i - 1) if not first else iter(())
                    after = factors(i + 1) if not last else iter(())

                    def beside(part, count):
                        for _ in range(count):
                            next(part, None)

                    for d in range(2):
                        for n in range(4):
                            wait(dve, "products_done", i, 4 * d + n + 1)
                            ins = tt(GM[d][:, n].rearrange("p a b -> p (a b)"), ps[:, 4 * d + n, :], keep[:, d, :], ALU.mult)
                        ins.then_inc(q["kept_ready"].sem, 1)
                    s = Steps("start_step", i)
                    for d in range(2):
                        lower, upper = level[:, LEVELS * d, :], level[:, LEVELS * (1 - d), :]
                        wait(dve, "m1_done", i, d + 1)
                        wait(dve, "kept_ready", i, d + 1)
                        for hh in range(2):
                            s.do(tt(M1[d][:].rearrange("p (t h) e -> p h t e", h=2)[:, hh], ps[:, 4 * d + hh, 0:2 * P].rearrange("p (a b) -> p a b", a=2),
                                    keep[:, 1 - d, 0:P].unsqueeze(1).to_broadcast([P, 2, P]), ALU.mult))
                        s.link()
                        wait(dve, "x_begun", i, d + 1)
                        begin_step()
                        dve.copy_predicated(Xi[d][:], lower.unsqueeze(1).to_broadcast([P, 4, P]), M1[d][:]).then_inc(q["xi_ready"].sem, 1)
                        dve.copy_predicated(XT[d][:], upper.unsqueeze(1).to_broadcast([P, 4, P]), GM[d][:, :, 0, :]).then_inc(q["x_ready"].sem, 1)
                    for lv in range(1, LEVELS):
                        if lv < GATES_AT:
                            beside(before, 2)
                        else:
                            beside(after, 1)
                        for d in range(2):
                            lower, upper = level[:, LEVELS * d + lv, :], level[:, LEVELS * (1 - d) + lv, :]
                            wait(dve, "step_done", i, 2 * (lv - 1) + d + 1)
                            wait(dve, "x_ready", i, 2 * (lv - 1) + d + 1)
                            begin_step()
                            if lv < LEVELS - 1:
                                dve.copy_predicated(Xi[d][:], lower.unsqueeze(1).to_broadcast([P, 4, P]), ps[:, 4 * d + 1, :].rearrange("p (a b) -> p a b", a=4)).then_inc(q["xi_ready"].sem, 1)
                            dve.copy_predicated(XT[d][:], upper.unsqueeze(1).to_broadcast([P, 4, P]),
                                                ps[:, 4 * d + 2, :].rearrange("p (a b) -> p a b", a=4)).then_inc(q["x_ready"].sem, 1)
                    beside(after, 2)
                    for d in range(2):
                        wait(dve, "state_done", i, d + 1)
                        for hh in range(2):
                            hs = half(hh)
                            ins = ts(S0[d][hs, hh, :], ps[hs, 4 * d + 3, 256 + hh * HEAD:256 + (hh + 1) * HEAD], ends[d][hs, 2:3], ends[d][hs, 1:2], ALU.mult, ALU.mult)
                        ins.then_inc(q["s0_ready"].sem, 1)

                for _ in factors(0, first=True):
                    pass
                all_pairs(dve, pair)
                for _ in output(pairs - 1):
                    pass


def network(nc, I, out):
    with ExitStack() as ctx:
        m = Model(nc, I, out, ctx)
        layers = [Run(m.weights, 6 * l, m.layer_pieces(l)) for l in range(2)]
        attention = Run(m.weights, 6, by_cols(I["attn_w_in_2"][0], 256) + by_cols(I["attn_w_out_2"][0], 256))
        recurrent = Run(m.weights, 6, [p for n in "rkvo" for p in by_cols(I[f"rk_w_{n}_2"][0], 256)])
        m.run = layers[0]
        with ExitStack() as inner:
            memory_rows, memory = m.tmp(inner, "memory_rows", [P, TT, D]), m.tmp(inner, "memory", [P, KC, SEQ])
            m.constants()
            m.hybrid_mixer(0, memory_rows, memory)
            m.cross_attention(0, memory, m.bias_rows(inner))
            m.norm_turn(m.h, "norm_ffn_g0", m.xT)
            gate, up, down = m.ffn_sources(I["ffn_w_gate"][0], I["ffn_w_up"][0], I["ffn_w_down"][0])
            m.ffn(I["ffn_w_gate"].shape[2] // CHUNK, gate, up, down, layers[1], m.h, True)
            m.hybrid_mixer(1)
            m.cross_attention(1, memory)
        m.next_gain = I["norm_final_g"].unsqueeze(0)
        m.experts(attention)
        m.close_and_norm(m.h, False, "norm2_00", m.xT)
        with ExitStack() as inner:
            u = m.tmp(inner, "u", [P, TT, D])
            gains = I["norm_g_2"]
            m.next_gain = gains[0, 1:2, :]
            m.attention_mixer(u)
            m.close_and_norm(u, True, "norm2_02", m.xT)
            m.next_gain = gains[0, 3:4, :]
            m.second_mlp(0, recurrent, u)
            m.close_and_norm(u, True, "norm2_10", m.xT)
            m.next_gain = gains[1, 1:2, :]
            Rwkv(m).run(u)
            m.close_and_norm(u, True, "norm2_12", m.xT)
            m.next_gain = gains[1, 3:4, :]
            m.second_mlp(1, None, u)
            m.add_normed(u, m.h)
        m.store_rows(m.h)


_INS = ["x", "mem", "norm_mix_g", "w_in", "conv_a_w", "conv_a_b", "ln_a_g", "ln_a_b", "conv_b_w", "ln_c_g", "ln_c_b",
        "gmlp_ws", "gmlp_b", "mix_out_g", "w_mix_out", "norm_x_g", "norm_mem_g", "w_xq", "w_xkv", "w_xo", "norm_ffn_g",
        "ffn_w_gate", "ffn_w_up", "ffn_w_down", "moe_router", "moe_w_gate", "moe_w_up", "moe_w_down", "norm_final_g",
        "rel_table_2", "norm_g_2", "attn_w_in_2", "attn_sink_2", "attn_w_out_2", "rk_mu_prev_2", "rk_mu_next_2",
        "rk_w_r_2", "rk_w_k_2", "rk_w_v_2", "rk_w_o_2", "rk_k_k_2", "rk_k_a_2", "rk_r_k_2", "rk_gn_w_2", "rk_gn_b_2",
        "rk_w0_2", "rk_w1_2", "rk_w2_2", "rk_a0_2", "rk_a1_2", "rk_a2_2", "rk_g1_2", "rk_g2_2", "mlp_w1_2", "mlp_w2_2"]


def kernel(**inputs):
    import numpy as _np
    import concourse.bacc as _bacc
    from concourse import mybir as _mybir
    from concourse.bass_utils import run_bass_kernel_spmd as _run

    nc = _bacc.Bacc("TRN2", target_bir_lowering=False, num_devices=1)
    data = {name: _np.ascontiguousarray(inputs[name]) for name in _INS}
    data["bucket_of_distance"], data["distance_mask"] = t5_constants()
    data.update(rwkv_constants())
    arrays, args = {}, {}
    for name, a in data.items():
        arrays[f"in_{name}_dram"] = a
        args[name] = nc.dram_tensor(f"in_{name}_dram", a.shape, _mybir.dt.from_np(a.dtype), kind="ExternalInput").ap()
    out = nc.dram_tensor("out_0_dram", (1, SEQ, D), _mybir.dt.float32, kind="ExternalOutput").ap()
    network(nc, args, out)
    r = _run(nc, [arrays], core_ids=[0])
    return r.results[0]["out_0_dram"]
```
